# Optimizing a Trainium2 kernel written in Bass

```python
import math
import jax, jax.numpy as jnp
from jax import lax
import numpy as np

D_MODEL = 1024
BATCH = 1
SEQ = 256
DEPTH = 1

N_META = 16
EPS = 1e-6

D_HY = 512
HY_GROUPS = 8
HY_SHORT = 3
HY_EMB = 33
HY_BANDS = (HY_EMB - 1) // 2
HY_FFN = 64
HY_TARGET = 1e-2
HY_DECAY_HI = 0.3
HY_DECAY_LO = 1.5

D_RG = 1024
RG_HEADS = 8
RG_HEAD_DIM = D_RG // RG_HEADS
RG_CONV = 4
RG_C = 8.0

PEER_HEADS = 8
N_KEYS = 128
N_EXPERTS = N_KEYS * N_KEYS
D_KEY = 256
D_HALF = D_KEY // 2
PEER_TOPK = 16
PEER_CHUNK = 16

D_IN = 3 * D_HY + 2 * D_RG + 2 * D_MODEL


def rmsnorm(x, g):
    xf = x.astype(jnp.float32)
    y = xf * lax.rsqrt(jnp.mean(xf * xf, axis=-1, keepdims=True) + EPS)
    return (y * g.astype(jnp.float32)).astype(x.dtype)

def hyena_filter(L, w1, b1, w2, b2, w3, b3, freq):
    f32 = jnp.float32
    t = jnp.linspace(0.0, 1.0, L, dtype=f32)[:, None]
    w = (2.0 * math.pi / L) * jnp.arange(L, dtype=f32)[:, None]
    bands = jnp.linspace(1e-4, HY_BANDS - 1, HY_BANDS, dtype=f32)[None, :]
    z = jnp.concatenate([t, jnp.cos(bands * w), -jnp.sin(bands * w)], axis=-1)
    freq = freq.astype(f32)
    hdn = jnp.sin(freq[0] * (z @ w1.astype(f32) + b1.astype(f32)))
    hdn = jnp.sin(freq[1] * (hdn @ w2.astype(f32) + b2.astype(f32)))
    k = (hdn @ w3.astype(f32) + b3.astype(f32)).reshape(L, 2, D_HY)
    deltas = jnp.abs(jnp.linspace(math.log(HY_TARGET) / HY_DECAY_HI,
                                  math.log(HY_TARGET) / HY_DECAY_LO, D_HY, dtype=f32))
    k = k * jnp.exp(-t * deltas)[:, None, :]
    k_fwd, k_bwd = k[:, 0], k[:, 1]
    return jnp.concatenate([k_fwd, jnp.zeros((1, D_HY), f32), k_bwd[:0:-1]], axis=0)

def fft_long_conv(u, k_full, skip):
    L = u.shape[1]
    uf = u.astype(jnp.float32)
    U = jnp.fft.rfft(uf, n=2 * L, axis=1)
    K = jnp.fft.rfft(k_full, axis=0)
    y = jnp.fft.irfft(U * K[None], n=2 * L, axis=1)[:, :L]
    return (y + uf * skip.astype(jnp.float32)).astype(u.dtype)

def hyena_branch(hy_in, conv_w, conv_b, w1, b1, w2, b2, w3, b3, freq, skip, w_proj):
    B, L, _ = hy_in.shape
    hp = jnp.pad(hy_in, ((0, 0), (1, 1), (0, 0)))
    u = hp[:, 0:L] * conv_w[0] + hp[:, 1:L + 1] * conv_w[1] + hp[:, 2:L + 2] * conv_w[2] + conv_b
    x0, x1, v = u[..., :D_HY], u[..., D_HY:2 * D_HY], u[..., 2 * D_HY:]
    k_full = hyena_filter(L, w1, b1, w2, b2, w3, b3, freq)
    y = fft_long_conv(v * x1, k_full, skip) * x0
    return y @ w_proj

def rglru_direction(x, conv_w, conv_b, gate_w, gate_b, lam):
    B, L, _ = x.shape
    xp = jnp.pad(x, ((0, 0), (RG_CONV - 1, 0), (0, 0)))
    xc = conv_b + sum(xp[:, RG_CONV - 1 - j:RG_CONV - 1 - j + L] * conv_w[j] for j in range(RG_CONV))
    xh = xc.reshape(B, L, RG_HEADS, RG_HEAD_DIM)
    gates = jnp.einsum('blhi,ghij->gblhj', xh, gate_w).reshape(2, B, L, D_RG)
    gates = gates.astype(jnp.float32) + gate_b.astype(jnp.float32)[:, None, None, :]
    r = jax.nn.sigmoid(gates[0])
    i = jax.nn.sigmoid(gates[1])
    log_a = -RG_C * r * jax.nn.softplus(-lam.astype(jnp.float32))
    a = jnp.exp(log_a)
    mult = jnp.sqrt(-jnp.expm1(2.0 * log_a))
    mult = mult.at[:, 0].set(1.0)
    b = mult * i * xc.astype(jnp.float32)

    def combine(p, q):
        a1, b1 = p
        a2, b2 = q
        return a1 * a2, a2 * b1 + b2

    _, h = lax.associative_scan(combine, (a, b), axis=1)
    return h.astype(x.dtype)

def rglru_branch(rg_x, rg_g, conv_w, conv_b, gate_w, gate_b, lam, w_proj):
    h_f = rglru_direction(rg_x, conv_w[0], conv_b[0], gate_w[0], gate_b[0], lam[0])
    h_b = rglru_direction(rg_x[:, ::-1], conv_w[1], conv_b[1], gate_w[1], gate_b[1], lam[1])[:, ::-1]
    y = (h_f + h_b) * jax.nn.gelu(rg_g)
    return y @ w_proj

def peer(x, wq, keys, u_tab, v_tab):
    B, L, D = x.shape
    K = PEER_TOPK
    q = (x @ wq).reshape(B, L, PEER_HEADS, 2, D_HALF)
    s = jnp.einsum('blhpd,hpkd->blhpk', q, keys).astype(jnp.float32)
    ts, ti = lax.top_k(s, K)
    cand = ts[..., 0, :, None] + ts[..., 1, None, :]
    cs, ci = lax.top_k(cand.reshape(B, L, PEER_HEADS, K * K), K)
    e1 = jnp.take_along_axis(ti[..., 0, :], ci // K, axis=-1)
    e2 = jnp.take_along_axis(ti[..., 1, :], ci % K, axis=-1)
    experts = e1 * N_KEYS + e2
    g = jax.nn.softmax(cs, axis=-1).astype(x.dtype)

    nc = L // PEER_CHUNK
    hk = PEER_HEADS * K

    def to_chunks(a, last):
        return a.reshape(B, nc, PEER_CHUNK, last).transpose(1, 0, 2, 3).reshape(nc, B * PEER_CHUNK, last)

    xs = (to_chunks(x, D), to_chunks(experts.reshape(B, L, hk), hk), to_chunks(g.reshape(B, L, hk), hk))

    def chunk_fn(args):
        xt, et, gt = args
        act = jax.nn.gelu(jnp.einsum('td,tkd->tk', xt, u_tab[et])) * gt
        return jnp.einsum('tk,tkd->td', act, v_tab[et])

    out = lax.map(chunk_fn, xs)
    return out.reshape(nc, B, PEER_CHUNK, D).transpose(1, 0, 2, 3).reshape(B, L, D)

def first_inputs(seed: int = 0) -> dict:
    key = jax.random.key(seed)
    ks = iter(jax.random.split(key, 40))
    f32 = jnp.float32

    def nrm(shape, scale):
        return jax.random.normal(next(ks), shape, f32) * scale

    L_TOT = SEQ + N_META
    x = nrm((BATCH, SEQ, D_MODEL), 1.0)
    meta = nrm((N_META, D_MODEL), 1.0)
    g_final = 1.0 + nrm((D_MODEL,), 0.02)
    g_mix = 1.0 + nrm((DEPTH, D_MODEL), 0.02)
    w_in = nrm((DEPTH, D_MODEL, D_IN), D_MODEL ** -0.5)
    b_gate = nrm((DEPTH, 2 * D_MODEL), 0.02)
    hy_conv_w = nrm((DEPTH, HY_SHORT, 3 * D_HY), HY_SHORT ** -0.5)
    hy_conv_b = nrm((DEPTH, 3 * D_HY), 0.02)
    hy_w1 = nrm((DEPTH, HY_EMB, HY_FFN), HY_EMB ** -0.5)
    hy_b1 = nrm((DEPTH, HY_FFN), 0.1)
    hy_w2 = nrm((DEPTH, HY_FFN, HY_FFN), HY_FFN ** -0.5)
    hy_b2 = nrm((DEPTH, HY_FFN), 0.1)
    hy_w3 = nrm((DEPTH, HY_FFN, 2 * D_HY), (HY_FFN * L_TOT / 4.0) ** -0.5)
    hy_b3 = nrm((DEPTH, 2 * D_HY), L_TOT ** -0.5)
    hy_freq = 1.0 + nrm((DEPTH, 2, HY_FFN), 0.02)
    hy_skip = nrm((DEPTH, D_HY), 1.0)
    hy_out = nrm((DEPTH, D_HY, D_MODEL), D_HY ** -0.5)
    rg_conv_w = nrm((DEPTH, 2, RG_CONV, D_RG), RG_CONV ** -0.5)
    rg_conv_b = nrm((DEPTH, 2, D_RG), 0.02)
    rg_gate_w = nrm((DEPTH, 2, 2, RG_HEADS, RG_HEAD_DIM, RG_HEAD_DIM), RG_HEAD_DIM ** -0.5)
    rg_gate_b = nrm((DEPTH, 2, 2, D_RG), 0.02)
    a_c = jax.random.uniform(next(ks), (DEPTH, 2, D_RG), f32, minval=0.9, maxval=0.999)
    a_base = a_c ** (1.0 / RG_C)
    rg_lambda = jnp.log(a_base) - jnp.log1p(-a_base)
    rg_out = nrm((DEPTH, D_RG, D_MODEL), D_RG ** -0.5)
    w_out = nrm((DEPTH, D_MODEL, D_MODEL), D_MODEL ** -0.5)
    g_ffn = 1.0 + nrm((DEPTH, D_MODEL), 0.02)
    peer_wq = nrm((DEPTH, D_MODEL, PEER_HEADS * D_KEY), D_MODEL ** -0.5)
    peer_keys = nrm((DEPTH, PEER_HEADS, 2, N_KEYS, D_HALF), D_HALF ** -0.5)
    peer_u = nrm((DEPTH, N_EXPERTS, D_MODEL), D_MODEL ** -0.5)
    peer_v = nrm((DEPTH, N_EXPERTS, D_MODEL), PEER_HEADS ** -0.5)
    return {'x': x, 'meta': meta, 'g_final': g_final, 'g_mix': g_mix, 'w_in': w_in, 'b_gate': b_gate,
            'hy_conv_w': hy_conv_w, 'hy_conv_b': hy_conv_b, 'hy_w1': hy_w1, 'hy_b1': hy_b1,
            'hy_w2': hy_w2, 'hy_b2': hy_b2, 'hy_w3': hy_w3, 'hy_b3': hy_b3, 'hy_freq': hy_freq,
            'hy_skip': hy_skip, 'hy_out': hy_out, 'rg_conv_w': rg_conv_w, 'rg_conv_b': rg_conv_b,
            'rg_gate_w': rg_gate_w, 'rg_gate_b': rg_gate_b, 'rg_lambda': rg_lambda, 'rg_out': rg_out,
            'w_out': w_out, 'g_ffn': g_ffn, 'peer_wq': peer_wq, 'peer_keys': peer_keys,
            'peer_u': peer_u, 'peer_v': peer_v}

def first_block(x, meta, g_final, g_mix, w_in, b_gate, hy_conv_w, hy_conv_b, hy_w1, hy_b1, hy_w2, hy_b2,
              hy_w3, hy_b3, hy_freq, hy_skip, hy_out, rg_conv_w, rg_conv_b, rg_gate_w, rg_gate_b,
              rg_lambda, rg_out, w_out, g_ffn, peer_wq, peer_keys, peer_u, peer_v):
    B = x.shape[0]
    h = jnp.concatenate([jnp.broadcast_to(meta.astype(x.dtype)[None], (B, N_META, D_MODEL)), x], axis=1)
    s_hy = 3 * D_HY
    s_rx = s_hy + D_RG
    s_rg = s_rx + D_RG
    for l in range(DEPTH):
        n = rmsnorm(h, g_mix[l])
        proj = n @ w_in[l]
        y_hy = hyena_branch(proj[..., :s_hy], hy_conv_w[l], hy_conv_b[l], hy_w1[l], hy_b1[l], hy_w2[l],
                            hy_b2[l], hy_w3[l], hy_b3[l], hy_freq[l], hy_skip[l], hy_out[l])
        y_rg = rglru_branch(proj[..., s_hy:s_rx], proj[..., s_rx:s_rg], rg_conv_w[l], rg_conv_b[l],
                            rg_gate_w[l], rg_gate_b[l], rg_lambda[l], rg_out[l])
        gl = proj[..., s_rg:] + b_gate[l]
        merged = jax.nn.sigmoid(gl[..., :D_MODEL]) * y_hy + jax.nn.sigmoid(gl[..., D_MODEL:]) * y_rg
        h = h + merged @ w_out[l]
        h = h + peer(rmsnorm(h, g_ffn[l]), peer_wq[l], peer_keys[l], peer_u[l], peer_v[l])
    h = rmsnorm(h, g_final)
    return h[:, N_META:]


DEPTH_2 = 2

N_A = DEPTH_2 // 2
N_B = DEPTH_2 - N_A
HEAD_DIM = 64
CHUNK = 128
N_SG = 12
SG_WIDTH = N_SG * HEAD_DIM
DIL_PAIRS = ((128, 1), (512, 4), (2048, 16))
HEADS_PER_DIL = 4
N_DIL_HEADS = HEADS_PER_DIL * len(DIL_PAIRS)
DIL_Q_WIDTH = N_DIL_HEADS * HEAD_DIM
DIL_OUT_WIDTH = HEADS_PER_DIL * HEAD_DIM
N_MEM = 256
MEM_HEADS = 4
MEM_WIDTH = MEM_HEADS * HEAD_DIM
N_EXPERTS_2 = 16
N_EXPERT_GROUPS = 4
EXPERTS_PER_GROUP = N_EXPERTS_2 // N_EXPERT_GROUPS
TOP_K = 2
D_EXPERT = 1024
MOE_BLOCK = 128
ALPHA = (2 * DEPTH_2) ** 0.25
BETA = (8 * DEPTH_2) ** -0.25
LN_EPS = 1e-5
ATT_SCALE = 1.0 / math.sqrt(HEAD_DIM)


def layer_norm(x, g, b):
    xf = x.astype(jnp.float32)
    mu = jnp.mean(xf, -1, keepdims=True)
    var = jnp.mean(jnp.square(xf - mu), -1, keepdims=True)
    return ((xf - mu) * lax.rsqrt(var + LN_EPS)).astype(x.dtype) * g + b

def alibi_slopes():
    return 2.0 ** (-8.0 * jnp.arange(1, N_DIL_HEADS + 1, dtype=jnp.float32) / N_DIL_HEADS)

def spatial_gating(u, v, w_s, b_s):
    B, S, G, Dh = v.shape
    vc = v.reshape(B, S // CHUNK, CHUNK, G, Dh)
    causal = jnp.tril(jnp.ones((CHUNK, CHUNK), bool))
    w = jnp.where(causal[None], w_s, 0).astype(v.dtype)
    s = jnp.einsum('gpq,bcqgd->bcpgd', w, vc) + b_s.T[None, None, :, :, None].astype(v.dtype)
    return u * s.reshape(B, S, G, Dh)

def dilated_branch(q, k, v, window, dilation, slopes):
    B, S, H, Dh = q.shape
    steps = window // dilation
    L = S // dilation
    N = B * dilation

    def by_residue(t):
        return t.reshape(B, L, dilation, H, Dh).transpose(0, 2, 3, 1, 4).reshape(N, H, L, Dh)

    qr, kr, vr = by_residue(q), by_residue(k), by_residue(v)
    nb = -(-L // CHUNK)
    pad = nb * CHUNK - L
    qr = jnp.pad(qr, ((0, 0), (0, 0), (0, pad), (0, 0)))
    kr = jnp.pad(kr, ((0, 0), (0, 0), (CHUNK, pad), (0, 0)))
    vr = jnp.pad(vr, ((0, 0), (0, 0), (CHUNK, pad), (0, 0)))
    qb = qr.reshape(N, H, nb, CHUNK, Dh)
    kb = kr.reshape(N, H, nb + 1, CHUNK, Dh)
    vb = vr.reshape(N, H, nb + 1, CHUNK, Dh)
    kband = jnp.concatenate([kb[:, :, :-1], kb[:, :, 1:]], axis=3)
    vband = jnp.concatenate([vb[:, :, :-1], vb[:, :, 1:]], axis=3)
    s = jnp.einsum('nhbqd,nhbkd->nhbqk', qb, kband).astype(jnp.float32) * ATT_SCALE
    iq = jnp.arange(CHUNK)[:, None]
    jk = jnp.arange(2 * CHUNK)[None, :]
    rel = CHUNK + iq - jk
    key_pos = (jnp.arange(nb)[:, None, None] - 1) * CHUNK + jk[None]
    valid = (rel >= 0)[None] & (rel <= steps)[None] & (key_pos >= 0)
    bias = -slopes[:, None, None, None] * (dilation * rel).astype(jnp.float32)[None, None]
    s = jnp.where(valid[None, None], s + bias[None], -jnp.inf)
    m = jnp.max(s, -1, keepdims=True)
    p = jnp.exp(s - m)
    l = jnp.sum(p, -1, keepdims=True)
    o = jnp.einsum('nhbqk,nhbkd->nhbqd', (p / l).astype(v.dtype), vband)
    lse = (m + jnp.log(l))[..., 0]
    o = o.reshape(N, H, nb * CHUNK, Dh)[:, :, :L]
    lse = lse.reshape(N, H, nb * CHUNK)[:, :, :L]
    o = o.reshape(B, dilation, H, L, Dh).transpose(0, 3, 1, 2, 4).reshape(B, S, H, Dh)
    lse = lse.reshape(B, dilation, H, L).transpose(0, 3, 1, 2).reshape(B, S, H)
    return o, lse

def dilated_mixture(q, k, v, slopes):
    outs, lses = [], []
    for g, (window, dilation) in enumerate(DIL_PAIRS):
        hs = slice(g * HEADS_PER_DIL, (g + 1) * HEADS_PER_DIL)
        o, lse = dilated_branch(q[:, :, hs], k[:, :, hs], v[:, :, hs], window, dilation, slopes[hs])
        outs.append(o)
        lses.append(lse)
    O = jnp.stack(outs, 0)
    wts = jax.nn.softmax(jnp.stack(lses, 0), 0)
    return jnp.sum(wts[..., None].astype(O.dtype) * O, 0)

def memory_attention(q, mk, mv):
    s = jnp.einsum('bshd,bmhd->bhsm', q, mk).astype(jnp.float32) * ATT_SCALE
    p = jax.nn.softmax(s, -1).astype(mv.dtype)
    return jnp.einsum('bhsm,bmhd->bshd', p, mv)

def route(h, w_router, b_router):
    T = h.shape[0]
    probs = jax.nn.softmax((h @ w_router).astype(jnp.float32), -1)
    sel = probs + b_router.astype(jnp.float32)
    grp = sel.reshape(T, N_EXPERT_GROUPS, EXPERTS_PER_GROUP)
    grp_score = jnp.sum(lax.top_k(grp, TOP_K)[0], -1)
    g_idx = jnp.argmax(grp_score, -1).astype(jnp.int32)
    in_grp = jnp.take_along_axis(grp, g_idx[:, None, None], axis=1)[:, 0]
    _, local = lax.top_k(in_grp, TOP_K)
    expert = g_idx[:, None] * EXPERTS_PER_GROUP + local.astype(jnp.int32)
    gate = jnp.take_along_axis(probs, expert, 1)
    gate = gate / jnp.sum(gate, -1, keepdims=True)
    return expert, gate

def moe_ffn(h, expert, gate, w_gate, w_up, w_down):
    T, D = h.shape
    n_slots = T * TOP_K
    e_flat = expert.reshape(-1)
    g_flat = gate.reshape(-1)
    tok = jnp.arange(n_slots, dtype=jnp.int32) // TOP_K
    order = jnp.argsort(e_flat)
    e_s, tok_s, g_s = e_flat[order], tok[order], g_flat[order]
    counts = jnp.bincount(e_flat, length=N_EXPERTS_2)
    starts = jnp.cumsum(counts) - counts
    padded = (counts + MOE_BLOCK - 1) // MOE_BLOCK * MOE_BLOCK
    pad_ends = jnp.cumsum(padded)
    pad_starts = pad_ends - padded
    dest = pad_starts[e_s] + (jnp.arange(n_slots) - starts[e_s])
    n_pad = n_slots + N_EXPERTS_2 * MOE_BLOCK
    n_blocks = n_pad // MOE_BLOCK
    slot_tok = jnp.zeros((n_pad,), jnp.int32).at[dest].set(tok_s)
    slot_gate = jnp.zeros((n_pad,), jnp.float32).at[dest].set(g_s)
    block_start = jnp.arange(n_blocks) * MOE_BLOCK
    block_expert = jnp.minimum(jnp.searchsorted(pad_ends, block_start, side='right'), N_EXPERTS_2 - 1)
    xb = h[slot_tok].reshape(n_blocks, MOE_BLOCK, D)

    def expert_block(args):
        xblk, e = args
        return (jax.nn.silu(xblk @ w_gate[e]) * (xblk @ w_up[e])) @ w_down[e]

    yb = lax.map(expert_block, (xb, block_expert))
    y = yb.reshape(n_pad, D) * slot_gate[:, None].astype(h.dtype)
    return jnp.zeros_like(h).at[slot_tok].add(y)

def _normal(k, shape, scale):
    return jax.random.normal(k, shape, jnp.float32) * scale

def second_inputs(seed: int = 0) -> dict:
    key = jax.random.key(seed)
    ks = jax.random.split(key, 24)
    D = D_MODEL
    return {
        "x": _normal(ks[0], (BATCH, SEQ, D), 1.0),
        "mem": _normal(ks[1], (BATCH, N_MEM, D), 1.0),
        "w_in_a": _normal(ks[2], (N_A, D, 2 * SG_WIDTH + MEM_WIDTH), D ** -0.5),
        "w_out_a": _normal(ks[3], (N_A, SG_WIDTH + MEM_WIDTH, D), (SG_WIDTH + MEM_WIDTH) ** -0.5 * BETA),
        "sg_ln_g": 1.0 + _normal(ks[4], (N_A, SG_WIDTH), 0.02),
        "sg_ln_b": _normal(ks[5], (N_A, SG_WIDTH), 0.02),
        "sg_w": _normal(ks[6], (N_A, N_SG, CHUNK, CHUNK), 0.5 * CHUNK ** -0.5),
        "sg_b": 1.0 + _normal(ks[7], (N_A, N_SG, CHUNK), 0.1),
        "w_in_b": _normal(ks[8], (N_B, D, DIL_Q_WIDTH + MEM_WIDTH), D ** -0.5),
        "w_out_b": _normal(ks[9], (N_B, DIL_OUT_WIDTH + MEM_WIDTH, D), (DIL_OUT_WIDTH + MEM_WIDTH) ** -0.5 * BETA),
        "w_k_shared": _normal(ks[10], (D, DIL_Q_WIDTH), D ** -0.5),
        "w_v_shared": _normal(ks[11], (D, DIL_Q_WIDTH), D ** -0.5 * BETA),
        "w_mem_k": _normal(ks[12], (DEPTH_2, D, MEM_WIDTH), D ** -0.5),
        "w_mem_v": _normal(ks[13], (DEPTH_2, D, MEM_WIDTH), D ** -0.5 * BETA),
        "ln1_g": 1.0 + _normal(ks[14], (DEPTH_2, D), 0.02),
        "ln1_b": _normal(ks[15], (DEPTH_2, D), 0.02),
        "ln2_g": 1.0 + _normal(ks[16], (DEPTH_2, D), 0.02),
        "ln2_b": _normal(ks[17], (DEPTH_2, D), 0.02),
        "w_router": _normal(ks[18], (D, N_EXPERTS_2), D ** -0.5),
        "b_router": _normal(ks[19], (N_EXPERTS_2,), 0.01),
        "w_gate": _normal(ks[20], (DEPTH_2, N_EXPERTS_2, D, D_EXPERT), D ** -0.5),
        "w_up": _normal(ks[21], (DEPTH_2, N_EXPERTS_2, D, D_EXPERT), D ** -0.5),
        "w_down": _normal(ks[22], (DEPTH_2, N_EXPERTS_2, D_EXPERT, D), D_EXPERT ** -0.5 * BETA),
    }

def second_block(x, mem, w_in_a, w_out_a, sg_ln_g, sg_ln_b, sg_w, sg_b, w_in_b, w_out_b,
              w_k_shared, w_v_shared, w_mem_k, w_mem_v, ln1_g, ln1_b, ln2_g, ln2_b,
              w_router, b_router, w_gate, w_up, w_down):
    B, S, D = x.shape
    M = mem.shape[1]
    slopes = alibi_slopes()
    k_sh = None
    v_sh = None
    for layer in range(DEPTH_2):
        mk = (mem @ w_mem_k[layer]).reshape(B, M, MEM_HEADS, HEAD_DIM)
        mv = (mem @ w_mem_v[layer]).reshape(B, M, MEM_HEADS, HEAD_DIM)
        if layer < N_A:
            a = layer
            proj = x @ w_in_a[a]
            u = jax.nn.gelu(proj[..., :SG_WIDTH], approximate=False)
            gv = jax.nn.gelu(proj[..., SG_WIDTH:2 * SG_WIDTH], approximate=False)
            qm = proj[..., 2 * SG_WIDTH:].reshape(B, S, MEM_HEADS, HEAD_DIM)
            gv = layer_norm(gv, sg_ln_g[a], sg_ln_b[a])
            mix = spatial_gating(u.reshape(B, S, N_SG, HEAD_DIM), gv.reshape(B, S, N_SG, HEAD_DIM),
                                 sg_w[a], sg_b[a]).reshape(B, S, SG_WIDTH)
            mo = memory_attention(qm, mk, mv).reshape(B, S, MEM_WIDTH)
            att = jnp.concatenate([mix, mo], -1) @ w_out_a[a]
        else:
            bl = layer - N_A
            if bl == 0:
                k_sh = (x @ w_k_shared).reshape(B, S, N_DIL_HEADS, HEAD_DIM)
                v_sh = (x @ w_v_shared).reshape(B, S, N_DIL_HEADS, HEAD_DIM)
            proj = x @ w_in_b[bl]
            q = proj[..., :DIL_Q_WIDTH].reshape(B, S, N_DIL_HEADS, HEAD_DIM)
            qm = proj[..., DIL_Q_WIDTH:].reshape(B, S, MEM_HEADS, HEAD_DIM)
            mix = dilated_mixture(q, k_sh, v_sh, slopes).reshape(B, S, DIL_OUT_WIDTH)
            mo = memory_attention(qm, mk, mv).reshape(B, S, MEM_WIDTH)
            att = jnp.concatenate([mix, mo], -1) @ w_out_b[bl]
        x = layer_norm(ALPHA * x + att, ln1_g[layer], ln1_b[layer])
        h = x.reshape(B * S, D)
        expert, gate = route(h, w_router, b_router)
        ffn = moe_ffn(h, expert, gate, w_gate[layer], w_up[layer], w_down[layer]).reshape(B, S, D)
        x = layer_norm(ALPHA * x + ffn, ln2_g[layer], ln2_b[layer])
    return x


def setup_inputs(seed=0):
    out = dict(first_inputs(seed))
    for name, value in second_inputs(seed + 1).items():
        if name != "x":
            out[name + "_2"] = value
    return out


def reference(
    x, meta, g_final, g_mix, w_in, b_gate, hy_conv_w, hy_conv_b, hy_w1, hy_b1, hy_w2, hy_b2,
    hy_w3, hy_b3, hy_freq, hy_skip, hy_out, rg_conv_w, rg_conv_b, rg_gate_w, rg_gate_b,
    rg_lambda, rg_out, w_out, g_ffn, peer_wq, peer_keys, peer_u, peer_v, mem_2, w_in_a_2,
    w_out_a_2, sg_ln_g_2, sg_ln_b_2, sg_w_2, sg_b_2, w_in_b_2, w_out_b_2, w_k_shared_2,
    w_v_shared_2, w_mem_k_2, w_mem_v_2, ln1_g_2, ln1_b_2, ln2_g_2, ln2_b_2, w_router_2,
    b_router_2, w_gate_2, w_up_2, w_down_2,
):
    x = first_block(
        x, meta, g_final, g_mix, w_in, b_gate, hy_conv_w, hy_conv_b, hy_w1, hy_b1, hy_w2, hy_b2,
        hy_w3, hy_b3, hy_freq, hy_skip, hy_out, rg_conv_w, rg_conv_b, rg_gate_w, rg_gate_b,
        rg_lambda, rg_out, w_out, g_ffn, peer_wq, peer_keys, peer_u, peer_v,
    )
    return second_block(
        x, mem_2, w_in_a_2, w_out_a_2, sg_ln_g_2, sg_ln_b_2, sg_w_2, sg_b_2, w_in_b_2,
        w_out_b_2, w_k_shared_2, w_v_shared_2, w_mem_k_2, w_mem_v_2, ln1_g_2, ln1_b_2, ln2_g_2,
        ln2_b_2, w_router_2, b_router_2, w_gate_2, w_up_2, w_down_2,
    )


_drawn_inputs = setup_inputs


def setup_inputs(seed=0):
    import zlib

    import numpy as np

    out = dict(_drawn_inputs(seed))
    spreads = {}
    factors = {'rg_gate_b': 4.338, 'sg_ln_g_2': 8.0, 'sg_ln_b_2': 8.0, 'hy_freq': 2.734}
    for name, (base, spread) in spreads.items():
        noise = np.random.default_rng([zlib.crc32(name.encode()), seed]).standard_normal(out[name].shape)
        drawn = base * np.exp(spread * noise) if base else spread * noise
        out[name] = __import__('jax').numpy.asarray(drawn.astype(out[name].dtype))
    for name, factor in factors.items():
        out[name] = (out[name] * factor).astype(out[name].dtype)
    return out
```

```python
import math
from contextlib import ExitStack

import numpy as np

import concourse.bass as bass
from concourse import mybir

F32 = mybir.dt.float32
U32 = mybir.dt.uint32
ALU = mybir.AluOpType
ACT = mybir.ActivationFunctionType
X_AXIS = mybir.AxisListType.X

P = 128
D = 1024
DC = D // P
T = 256
TT = T // P
NM = 16
L = T + NM
EPS = 1e-6

D_HY = 512
HT = D_HY // P
HY_EMB = 33
HY_FFN = 64
D_RG = 1024
RH = D_RG // P
RG_CONV = 4
RG_C = 8.0
D_IN = 3 * D_HY + 2 * D_RG + 2 * D
PROJ_TILES = D_IN // P
BLOCKS = PROJ_TILES // 4
T_RX, T_HY, T_RG, T_G1, T_G2 = 0, RH, RH + 3 * HT, 2 * RH + 3 * HT, 3 * RH + 3 * HT

NFFT = 2 * L
NF = NFFT // 2 + 1
FP = NF // 3
TC = ((0, P), (P, P), (2 * P, L - 2 * P))

PH = 8
NKEYS = 128
TOPK = 16
SLOTS = PH * TOPK

SG_W = 768
N_SG = 12
HD = 64
MEM_H = 4
MEM_W = MEM_H * HD
DILS = ((128, 1), (512, 4), (2048, 16))
HPD = 4
N_DH = HPD * len(DILS)
NE = 16
NGRP = 4
EPG = NE // NGRP
ALPHA = 4 ** 0.25
LN_EPS = 1e-5
ATT_SCALE = 1.0 / math.sqrt(HD)
BIG = 1e30

TWO_PI_HI = 6.28125
TWO_PI_LO = 2 * math.pi - TWO_PI_HI
ROUND = 1.5 * 2.0 ** 23
PI_IN = 3.1415925

_widths = (("gmix", DC), ("pbias", PROJ_TILES), ("hyw", 3 * 3 * HT), ("hyb", 3 * HT), ("rgw", 2 * RG_CONV * RH),
           ("rgb", 2 * RH), ("gbias", 4 * RH), ("lam", 2 * RH), ("skip", HT))
COL = {}
NCOLS = 0
for _name, _w in _widths:
    COL[_name] = NCOLS
    NCOLS += _w


class Room:

    def __init__(self, total, at=0):
        self.total, self.at = total, at

    def take(self, n):
        o = self.at
        self.at += n
        assert self.at <= self.total, (self.at, self.total)
        return o


class Count:

    def __init__(self, sem):
        self.sem, self.n = sem, 0

    def by(self, ins, eng=None):
        ins.then_inc(self.sem, 1)
        self.n += 1
        if eng is not None:
            eng.wait_ge(self.sem, self.n)

    def here(self, eng):
        eng.wait_ge(self.sem, self.n)


class Kit:
    pass


def mixing_stage(K):
    nc, cut, bank, sem, d, ident, H = K.nc, K.cut, K.bank, K.sem, K.dram, K.ident, K.h_res
    v, a, pe = nc.vector, nc.scalar, nc.tensor

    at = Room(K.cols)
    nT = at.take(DC * L)
    proj = at.take(PROJ_TILES * L)
    ring = at.take(2 * DC * 512)
    gatew = at.take(4 * RH * P)
    xc = at.take(2 * RH * L)
    rr = at.take(2 * RH * L)
    ii = at.take(RH * L)
    th = at.take(RH * L)
    hc = at.take(3 * HT * L)
    dft = at.take(2 * 3 * NF)
    kspec = at.take(2 * 3 * D_HY)
    tmps = at.take(2 * D_HY)
    colss = at.take(NCOLS)
    small = at.take(290)
    hids = at.take(L)

    NT = cut(nT, P, DC, L)
    PROJ = cut(proj, P, PROJ_TILES, L)
    RING = [cut(ring + k * DC * 512, P, DC, 512) for k in range(2)]
    RGOUT = cut(ring, P, DC, D)
    GATEW = cut(gatew, P, 4 * RH, P)
    HYOUT = cut(gatew, P, HT, D)
    XN = cut(xc, P, 3, D)
    KFB = cut(xc + 3 * D, P, 2, D_HY)
    XC = cut(xc, P, 2 * RH, L)
    WOUT = cut(xc, P, DC, D)
    RR = cut(rr, P, 2 * RH, L)
    KPM = cut(rr, P, 2, 3, D_HY)
    II = cut(ii, P, RH, L)
    YRG = cut(ii, P, DC, T)
    TH = cut(th, P, RH, L)
    MERGED = cut(th, P, DC, T)
    DECAY = cut(ii, P, 2, 3, D_HY)
    HCV = cut(hc, P, 3 * HT, L)
    YHY = cut(hc + HT * L, P, HT, T)
    DFT = cut(dft, P, 2, 3, NF)
    IDFT = cut(nT, P, 2, 3, T)
    KSP = cut(kspec, P, 2, 3, D_HY)
    W3 = cut(tmps, P, 2 * D_HY)
    TMP = cut(tmps, P, 2, D_HY)
    UTOK = cut(proj, P, 3, D_HY)
    YSP = cut(proj + T_HY * L, P, 2, 3, D_HY)
    COLS = cut(colss, P, NCOLS)
    SM = cut(small, P, 290)
    ZT = cut(hids, HY_EMB, L)
    ARG = cut(kspec, HY_FFN, L)
    TURNS = cut(kspec + L, HY_FFN, L)
    HID = cut(hids, P, L)
    W1, W2, HB = SM[0:HY_EMB, 0:64], SM[0:HY_FFN, 64:128], SM[0:HY_FFN, 128:132]
    LT = [SM[:, 140 + 16 * n:156 + 16 * n] for n in range(8)]
    LAMC, NLAMC = LT[6], LT[7]
    SS, RSTD = SM[:, 280:283], SM[:, 284:287]
    SQ = cut(rr, P, D)

    def col(name, n=0):
        return COLS[:, COL[name] + n:COL[name] + n + 1]

    s_hy = K.lasting_sem("mix_hyena_in")
    s_x, s_cols, s_idft, s_gw, s_rgo, s_hyo, s_wo = (sem("mix_" + n) for n in (
        "x_in", "cols_in", "idft_in", "gatew_in", "rgout_in", "hyout_in", "wout_in"))
    s_ring = [sem(f"mix_ring{k}_in") for k in range(2)]
    s_sq, s_root, s_nT, s_turn = sem("mix_squares"), sem("mix_root"), sem("mix_nT"), sem("mix_turned")
    s_ms, s_xn = sem("mix_meansq"), sem("mix_xn")
    s_mm, s_ev = sem("mix_proj_mm"), sem("mix_proj")
    s_fmm, s_arg, s_sin, s_kmm, s_kpm = (sem("mix_filter_" + n) for n in ("mm", "arg", "sin", "kmm", "k"))
    s_kfm, s_ksp = sem("mix_kspec_mm"), sem("mix_kspec")
    s_absl, s_el, s_lamc = sem("mix_abs_lambda"), sem("mix_exp_lambda"), sem("mix_decay_rate")
    s_rgc, s_hyc = sem("mix_rg_conv"), sem("mix_hy_conv")
    s_gm, s_ga, s_at, s_m2, s_mu, s_scan = (sem("mix_rg_" + n) for n in (
        "gate_mm", "gates", "a_tanh", "mult_sq", "mult", "scan"))
    s_sg, s_u, s_utm, s_ut = sem("mix_sigmoids"), sem("mix_u"), sem("mix_u_turned"), sem("mix_u_tok")
    s_usm, s_ysp, s_ymm, s_yhy, s_yrg = (sem("mix_" + n) for n in ("uspec_mm", "yspec", "y_mm", "yhy", "yrg"))
    s_hom, s_rom, s_mg, s_wm = sem("mix_hyout_mm"), sem("mix_rgout_mm"), sem("mix_merged"), sem("mix_wout_mm")
    N_HY = 5 + 2 * 4
    N_GATES = 4 * RH

    with nc.Block() as block:
        @block.sync
        def _(sp):
            sp.dma_start(H[:, :, :], d["x"].rearrange("(m p) n -> p m n", p=P)).then_inc(s_x, 16)
            sp.dma_start(XN[0:NM, 2, :], d["meta"]).then_inc(s_x, 16)
            sp.dma_start(COLS, d["cols"]).then_inc(s_cols, 16)
            w_in = d["w_in"].rearrange("(c p) n -> p c n", p=P)
            for k in range(2):
                sp.dma_start(RING[k], w_in[:, :, k * 512:(k + 1) * 512]).then_inc(s_ring[k], 16)

            def refill(b, k):
                sp.wait_ge(s_mm, b * 4 - 4)
                sp.dma_start(RING[k], w_in[:, :, bass.ds(b * 512, 512)]).then_inc(s_ring[k], 16)

            with sp.Fori(1, BLOCKS // 2) as i:
                for k in range(2):
                    refill(i * 2 + k, k)
            refill(BLOCKS - 1, 0)
            sp.dma_start(GATEW, d["gate_w"].rearrange("a g h i j -> i (a g h) j")).then_inc(s_gw, 16)
            sp.wait_ge(s_mm, PROJ_TILES)
            for k in range(2):
                sp.dma_start(IDFT[0:FP, k, :, :], d["idft"][k].rearrange("(c p) n -> p c n", p=FP)).then_inc(s_idft, 16)
            sp.dma_start(RGOUT, d["rg_out"].rearrange("(c p) n -> p c n", p=P)).then_inc(s_rgo, 16)
            sp.wait_ge(s_gm, N_GATES)
            sp.dma_start(HYOUT, d["hy_out"].rearrange("(c p) n -> p c n", p=P)).then_inc(s_hyo, 16)
            sp.wait_ge(s_yrg, 2)
            sp.dma_start(WOUT, d["w_out"].rearrange("(c p) n -> p c n", p=P)).then_inc(s_wo, 16)

        @block.gpsimd
        def _(pool):
            nc.gpsimd.memset(ident, 0.0).then_inc(K.s_ident, 1)
            pool.wait_ge(K.s_ident, 1)
            nc.gpsimd.affine_select(out=ident, in_=ident, compare_op=ALU.not_equal, fill=1.0, base=0,
                                    pattern=[[-1, P]], channel_multiplier=1).then_inc(K.s_ident, 1)
            pool.dma_start(ZT, d["zT"]).then_inc(s_hy, 16)
            pool.dma_start(W1, d["hy_w1"]).then_inc(s_hy, 16)
            pool.dma_start(W2, d["hy_w2"]).then_inc(s_hy, 16)
            pool.dma_start(HB, d["hy_bf"]).then_inc(s_hy, 16)
            pool.dma_start(W3[0:HY_FFN + 1, :], d["hy_w3b"]).then_inc(s_hy, 16)
            for k in range(2):
                for c, (t0, n) in ((0, TC[0]), (2, TC[2])):
                    for dst, src in ((DECAY, "decay"), (DFT, "dft")):
                        if c == 0:
                            pool.dma_start(dst[:, k, 0:2, :], d[src][k, 0:2 * P, :].rearrange(
                                "(c p) n -> p c n", p=P)).then_inc(s_hy, 16)
                        else:
                            pool.dma_start(dst[0:n, k, 2, :], d[src][k, t0:L, :]).then_inc(s_hy, 16)

        @block.scalar
        def _(act):
            act.wait_ge(s_x, 32)
            act.wait_ge(s_ms, 1)
            for m in range(3):
                p = NM if m == 2 else P
                src = XN[0:NM, 2, :] if m == 2 else H[:, m, :]
                a.activation(SQ[0:p, :], src, ACT.Square, accum_out=SS[0:p, m:m + 1]).then_inc(s_sq, 1)
                act.wait_ge(s_sq, m + 1)
            act.wait_ge(s_ms, 2)
            a.activation(RSTD, SS, ACT.Sqrt).then_inc(s_root, 1)
            act.wait_ge(s_absl, 1)
            a.activation(LT[1], LT[0], ACT.Exp).then_inc(s_el, 1)
            act.wait_ge(s_arg, 1)
            a.activation(ARG, ARG, ACT.Sin).then_inc(s_sin, 1)
            act.wait_ge(s_arg, 2)
            act.wait_ge(s_fmm, 1)
            a.activation(HID[0:HY_FFN, :], ARG, ACT.Sin).then_inc(s_sin, 1)
            for n in range(6):
                act.wait_ge(s_kfm, n + 1)
                a.activation(KSP[0:FP, n // 3, n % 3, :], bank[4 + n % 4][0:FP, :], ACT.Copy).then_inc(s_ksp, 1)
            with act.Fori(0, PROJ_TILES // 2) as i:
                for k in range(2):
                    act.wait_ge(s_mm, i * 2 + k + 1)
                    a.activation(PROJ[:, bass.ds(i * 2 + k, 1), :], bank[k][:, 0:L], ACT.Identity,
                                 bias=COLS[:, bass.ds(i * 2 + k + COL["pbias"], 1)]).then_inc(s_ev, 1)
            act.wait_ge(s_ev, PROJ_TILES)
            act.wait_ge(s_lamc, 1)
            n = 0
            for dr in range(2):
                if dr:
                    act.wait_ge(s_scan, RH)
                for h in range(2 * RH):
                    act.wait_ge(s_gm, n + 1)
                    out = RR[:, dr * RH + h, :] if h < RH else II[:, h - RH, :]
                    a.activation(out, bank[2 + n % 2][:, 0:L], ACT.Sigmoid, bias=col("gbias", n)).then_inc(s_ga, 1)
                    n += 1
                act.wait_ge(s_ga, n)
                for h in range(RH):
                    c = dr * RH + h
                    a.activation(TH[:, h, :], RR[:, c, :], ACT.Tanh, scale=LAMC[:, c:c + 1]).then_inc(s_at, 1)
                act.wait_ge(s_at, dr * 2 * RH + RH)
                for h in range(RH):
                    c = dr * RH + h
                    a.activation(RR[:, c, :], RR[:, c, :], ACT.Exp, scale=NLAMC[:, c:c + 1]).then_inc(s_at, 1)
                act.wait_ge(s_m2, dr + 1)
                a.activation(TH, TH, ACT.Sqrt).then_inc(s_mu, 1)
                if dr == 0:
                    g = PROJ[:, T_G1:T_G1 + 2 * DC, NM:]
                    a.activation(g, g, ACT.Sigmoid).then_inc(s_sg, 1)
                    g = PROJ[:, T_RG:T_RG + RH, NM:]
                    a.activation(g, g, ACT.Gelu_apprx_tanh).then_inc(s_sg, 1)

        @block.tensor
        def _(te):
            te.wait_ge(s_hy, 16 * N_HY)
            pe.matmul(bank[6][0:HY_FFN, 0:L], W1, ZT, start=True, stop=True).then_inc(s_fmm, 1)
            te.wait_ge(K.s_ident, 2)
            te.wait_ge(s_xn, 3)
            for c in range(DC):
                if c >= 2:
                    te.wait_ge(s_nT, c - 1)
                cs = slice(c * P, (c + 1) * P)
                pe.transpose(bank[4 + c % 2][:, 0:NM], XN[0:NM, 2, cs], ident[0:NM, 0:NM])
                pe.transpose(bank[4 + c % 2][:, NM:NM + P], XN[:, 0, cs], ident)
                pe.transpose(bank[4 + c % 2][:, NM + P:L], XN[:, 1, cs], ident).then_inc(s_turn, 1)
            te.wait_ge(s_sin, 1)
            pe.matmul(bank[7][0:HY_FFN, 0:L], W2, ARG, start=True, stop=True).then_inc(s_fmm, 1)
            te.wait_ge(s_sin, 2)
            te.wait_ge(s_kpm, 1)
            te.wait_ge(s_nT, DC)
            for c, (t0, n) in enumerate(TC):
                if c == 2:
                    te.wait_ge(s_kpm, 2)
                for k in range(2):
                    pe.matmul(bank[4 + (2 * c + k + 2) % 4][0:n, :], HID[0:HY_FFN + 1, t0:t0 + n],
                              W3[0:HY_FFN + 1, k * D_HY:(k + 1) * D_HY], start=True, stop=True).then_inc(s_kmm, 1)
            te.wait_ge(s_kpm, 4)
            for n in range(6):
                if n >= 4:
                    te.wait_ge(s_ksp, n - 3)
                k, f = n // 3, n % 3
                for c, (t0, p) in enumerate(TC):
                    m = pe.matmul(bank[4 + n % 4][0:FP, :], DFT[0:p, k, c, f * FP:(f + 1) * FP], KPM[0:p, k, c, :],
                                  start=(c == 0), stop=(c == 2))
                m.then_inc(s_kfm, 1)

            def project(i, k, first=False):
                te.wait_ge(s_ring[k], i * 16 + 16)
                for q in range(4):
                    if not (first and q < 2):
                        te.wait_ge(s_ev, i * 8 + k * 4 + q - 1)
                    for c in range(DC):
                        m = pe.matmul(bank[q % 2][:, 0:L], RING[k][:, c, q * P:(q + 1) * P], NT[:, c, :],
                                      start=(c == 0), stop=(c == DC - 1))
                    m.then_inc(s_mm, 1)

            project(0, 0, True)
            project(0, 1)
            with te.Fori(1, BLOCKS // 2) as i:
                for k in range(2):
                    project(i, k)
            project(BLOCKS // 2, 0)

            def gates(dr):
                for h in range(2 * RH):
                    n = dr * 2 * RH + h
                    if n >= 2:
                        te.wait_ge(s_ga, n - 1)
                    pe.matmul(bank[2 + n % 2][:, 0:L], GATEW[:, n, :], XC[:, dr * RH + h % RH, :],
                              start=True, stop=True).then_inc(s_gm, 1)

            te.wait_ge(s_gw, 16)
            te.wait_ge(s_rgc, 8 * RH)
            gates(0)
            te.wait_ge(s_u, HT)
            te.wait_ge(s_ksp, 6)
            for c, (t0, n) in enumerate(TC):
                for t in range(HT):
                    m = pe.transpose(bank[4 + c][0:n, t * P:(t + 1) * P], HCV[:, t, t0:t0 + n], ident)
                m.then_inc(s_utm, 1)
            te.wait_ge(s_ut, 3)
            for f in range(3):
                if f == 2:
                    te.wait_ge(s_ysp, 1)
                for k in range(2):
                    for c, (t0, p) in enumerate(TC):
                        m = pe.matmul(bank[4 + (2 * f + k) % 4][0:FP, :], DFT[0:p, k, c, f * FP:(f + 1) * FP],
                                      UTOK[0:p, c, :], start=(c == 0), stop=(c == 2))
                m.then_inc(s_usm, 1)
            gates(1)
            te.wait_ge(s_ysp, 3)
            te.wait_ge(s_idft, 32)
            for t in range(HT):
                for n in range(6):
                    m = pe.matmul(bank[4 + t // 2][:, (t % 2) * T:(t % 2 + 1) * T],
                                  YSP[0:FP, n // 3, n % 3, t * P:(t + 1) * P], IDFT[0:FP, n // 3, n % 3, :],
                                  start=(n == 0), stop=(n == 5))
                m.then_inc(s_ymm, 1)
            te.wait_ge(s_yhy, HT)
            te.wait_ge(s_hyo, 16)
            for o in range(DC):
                for c in range(HT):
                    m = pe.matmul(bank[(6 + o // 2) % 8][:, (o % 2) * T:(o % 2 + 1) * T],
                                  HYOUT[:, c, o * P:(o + 1) * P], YHY[:, c, :], start=(c == 0), stop=(c == HT - 1))
            m.then_inc(s_hom, 1)
            te.wait_ge(s_yrg, 2)
            te.wait_ge(s_rgo, 16)
            for o in range(DC):
                for c in range(DC):
                    m = pe.matmul(bank[2 + o // 2][:, (o % 2) * T:(o % 2 + 1) * T],
                                  RGOUT[:, c, o * P:(o + 1) * P], YRG[:, c, :], start=(c == 0), stop=(c == DC - 1))
                if o % 2:
                    m.then_inc(s_rom, 1)
            te.wait_ge(s_mg, 4)
            te.wait_ge(s_wo, 16)
            for n in range(4):
                for c in range(DC):
                    m = pe.matmul(bank[n][:, :], MERGED[:, c, (n // 2) * P:(n // 2 + 1) * P],
                                  WOUT[:, c, (n % 2) * 512:(n % 2 + 1) * 512], start=(c == 0), stop=(c == DC - 1))
                m.then_inc(s_wm, 1)

        @block.vector
        def _(ve):
            ch = Count(K.s_dve)
            ch.n = K.dve_n

            def do(ins):
                ch.by(ins, ve)

            v.memset(SS, 0.0).then_inc(s_ms, 1)
            ve.wait_ge(s_sq, 3)
            ve.wait_ge(s_ms, 1)
            v.tensor_scalar(SS, SS, 1.0 / D, EPS, ALU.mult, ALU.add).then_inc(s_ms, 1)
            ve.wait_ge(s_root, 1)
            do(v.reciprocal(RSTD, RSTD))
            for m in range(3):
                p = NM if m == 2 else P
                src = XN[0:NM, 2, :] if m == 2 else H[:, m, :]
                v.tensor_scalar(XN[0:p, m, :], src, RSTD[0:p, m:m + 1], None, ALU.mult).then_inc(s_xn, 1)
            ve.wait_ge(s_cols, 16)
            lam = COLS[:, COL["lam"]:COL["lam"] + 2 * RH]
            v.scalar_tensor_tensor(LT[0], lam, -1.0, lam, ALU.mult, ALU.min).then_inc(s_absl, 1)

            def angle(src, b):
                do(v.tensor_scalar(ARG, src, HB[:, b:b + 1], HB[:, b + 1:b + 2], ALU.add, ALU.mult))
                do(v.tensor_scalar(TURNS, ARG, 1.0 / (2 * math.pi), ROUND, ALU.mult, ALU.add))
                do(v.tensor_scalar(TURNS, TURNS, ROUND, None, ALU.subtract))
                do(v.scalar_tensor_tensor(ARG, TURNS, -TWO_PI_HI, ARG, ALU.mult, ALU.add))
                do(v.scalar_tensor_tensor(ARG, TURNS, -TWO_PI_LO, ARG, ALU.mult, ALU.add))
                v.tensor_scalar(ARG, ARG, PI_IN, -PI_IN, ALU.min, ALU.max).then_inc(s_arg, 1)

            ve.wait_ge(s_fmm, 1)
            angle(bank[6][0:HY_FFN, 0:L], 0)
            for c in range(DC):
                ve.wait_ge(s_turn, c + 1)
                v.tensor_scalar(NT[:, c, :], bank[4 + c % 2][:, 0:L], col("gmix", c), None, ALU.mult).then_inc(s_nT, 1)
            ve.wait_ge(s_fmm, 2)
            angle(bank[7][0:HY_FFN, 0:L], 2)
            v.memset(HID[HY_FFN:HY_FFN + 1, :], 1.0).then_inc(s_kpm, 1)
            ve.wait_ge(s_el, 1)
            do(v.tensor_scalar(LT[2], LT[1], 2.0, None, ALU.add))
            do(v.reciprocal(LT[2], LT[2]))
            do(v.tensor_tensor(LT[2], LT[1], LT[2], ALU.mult))
            do(v.tensor_tensor(LT[3], LT[2], LT[2], ALU.mult))
            do(v.tensor_scalar(LT[4], LT[3], 1.0 / 17, None, ALU.mult))
            for n in range(15, 1, -2):
                do(v.scalar_tensor_tensor(LT[4], LT[4], 1.0 / n, LT[3], ALU.add, ALU.mult))
            do(v.scalar_tensor_tensor(LT[4], LT[4], 1.0, LT[2], ALU.add, ALU.mult))
            do(v.tensor_scalar(LT[5], lam, -1.0, 0.0, ALU.mult, ALU.max))
            do(v.scalar_tensor_tensor(LT[5], LT[4], 2.0, LT[5], ALU.mult, ALU.add))
            do(v.tensor_scalar(LAMC, LT[5], RG_C, None, ALU.mult))
            v.tensor_scalar(NLAMC, LT[5], -RG_C, None, ALU.mult).then_inc(s_lamc, 1)
            ve.wait_ge(s_xn, 3)
            for c, (t0, n) in enumerate(TC):
                ve.wait_ge(s_kmm, 2 * c + 2)
                for k in range(2):
                    do(v.tensor_tensor(KFB[0:n, k, :], bank[4 + (2 * c + k + 2) % 4][0:n, :], DECAY[0:n, k, c, :], ALU.mult))
                do(v.tensor_tensor(KPM[0:n, 0, c, :], KFB[0:n, 0, :], KFB[0:n, 1, :], ALU.add))
                v.tensor_tensor(KPM[0:n, 1, c, :], KFB[0:n, 0, :], KFB[0:n, 1, :], ALU.subtract).then_inc(s_kpm, 1)
                ve.wait_ge(s_kpm, c + 2)
            ve.wait_ge(s_nT, DC)
            with ve.Fori(0, RH) as h:
                ve.wait_ge(s_ev, h + 1)
                src = PROJ[:, bass.ds(h + T_RX, 1), :]

                def out(dr, lo, hi):
                    return XC[:, bass.ds(h + dr * RH, 1), lo:hi]

                def weight(dr, j):
                    return COLS[:, bass.ds(h + COL["rgw"] + (dr * RG_CONV + j) * RH, 1)]

                for j in range(RG_CONV):
                    if j:
                        ve.wait_ge(s_rgc, h * 8 + 2 * j)
                    if j == 0:
                        for dr in range(2):
                            v.tensor_scalar(out(dr, 0, L), src, weight(dr, 0),
                                            COLS[:, bass.ds(h + COL["rgb"] + dr * RH, 1)], ALU.mult, ALU.add).then_inc(s_rgc, 1)
                    else:
                        v.scalar_tensor_tensor(out(0, j, L), PROJ[:, bass.ds(h + T_RX, 1), 0:L - j], weight(0, j),
                                               out(0, j, L), ALU.mult, ALU.add).then_inc(s_rgc, 1)
                        v.scalar_tensor_tensor(out(1, 0, L - j), PROJ[:, bass.ds(h + T_RX, 1), j:L], weight(1, j),
                                               out(1, 0, L - j), ALU.mult, ALU.add).then_inc(s_rgc, 1)
            with ve.Fori(0, 3 * HT) as t:
                ve.wait_ge(s_ev, t + T_HY + 1)

                def tile(lo, hi):
                    return PROJ[:, bass.ds(t + T_HY, 1), lo:hi]

                def conv(lo, hi):
                    return HCV[:, bass.ds(t, 1), lo:hi]

                def tap(j):
                    return COLS[:, bass.ds(t + COL["hyw"] + j * 3 * HT, 1)]

                v.tensor_scalar(conv(0, L), tile(0, L), tap(1), COLS[:, bass.ds(t + COL["hyb"], 1)],
                                ALU.mult, ALU.add).then_inc(s_hyc, 1)
                ve.wait_ge(s_hyc, t * 3 + 1)
                v.scalar_tensor_tensor(conv(1, L), tile(0, L - 1), tap(0), conv(1, L), ALU.mult, ALU.add).then_inc(s_hyc, 1)
                ve.wait_ge(s_hyc, t * 3 + 2)
                v.scalar_tensor_tensor(conv(0, L - 1), tile(1, L), tap(2), conv(0, L - 1), ALU.mult, ALU.add).then_inc(s_hyc, 1)
            ve.wait_ge(s_hyc, 9 * HT)
            for t in range(HT):
                v.tensor_tensor(HCV[:, t, :], HCV[:, t, :], HCV[:, HT + t, :], ALU.mult).then_inc(s_u, 1)
            for c, (t0, n) in enumerate(TC):
                ve.wait_ge(s_utm, c + 1)
                ve.wait_ge(s_rgc, 8 * RH)
                v.tensor_copy(UTOK[0:n, c, :], bank[4 + c][0:n, :]).then_inc(s_ut, 1)

            def rg_input(dr):
                ve.wait_ge(s_at, 2 * RH * dr + RH)
                dst = RR[:, (1 - dr) * RH:(2 - dr) * RH, :]
                ve.wait_ge(s_kfm, 6)
                if dr:
                    ve.wait_ge(s_scan, RH)
                do(v.tensor_scalar(dst, TH, 1.0, None, ALU.add))
                do(v.reciprocal(dst, dst))
                v.scalar_tensor_tensor(TH, TH, 2.0, dst, ALU.mult, ALU.mult).then_inc(s_m2, 1)

            def rg_scan(dr):
                ve.wait_ge(s_mu, dr + 1)
                first = 0 if dr == 0 else L - 1
                do(v.memset(TH[:, :, first:first + 1], 1.0))
                do(v.tensor_tensor(II, II, TH, ALU.mult))
                XD = XC[:, dr * RH:(dr + 1) * RH, :]
                do(v.tensor_tensor(II, II, XD, ALU.mult))
                ve.wait_ge(s_at, 2 * RH * (dr + 1))
                ve.wait_ge(s_gm, 2 * RH * (dr + 1))
                for h in range(RH):
                    o, x, y = XC[:, dr * RH + h, :], RR[:, dr * RH + h, :], II[:, h, :]
                    if dr:
                        o, x, y = o[:, ::-1], x[:, ::-1], y[:, ::-1]
                    v.tensor_tensor_scan(o, x, y, 0.0, ALU.mult, ALU.add).then_inc(s_scan, 1)

            rg_input(0)
            for f in range(3):
                ve.wait_ge(s_usm, f + 1)
                ve.wait_ge(s_hyc, 9 * HT)
                ve.wait_ge(s_ksp, 6)
                uc, us = (bank[4 + (2 * f + k) % 4][0:FP, :] for k in range(2))
                t0, t1 = TMP[0:FP, 0, :], TMP[0:FP, 1, :]
                kc, ks = KSP[0:FP, 0, f, :], KSP[0:FP, 1, f, :]
                do(v.tensor_tensor(t0, uc, kc, ALU.mult))
                do(v.tensor_tensor(t1, us, ks, ALU.mult))
                do(v.tensor_tensor(YSP[0:FP, 0, f, :], t0, t1, ALU.subtract))
                do(v.tensor_tensor(t0, uc, ks, ALU.mult))
                do(v.tensor_tensor(t1, us, kc, ALU.mult))
                v.tensor_tensor(YSP[0:FP, 1, f, :], t0, t1, ALU.add).then_inc(s_ysp, 1)
                ve.wait_ge(s_ysp, f + 1)
            rg_scan(0)
            for t in range(HT):
                ve.wait_ge(s_ymm, t // 2 * 2 + 2)
                if t == 0:
                    ve.wait_ge(s_u, HT)
                do(v.scalar_tensor_tensor(YHY[:, t, :], HCV[:, t, NM:], col("skip", t),
                                          bank[4 + t // 2][:, (t % 2) * T:(t % 2 + 1) * T], ALU.mult, ALU.add))
                v.tensor_tensor(YHY[:, t, :], YHY[:, t, :], HCV[:, 2 * HT + t, NM:], ALU.mult).then_inc(s_yhy, 1)
            rg_input(1)
            rg_scan(1)
            ve.wait_ge(s_scan, 2 * RH)
            v.tensor_tensor(YRG, XC[:, 0:RH, NM:], XC[:, RH:, NM:], ALU.add).then_inc(s_yrg, 1)
            ve.wait_ge(s_yrg, 1)
            ve.wait_ge(s_sg, 2)
            v.tensor_tensor(YRG, YRG, PROJ[:, T_RG:T_RG + RH, NM:], ALU.mult).then_inc(s_yrg, 1)
            ve.wait_ge(s_hom, 1)
            for n in range(4):
                ve.wait_ge(s_rom, n + 1)
                g1 = PROJ[:, T_G1 + 2 * n:T_G1 + 2 * n + 2, NM:]
                g2 = PROJ[:, T_G2 + 2 * n:T_G2 + 2 * n + 2, NM:]
                hy = bank[(6 + n) % 8][:, :].rearrange("p (a b) -> p a b", a=2)
                rg = bank[2 + n][:, :].rearrange("p (a b) -> p a b", a=2)
                t0 = TMP[:, 0, :].rearrange("p (a b) -> p a b", a=2)
                t1 = TMP[:, 1, :].rearrange("p (a b) -> p a b", a=2)
                do(v.tensor_tensor(t0, hy, g1, ALU.mult))
                do(v.tensor_tensor(t1, rg, g2, ALU.mult))
                v.tensor_tensor(MERGED[:, 2 * n:2 * n + 2, :], t0, t1, ALU.add).then_inc(s_mg, 1)
                ve.wait_ge(s_mg, n + 1)
            for n in range(4):
                ve.wait_ge(s_wm, n + 1)
                o = H[:, n // 2, (n % 2) * 512:(n % 2 + 1) * 512]
                do(v.tensor_tensor(o, o, bank[n][:, :], ALU.add))
            K.dve_n = ch.n


def peer_stage(K):
    nc, cut, bank, sem, d, ident, H = K.nc, K.cut, K.bank, K.sem, K.dram, K.ident, K.h_res
    v, a, pe = nc.vector, nc.scalar, nc.tensor
    R = 8
    HP = 2 * PH
    N = TT * SLOTS
    assert SLOTS % R == 0

    at = Room(K.cols)
    XF = cut(at.take(TT * D), P, TT, D)
    XT = cut(at.take(DC * T), P, DC, T)
    wqo = at.take(DC * HP * P)
    WQ = cut(wqo, P, 4, DC, 4 * P)
    QT = cut(at.take(HP * T), P, HP, T)
    KEYS = cut(at.take(HP * NKEYS), P, HP, NKEYS)
    S = cut(at.take(TT * HP * NKEYS), P, TT, HP, NKEYS)
    S2 = cut(wqo, P, 2 * D)
    EQ = cut(wqo + 2 * D, P, SLOTS, TOPK)
    CAND = cut(wqo + 4 * D, P, PH, TOPK * TOPK)
    TS = cut(at.take(HP * TOPK), P, PH, 2, TOPK)
    TIo = at.take(HP * TOPK)
    TI = cut(TIo, P, PH, 2, TOPK).bitcast(U32)
    TIF = cut(at.take(HP * TOPK), P, PH, 2, TOPK)
    CS = cut(at.take(SLOTS), P, PH, TOPK)
    CI = cut(at.take(SLOTS), P, PH, TOPK).bitcast(U32)
    CJ = cut(at.take(SLOTS), P, SLOTS).bitcast(U32)
    CF = cut(at.take(2 * SLOTS), P, 2, SLOTS)
    E12 = cut(at.take(2 * SLOTS), P, 2, SLOTS)
    IDX = cut(at.take(TT * SLOTS), P, TT * SLOTS).bitcast(U32)
    GATE = cut(at.take(TT * SLOTS), P, TT, SLOTS)
    DOT = cut(at.take(TT * SLOTS), P, TT, SLOTS)
    WGT = cut(at.take(TT * SLOTS), P, TT, SLOTS)
    ROWS = cut(at.take(R * D), P, R, D)
    PROD = cut(at.take(D), P, D)
    DIAG = cut(at.take(R * P), P, R, P)
    GF = cut(at.take(D), P, D)
    GL = cut(at.take(D), P, D)
    IOTA = cut(at.take(TOPK), P, TOPK)
    ICOL = cut(at.take(R), P, R).bitcast(U32)
    SM = cut(at.take(25), P, 25)
    DOTS = cut(at.take(R), P, R)
    SS, RSTD, SUM, RSUM = SM[:, 0:2], SM[:, 2:4], SM[:, 4:12], SM[:, 12:20]
    HELD, HELD0 = SM[:, 24:25], IOTA[:, 0:1]

    s_g, s_keys = sem("peer_gains_in"), sem("peer_keys_in")
    s_wq = [sem(f"peer_wq{k}_in") for k in range(4)]
    s_iota = sem("peer_iota")
    s_sq, s_ms, s_root, s_xf, s_tr, s_xt = (sem("peer_" + n) for n in ("squares", "meansq", "root", "xn", "turned", "xT"))
    s_qm, s_q, s_sm, s_s = sem("peer_q_mm"), sem("peer_qT"), sem("peer_score_mm"), sem("peer_scores")
    s_cs, s_ex, s_idx = sem("peer_chosen"), sem("peer_exp"), sem("peer_indices")
    s_icol = sem("peer_index_col")
    s_row = [K.lasting_sem(f"peer_row{k}_in") for k in range(R)]
    s_dot, s_gel, s_wgt, s_diag, s_pv = (sem("peer_" + n) for n in ("dots", "gelu", "weights", "diag", "rows_summed"))
    s_h, s_turn = sem("peer_h"), sem("peer_dots_kept")

    with nc.Block() as block:
        @block.sync
        def _(sp):
            sp.dma_start(GF, d["g_ffn"].partition_broadcast(P)).then_inc(s_g, 16)
            sp.dma_start(GL, d["g_final"].partition_broadcast(P)).then_inc(s_g, 16)
            wq = d["wq"].rearrange("(c p) n -> p c n", p=P)
            for k in range(4):
                sp.dma_start(WQ[:, k, :, :], wq[:, :, k * 4 * P:(k + 1) * 4 * P]).then_inc(s_wq[k], 16)
            sp.dma_start(KEYS, d["keysT"]).then_inc(s_keys, 16)

        @block.gpsimd
        def _(pool):
            K.clear_stale(pool)
            nc.gpsimd.iota(IOTA, pattern=[[1, TOPK]], base=0, channel_multiplier=0,
                           allow_small_or_imprecise_dtypes=True).then_inc(s_iota, 1)

            def gather(table, slot, k):
                nc.gpsimd.tensor_copy(ICOL[:, k:k + 1], IDX[:, bass.ds(slot, 1)]).then_inc(s_icol, 1)

            def hold(n):
                pool.wait_ge(s_icol, n * 2 + 1)
                nc.gpsimd.tensor_tensor(HELD, HELD0, HELD0, ALU.add).then_inc(s_icol, 1)

            def send(table, k):
                nc.gpsimd.indirect_dma_start(ROWS[:, k, :], None, table,
                                             bass.IndirectOffsetOnAxis(ICOL[:, k:k + 1], 0)).then_inc(s_row[k], 16)

            pool.wait_ge(s_iota, 1)
            pool.wait_ge(s_idx, 1)
            for k in range(R):
                gather(d["peer_u"], k, k)
                hold(k)
                send(d["peer_u"], k)
            for t in range(TT):
                pool.wait_ge(s_idx, t + 1)
                with pool.Fori(1 if t == 0 else t * SLOTS // R, (t + 1) * SLOTS // R) as i:
                    for k in range(R):
                        pool.wait_ge(s_dot, i * R + (k - R + 1))
                        gather(d["peer_u"], i * R + k, k)
                        hold(i * R + k)
                        send(d["peer_u"], k)
            for k in range(R):
                pool.wait_ge(s_dot, N - R + k + 1)
                gather(d["peer_v"], k, k)
                hold(N + k)
                send(d["peer_v"], k)
            with pool.Fori(1, N // R) as i:
                for k in range(R):
                    pool.wait_ge(s_pv, i * R + (k - R + 1))
                    gather(d["peer_v"], i * R + k, k)
                    hold(i * R + (N + k))
                    send(d["peer_v"], k)

        def normalise_act(act, src, base):
            act.wait_ge(s_ms, 1)
            for t in range(TT):
                a.activation(PROD, src[:, t, :], ACT.Square, accum_out=SS[:, t:t + 1]).then_inc(s_sq, 1)
                act.wait_ge(s_sq, base + t + 1)

        @block.scalar
        def _(act):
            normalise_act(act, H, 0)
            act.wait_ge(s_ms, 2)
            a.activation(RSTD, SS, ACT.Sqrt).then_inc(s_root, 1)
            for c in range(DC):
                act.wait_ge(s_tr, c + 1)
                a.activation(XT[:, c, :], bank[c % 2][:, 0:T], ACT.Copy).then_inc(s_xt, 1)
            for n in range(HP):
                act.wait_ge(s_qm, n + 1)
                a.activation(QT[:, n, :], bank[2 + n % 2][:, 0:T], ACT.Copy).then_inc(s_q, 1)
            for n in range(2 * 4):
                act.wait_ge(s_sm, n + 1)
                a.activation(S[:, n // 4, n % 4 * 4:n % 4 * 4 + 4, :], bank[4 + n % 4][:, :].rearrange(
                    "p (a b) -> p a b", a=4), ACT.Copy).then_inc(s_s, 1)
            for t in range(TT):
                act.wait_ge(s_cs, t + 1)
                a.activation(GATE[:, t, :], GATE[:, t, :], ACT.Exp).then_inc(s_ex, 1)
            for t in range(TT):
                act.wait_ge(s_turn, (t + 1) * SLOTS // R)
                a.activation(WGT[:, t, :], DOT[:, t, :], ACT.Gelu_apprx_tanh).then_inc(s_gel, 1)
            act.wait_ge(s_wgt, TT)
            weight = WGT.rearrange("p a b -> p (a b)")

            def diag(slot, k):
                a.activation(DIAG[:, k, :], ident, ACT.Copy, scale=weight[:, bass.ds(slot, 1)]).then_inc(s_diag, 1)

            for k in range(R):
                diag(k, k)
            with act.Fori(1, N // R) as i:
                for k in range(R):
                    act.wait_ge(s_pv, i * R + (k - R + 1))
                    diag(i * R + k, k)
            act.wait_ge(s_h, 1)
            for t in range(TT):
                a.activation(PROD, H[:, t, :], ACT.Square, accum_out=SS[:, t:t + 1]).then_inc(s_sq, 1)
                act.wait_ge(s_sq, TT + t + 1)
            act.wait_ge(s_ms, 3)
            a.activation(RSTD, SS, ACT.Sqrt).then_inc(s_root, 1)

        @block.tensor
        def _(te):
            te.wait_ge(s_xf, TT)
            for c in range(DC):
                if c >= 2:
                    te.wait_ge(s_xt, c - 1)
                for t in range(TT):
                    m = pe.transpose(bank[c % 2][:, t * P:(t + 1) * P], XF[:, t, c * P:(c + 1) * P], ident)
                m.then_inc(s_tr, 1)
            te.wait_ge(s_xt, DC)
            for n in range(HP):
                te.wait_ge(s_wq[n // 4], 16)
                if n >= 2:
                    te.wait_ge(s_q, n - 1)
                for c in range(DC):
                    m = pe.matmul(bank[2 + n % 2][:, 0:T], WQ[:, n // 4, c, n % 4 * P:(n % 4 + 1) * P], XT[:, c, :],
                                  start=(c == 0), stop=(c == DC - 1))
                m.then_inc(s_qm, 1)
            te.wait_ge(s_keys, 16)
            te.wait_ge(s_q, HP)
            for n in range(2 * 4):
                if n >= 4:
                    te.wait_ge(s_s, n - 3)
                for j in range(4):
                    hp = n % 4 * 4 + j
                    m = pe.matmul(bank[4 + n % 4][:, j * P:(j + 1) * P], QT[:, hp, n // 4 * P:(n // 4 + 1) * P],
                                  KEYS[:, hp, :], start=True, stop=True)
                m.then_inc(s_sm, 1)

            def add_rows(i, k, t, turn, start, stop):
                te.wait_ge(s_row[k], turn * 16 + 16)
                te.wait_ge(s_diag, i * R + (k + 1))
                for n in range(2):
                    m = pe.matmul(bank[2 * t + n][:, :], DIAG[:, k, :], ROWS[:, k, n * 512:(n + 1) * 512],
                                  start=start, stop=stop)
                m.then_inc(s_pv, 1)

            U_TURNS = N // R
            for t in range(TT):
                lo, hi = t * SLOTS // R, (t + 1) * SLOTS // R
                for k in range(R):
                    add_rows(lo, k, t, U_TURNS + lo, k == 0, False)
                with te.Fori(lo + 1, hi - 1) as i:
                    for k in range(R):
                        add_rows(i, k, t, i + U_TURNS, False, False)
                for k in range(R):
                    add_rows(hi - 1, k, t, U_TURNS + hi - 1, False, k == R - 1)

        @block.vector
        def _(ve):
            ch = Count(K.s_dve)
            ch.n = K.dve_n

            def do(ins):
                ch.by(ins, ve)

            v.memset(SS, 0.0).then_inc(s_ms, 1)
            ve.wait_ge(s_sq, TT)
            ve.wait_ge(s_ms, 1)
            v.tensor_scalar(SS, SS, 1.0 / D, EPS, ALU.mult, ALU.add).then_inc(s_ms, 1)
            ve.wait_ge(s_root, 1)
            do(v.reciprocal(RSTD, RSTD))
            ve.wait_ge(s_g, 32)
            for t in range(TT):
                v.scalar_tensor_tensor(XF[:, t, :], H[:, t, :], RSTD[:, t:t + 1], GF, ALU.mult, ALU.mult).then_inc(s_xf, 1)
            ve.wait_ge(s_iota, 1)

            def top16(val, idx, src, spare):
                do(v.max(val[:, 0:8], src))
                do(v.match_replace(spare, val[:, 0:8], src, -BIG))
                do(v.max_index(idx[:, 0:8], val[:, 0:8], src))
                do(v.max(val[:, 8:16], spare))
                do(v.max_index(idx[:, 8:16], val[:, 8:16], spare))

            for t in range(TT):
                for hp in range(HP):
                    if hp % 4 == 0:
                        ve.wait_ge(s_s, t * 4 + hp // 4 + 1)
                    top16(TS[:, hp // 2, hp % 2, :], TI[:, hp // 2, hp % 2, :], S[:, t, hp, :], S2[:, 0:NKEYS])
                do(v.tensor_copy(TIF, TI))
                full = [P, PH, TOPK, TOPK]
                do(v.tensor_tensor(CAND.rearrange("p h (i j) -> p h i j", i=TOPK),
                                   TS[:, :, 0, :].unsqueeze(3).to_broadcast(full),
                                   TS[:, :, 1, :].unsqueeze(2).to_broadcast(full), ALU.add))
                for h in range(PH):
                    top16(CS[:, h, :], CI[:, h, :], CAND[:, h, :], S2[:, 0:TOPK * TOPK])
                gate = GATE[:, t, :].rearrange("p (h k) -> p h k", h=PH)
                v.tensor_tensor(gate, CS, CS[:, :, 0:1].to_broadcast([P, PH, TOPK]), ALU.subtract).then_inc(s_cs, 1)
                ci = CI.rearrange("p h k -> p (h k)")
                eq4 = EQ.rearrange("p (h k) i -> p h k i", h=PH)
                for half in range(2):
                    op = (ALU.logical_shift_right, 4) if half == 0 else (ALU.bitwise_and, 15)
                    do(v.tensor_scalar(CJ, ci, op[1], None, op[0]))
                    do(v.tensor_copy(CF[:, half, :], CJ))
                    do(v.tensor_tensor(EQ, CF[:, half, :].unsqueeze(2).to_broadcast([P, SLOTS, TOPK]),
                                       IOTA.unsqueeze(1).to_broadcast([P, SLOTS, TOPK]), ALU.is_equal))
                    do(v.tensor_tensor(eq4, eq4, TIF[:, :, half, :].unsqueeze(2).to_broadcast(full), ALU.mult))
                    do(v.tensor_reduce(E12[:, half, :], EQ, X_AXIS, ALU.add))
                v.scalar_tensor_tensor(IDX[:, t * SLOTS:(t + 1) * SLOTS], E12[:, 0, :], float(NKEYS), E12[:, 1, :],
                                       ALU.mult, ALU.add).then_inc(s_idx, 1)
                ve.wait_ge(s_ex, t + 1)
                do(v.tensor_reduce(SUM, gate, X_AXIS, ALU.add))
                do(v.reciprocal(RSUM, SUM))
                do(v.tensor_tensor(gate, gate, RSUM.unsqueeze(2).to_broadcast([P, PH, TOPK]), ALU.mult))
            for t in range(TT):
                dot = DOT.rearrange("p a b -> p (a b)")
                with ve.Fori(t * SLOTS // R, (t + 1) * SLOTS // R) as i:
                    for k in range(R):
                        ve.wait_ge(s_row[k], i * 16 + 16)
                        v.tensor_tensor_reduce(S2[:, k % 2 * D:(k % 2 + 1) * D], ROWS[:, k, :], XF[:, t, :],
                                               1.0, 0.0, ALU.mult, ALU.add, DOTS[:, k:k + 1]).then_inc(s_dot, 1)
                        ve.wait_ge(s_dot, i * R + (k + 1))
                    v.tensor_copy(dot[:, bass.ds(i * R, R)], DOTS).then_inc(s_turn, 1)
                    ve.wait_ge(s_turn, i + 1)
                ve.wait_ge(s_gel, t + 1)
                v.tensor_tensor(WGT[:, t, :], WGT[:, t, :], GATE[:, t, :], ALU.mult).then_inc(s_wgt, 1)
            for t in range(TT):
                ve.wait_ge(s_pv, (t + 1) * SLOTS)
                for n in range(2):
                    o = H[:, t, n * 512:(n + 1) * 512]
                    do(v.tensor_tensor(o, o, bank[2 * t + n][:, :], ALU.add))
            v.memset(SS, 0.0).then_inc(s_h, 1)
            ve.wait_ge(s_sq, 2 * TT)
            v.tensor_scalar(SS, SS, 1.0 / D, EPS, ALU.mult, ALU.add).then_inc(s_ms, 1)
            ve.wait_ge(s_root, 2)
            do(v.reciprocal(RSTD, RSTD))
            for t in range(TT):
                do(v.scalar_tensor_tensor(H[:, t, :], H[:, t, :], RSTD[:, t:t + 1], GL, ALU.mult, ALU.mult))
            K.dve_n = ch.n


def layer_norm_scales(ve, do, v, src, cent, scratch, mean, ss, width, var_done):
    for t in range(TT):
        do(v.tensor_reduce(mean[:, t:t + 1], src[:, t, :], X_AXIS, ALU.add))
    do(v.tensor_scalar(mean, mean, 1.0 / width, None, ALU.mult))
    for t in range(TT):
        do(v.tensor_scalar(cent[:, t, :], src[:, t, :], mean[:, t:t + 1], None, ALU.subtract))
        do(v.tensor_tensor_reduce(scratch[:, 0:width], cent[:, t, :], cent[:, t, :], 1.0, 0.0, ALU.mult, ALU.add, ss[:, t:t + 1]))
    v.tensor_scalar(ss, ss, 1.0 / width, LN_EPS, ALU.mult, ALU.add).then_inc(var_done, 1)


def layer_norm_apply(ve, do, v, dst, cent, rstd, g, b, root_done, n):
    ve.wait_ge(root_done, n)
    do(v.reciprocal(rstd, rstd))
    for t in range(TT):
        do(v.scalar_tensor_tensor(dst[:, t, :], cent[:, t, :], rstd[:, t:t + 1], g, ALU.mult, ALU.mult))
    for t in range(TT):
        do(v.tensor_tensor(dst[:, t, :], dst[:, t, :], b, ALU.add))


def attention_stage(K, layer):
    nc, cut, bank, d, ident, H = K.nc, K.cut, K.bank, K.dram, K.ident, K.h_res
    v, a, pe = nc.vector, nc.scalar, nc.tensor
    gating = layer == 0

    def sem(name):
        return K.sem(f"att{layer}_{name}")

    HEADS = MEM_H if gating else N_DH + MEM_H
    DIL = HEADS - MEM_H
    UNITS = [(h, t) for t in range(TT) for h in range(HEADS)]
    CW = SG_W + MEM_W if gating else HPD * HD + MEM_W
    CC = CW // P
    QTILES = 2 if gating else (DIL + MEM_H) * HD // P

    at = Room(K.cols)
    XT = cut(at.take(DC * T), P, DC, T)
    MEMT = cut(at.take(DC * T), P, DC, T)
    wmk = at.take(DC * MEM_W)
    WMK = cut(wmk, P, DC, MEM_W)
    WMV = cut(at.take(DC * MEM_W), P, DC, MEM_W)
    MKT = cut(at.take(2 * T), P, 2, T)
    MV = cut(at.take(2 * MEM_W), P, 2, MEM_W)
    QT = cut(at.take(QTILES * T), P, QTILES, T)
    SB = cut(at.take(2 * T), P, 2, T)
    PB = cut(at.take(2 * T), P, 2, T)
    PT = cut(at.take(2 * T), P, 2, 2, P)
    OALL = cut(at.take(TT * HEADS * HD), P, TT, HEADS, HD)
    MIX = cut(at.take(TT * CW), P, TT, CW)
    MIXT = cut(at.take(CC * T), P, CC, T)
    WO = cut(at.take(CC * D) if gating else wmk, P, CC, D)
    LG = cut(at.take(D), P, D)
    LB = cut(at.take(D), P, D)
    SCR = cut(at.take(D), P, D)
    stats = cut(at.take(400), P, 400)
    NEGM, LSUM, RL = (stats[:, 64 * n:64 * n + TT * HEADS].rearrange("p (t h) -> p t h", t=TT) for n in range(3))
    MEAN, SS, RSTD = stats[:, 200:202], stats[:, 202:204], stats[:, 204:206]
    SGB = stats[:, 210:210 + N_SG]
    lse, lmx, lex, lsm = (stats[:, 224 + 24 * n:248 + 24 * n] for n in range(4))
    if gating:
        WIN = cut(at.take(DC * (2 * SG_W + MEM_W)), P, DC, 2 * SG_W + MEM_W)
        UG = cut(at.take(TT * 2 * SG_W), P, TT, 2 * SG_W)
        SGW = cut(at.take(N_SG * P), P, N_SG, P)
        SGG = cut(at.take(SG_W), P, SG_W)
        SGO = cut(at.take(SG_W), P, SG_W)
        q_at = 2 * SG_W
    else:
        WIN = cut(at.take(DC * (DIL * HD + MEM_W)), P, DC, DIL * HD + MEM_W)
        WK = cut(at.take(DC * DIL * HD), P, DC, DIL * HD)
        WV = cut(at.take(DC * DIL * HD), P, DC, DIL * HD)
        KT = cut(at.take(DIL * HD // P * T), P, DIL * HD // P, T)
        VV = cut(at.take(TT * DIL * HD), P, TT, DIL * HD)
        BIAS = cut(at.take(DIL * (P + T)), P, DIL, P + T)
        q_at = 0
    CENT = cut(0, P, TT, D)
    assert CENT is not None

    s_mem, s_win, s_kv, s_wo, s_par = (sem(n) for n in ("mem_in", "win_in", "kv_in", "wout_in", "params_in"))
    s_xt, s_x, s_mk, s_mko = sem("x_turned"), sem("xT"), sem("mem_kv_mm"), sem("mem_kv")
    s_pm, s_pj = sem("proj_mm"), sem("proj")
    s_sm, s_sb, s_ex, s_tm, s_pt, s_vm, s_o = (sem(n) for n in (
        "score_mm", "score_max", "exp", "p_turned", "pT", "pv_mm", "heads"))
    s_var, s_root = sem("variance"), sem("root")
    s_msk, s_gv, s_gm, s_mix = sem("masked"), sem("gv"), sem("gate_mm"), sem("mix")
    s_lse, s_ln, s_le = sem("sums"), sem("log_sum"), sem("lse_exp")
    s_mt, s_mixt, s_om = sem("mix_turned"), sem("mixT"), sem("out_mm")
    JOBS = [("q", n) for n in range(QTILES)]
    if gating:
        JOBS += [("ug", n) for n in range(3 * TT)]
    else:
        JOBS += [("k", n) for n in range(DIL * HD // P)] + [("v", n) for n in range(2 * TT)]
    NPAR = 5 if gating else 3

    def keys_of(u):
        h, t = UNITS[u]
        return P * (t + 1) if h < DIL else T

    with nc.Block() as block:
        @block.sync
        def _(sp):
            def rows(name):
                return d[name].rearrange("(c p) n -> p c n", p=P)

            sp.dma_start(MEMT, rows("memT")).then_inc(s_mem, 16)
            sp.dma_start(WMK, rows(f"w_mem_k{layer}")).then_inc(s_mem, 16)
            sp.dma_start(WMV, rows(f"w_mem_v{layer}")).then_inc(s_mem, 16)
            sp.dma_start(WIN, rows(f"w_in{layer}")).then_inc(s_win, 16)
            if not gating:
                sp.dma_start(WK, rows("w_k")).then_inc(s_kv, 16)
                sp.dma_start(WV, rows("w_v")).then_inc(s_kv, 16)
                sp.dma_start(BIAS, d["dil_bias"]).then_inc(s_par, 16)
            else:
                sp.dma_start(SGW, d["sg_wT"]).then_inc(s_par, 16)
                sp.dma_start(SGB, d["sg_bT"]).then_inc(s_par, 16)
                sp.dma_start(SGG, d["sg_ln_g"].partition_broadcast(P)).then_inc(s_par, 16)
                sp.dma_start(SGO, d["sg_ln_b"].partition_broadcast(P)).then_inc(s_par, 16)
            sp.dma_start(LG, d["ln1_g"][layer].partition_broadcast(P)).then_inc(s_wo, 16)
            sp.dma_start(LB, d["ln1_b"][layer].partition_broadcast(P)).then_inc(s_wo, 16)
            if not gating:
                sp.wait_ge(s_mk, 4)
            sp.dma_start(WO, rows(f"w_out{layer}")).then_inc(s_wo, 16)

        @block.gpsimd
        def _(pool):
            K.clear_stale(pool)
            if gating:
                pool.wait_ge(s_par, 64)
                nc.gpsimd.affine_select(out=SGW, in_=SGW, compare_op=ALU.is_ge, fill=0.0, base=0,
                                        pattern=[[0, N_SG], [1, P]], channel_multiplier=-1).then_inc(s_msk, 1)

        @block.scalar
        def _(act):
            for n in range(4):
                act.wait_ge(s_mk, n + 1)
                dst = MKT[:, n, :] if n < 2 else MV[:, n - 2, :]
                a.activation(dst, bank[4 + n][:, 0:T], ACT.Copy).then_inc(s_mko, 1)
            for c in range(DC):
                act.wait_ge(s_xt, c + 1)
                a.activation(XT[:, c, :], bank[c % 2][:, 0:T], ACT.Copy).then_inc(s_x, 1)
            for n, (kind, i) in enumerate(JOBS):
                act.wait_ge(s_pm, n + 1)
                b = bank[2 + n % 2]
                if kind == "q":
                    m = a.activation(QT[:, i, :], b[:, 0:T], ACT.Copy)
                elif kind == "k":
                    m = a.activation(KT[:, i, :], b[:, 0:T], ACT.Copy)
                elif kind == "v":
                    w = DIL * HD // 2
                    m = a.activation(VV[:, i // 2, i % 2 * w:(i % 2 + 1) * w], b[:, 0:w], ACT.Copy)
                else:
                    m = a.activation(UG[:, i // 3, i % 3 * 512:(i % 3 + 1) * 512], b[:, :], ACT.Gelu)
                m.then_inc(s_pj, 1)
            if gating:
                act.wait_ge(s_var, 1)
                a.activation(RSTD, SS, ACT.Sqrt).then_inc(s_root, 1)

            def turned(u):
                act.wait_ge(s_tm, u + 1)
                if u >= 2:
                    act.wait_ge(s_vm, u - 1)
                n = keys_of(u) // P
                a.activation(PT[:, u % 2, 0:n, :], bank[2 + u % 2][:, 0:n * P].rearrange(
                    "p (a b) -> p a b", a=n), ACT.Copy).then_inc(s_pt, 1)

            for u, (h, t) in enumerate(UNITS):
                n = keys_of(u)
                act.wait_ge(s_sb, u + 1)
                if u >= 2:
                    act.wait_ge(s_tm, u - 1)
                a.activation(PB[:, u % 2, 0:n], SB[:, u % 2, 0:n], ACT.Exp, bias=NEGM[:, t, h:h + 1],
                             accum_out=LSUM[:, t, h:h + 1]).then_inc(s_ex, 1)
                if u:
                    turned(u - 1)
            turned(len(UNITS) - 1)
            if not gating:
                act.wait_ge(s_ex, len(UNITS))
                a.activation(lse.rearrange("p (t h) -> p t h", t=TT), LSUM[:, :, 0:DIL], ACT.Ln).then_inc(s_ln, 1)
                act.wait_ge(s_lse, 1)
                a.activation(lex, lex, ACT.Exp).then_inc(s_le, 1)
            act.wait_ge(s_mt, 1)
            for c in range(CC):
                act.wait_ge(s_mt, c + 1)
                a.activation(MIXT[:, c, :], bank[c % 2][:, 0:T], ACT.Copy).then_inc(s_mixt, 1)
            act.wait_ge(s_var, 2 if gating else 1)
            a.activation(RSTD, SS, ACT.Sqrt).then_inc(s_root, 1)

        @block.tensor
        def _(te):
            te.wait_ge(s_mem, 48)
            for n in range(4):
                for c in range(DC):
                    if n < 2:
                        m = pe.matmul(bank[4 + n][:, 0:T], WMK[:, c, n * P:(n + 1) * P], MEMT[:, c, :],
                                      start=(c == 0), stop=(c == DC - 1))
                    else:
                        m = pe.matmul(bank[4 + n][:, 0:MEM_W], MEMT[:, c, (n - 2) * P:(n - 1) * P], WMV[:, c, :],
                                      start=(c == 0), stop=(c == DC - 1))
                m.then_inc(s_mk, 1)
            for c in range(DC):
                if c >= 2:
                    te.wait_ge(s_x, c - 1)
                for t in range(TT):
                    m = pe.transpose(bank[c % 2][:, t * P:(t + 1) * P], H[:, t, c * P:(c + 1) * P], ident)
                m.then_inc(s_xt, 1)
            te.wait_ge(s_x, DC)
            te.wait_ge(s_win, 16)
            for n, (kind, i) in enumerate(JOBS):
                if n >= 2:
                    te.wait_ge(s_pj, n - 1)
                if kind in "kv":
                    te.wait_ge(s_kv, 32)
                b = bank[2 + n % 2]
                for c in range(DC):
                    if kind in "qk":
                        w = WIN[:, c, q_at + i * P:q_at + (i + 1) * P] if kind == "q" else WK[:, c, i * P:(i + 1) * P]
                        m = pe.matmul(b[:, 0:T], w, XT[:, c, :], start=(c == 0), stop=(c == DC - 1))
                    elif kind == "v":
                        w = DIL * HD // 2
                        m = pe.matmul(b[:, 0:w], XT[:, c, i // 2 * P:(i // 2 + 1) * P], WV[:, c, i % 2 * w:(i % 2 + 1) * w],
                                      start=(c == 0), stop=(c == DC - 1))
                    else:
                        m = pe.matmul(b[:, :], XT[:, c, i // 3 * P:(i // 3 + 1) * P], WIN[:, c, i % 3 * 512:(i % 3 + 1) * 512],
                                      start=(c == 0), stop=(c == DC - 1))
                m.then_inc(s_pm, 1)
            te.wait_ge(s_pj, len(JOBS))
            te.wait_ge(s_mko, 4)

            def scores(u):
                h, t = UNITS[u]
                r = slice(h % 2 * HD, (h % 2 + 1) * HD)
                if u >= 2:
                    te.wait_ge(s_sb, u - 1)
                keys = MKT[r, (h - DIL) // 2, :] if h >= DIL else KT[r, h // 2, 0:keys_of(u)]
                pe.matmul(bank[u % 2][:, 0:keys_of(u)], QT[r, h // 2, t * P:(t + 1) * P], keys,
                          start=True, stop=True).then_inc(s_sm, 1)

            def turn(u):
                te.wait_ge(s_ex, u + 1)
                if u >= 2:
                    te.wait_ge(s_pt, u - 1)
                for n in range(keys_of(u) // P):
                    m = pe.transpose(bank[2 + u % 2][:, n * P:(n + 1) * P], PB[:, u % 2, n * P:(n + 1) * P], ident)
                m.then_inc(s_tm, 1)

            def values(u):
                h, t = UNITS[u]
                te.wait_ge(s_pt, u + 1)
                n = keys_of(u) // P
                b = bank[4 + 2 * t + h // 8]
                for k in range(n):
                    vals = MV[:, k, (h - DIL) * HD:(h - DIL + 1) * HD] if h >= DIL else VV[:, k, h * HD:(h + 1) * HD]
                    m = pe.matmul(b[:, h % 8 * HD:(h % 8 + 1) * HD], PT[:, u % 2, k, :], vals,
                                  start=(k == 0), stop=(k == n - 1))
                m.then_inc(s_vm, 1)

            for u in range(len(UNITS) + 2):
                if u < len(UNITS):
                    scores(u)
                if 0 < u <= len(UNITS):
                    turn(u - 1)
                if u >= 2:
                    values(u - 2)
            if gating:
                te.wait_ge(s_gv, 1)
                te.wait_ge(s_msk, 1)
                te.wait_ge(s_sb, len(UNITS))
                te.wait_ge(s_pt, len(UNITS))
                for g in range(N_SG):
                    m = pe.matmul(bank[g // 4][:, g % 4 * P:(g % 4 + 1) * P].rearrange("p (a b) -> p a b", a=TT), SGW[:, g, :],
                                  UG[:, :, SG_W + g * HD:SG_W + (g + 1) * HD], start=True, stop=True)
                    if g % 4 == 3:
                        m.then_inc(s_gm, 1)
            te.wait_ge(s_mix, 1)
            for c in range(CC):
                if c >= 2:
                    te.wait_ge(s_mixt, c - 1)
                for t in range(TT):
                    m = pe.transpose(bank[c % 2][:, t * P:(t + 1) * P], MIX[:, t, c * P:(c + 1) * P], ident)
                m.then_inc(s_mt, 1)
            te.wait_ge(s_mixt, CC)
            te.wait_ge(s_wo, 48)
            for n in range(4):
                for c in range(CC):
                    m = pe.matmul(bank[4 + n][:, :], MIXT[:, c, n // 2 * P:(n // 2 + 1) * P],
                                  WO[:, c, n % 2 * 512:(n % 2 + 1) * 512], start=(c == 0), stop=(c == CC - 1))
                m.then_inc(s_om, 1)

        @block.vector
        def _(ve):
            ch = Count(K.s_dve)
            ch.n = K.dve_n

            def do(ins):
                ch.by(ins, ve)

            if gating:
                GV = UG[:, :, SG_W:]
                ve.wait_ge(s_pj, len(JOBS))
                ve.wait_ge(s_par, 64)
                layer_norm_scales(ve, do, v, GV, GV, SCR, MEAN, SS, SG_W, s_var)
                layer_norm_apply(ve, do, v, GV, GV, RSTD, SGG, SGO, s_root, 1)
                v.memset(MEAN, 0.0).then_inc(s_gv, 1)
                ve.wait_ge(s_gv, 1)
            else:
                ve.wait_ge(s_par, 16)
            for u, (h, t) in enumerate(UNITS):
                n = keys_of(u)
                ve.wait_ge(s_sm, u + 1)
                if u >= 2:
                    ve.wait_ge(s_ex, u - 1)
                if h >= DIL:
                    do(v.tensor_scalar(SB[:, u % 2, 0:n], bank[u % 2][:, 0:n], ATT_SCALE, None, ALU.mult))
                else:
                    do(v.scalar_tensor_tensor(SB[:, u % 2, 0:n], bank[u % 2][:, 0:n], ATT_SCALE,
                                              BIAS[:, h, t * P:t * P + n], ALU.mult, ALU.add))
                v.tensor_reduce(NEGM[:, t, h:h + 1], SB[:, u % 2, 0:n], X_AXIS, ALU.max, negate=True).then_inc(s_sb, 1)
            ve.wait_ge(s_vm, len(UNITS))
            ve.wait_ge(s_ex, len(UNITS))
            for t in range(TT):
                for b in range((HEADS + 7) // 8):
                    hs = slice(b * 8, min(b * 8 + 8, HEADS))
                    do(v.tensor_copy(OALL[:, t, hs, :], bank[4 + 2 * t + b][:, 0:(hs.stop - hs.start) * HD].rearrange(
                        "p (a b) -> p a b", b=HD)))
            do(v.reciprocal(RL, LSUM))
            if not gating:
                def tgj(x):
                    return x.rearrange("p (t g j) -> p t g j", t=TT, g=len(DILS))

                do(v.tensor_copy(lex.rearrange("p (t h) -> p t h", t=TT), NEGM[:, :, 0:DIL]))
                ve.wait_ge(s_ln, 1)
                do(v.tensor_tensor(lse, lse, lex, ALU.subtract))
                top = lmx[:, 0:TT * HPD].rearrange("p (t j) -> p t j", t=TT)
                do(v.tensor_tensor(top, tgj(lse)[:, :, 0, :], tgj(lse)[:, :, 1, :], ALU.max))
                do(v.tensor_tensor(top, top, tgj(lse)[:, :, 2, :], ALU.max))
                full = [P, TT, len(DILS), HPD]
                v.tensor_tensor(tgj(lex), tgj(lse), top.unsqueeze(2).to_broadcast(full), ALU.subtract).then_inc(s_lse, 1)
                ve.wait_ge(s_le, 1)
                tot = lsm[:, 0:TT * HPD].rearrange("p (t j) -> p t j", t=TT)
                do(v.tensor_tensor(tot, tgj(lex)[:, :, 0, :], tgj(lex)[:, :, 1, :], ALU.add))
                do(v.tensor_tensor(tot, tot, tgj(lex)[:, :, 2, :], ALU.add))
                do(v.reciprocal(tot, tot))
                do(v.tensor_tensor(tgj(lex), tgj(lex), tot.unsqueeze(2).to_broadcast(full), ALU.mult))
                do(v.tensor_tensor(RL[:, :, 0:DIL], RL[:, :, 0:DIL], lex.rearrange("p (t h) -> p t h", t=TT), ALU.mult))
            for t in range(TT):
                do(v.tensor_tensor(OALL[:, t, :, :], OALL[:, t, :, :], RL[:, t, :].unsqueeze(2).to_broadcast([P, HEADS, HD]), ALU.mult))
                mem = MIX[:, t, CW - MEM_W:].rearrange("p (h e) -> p h e", h=MEM_H)
                do(v.tensor_copy(mem, OALL[:, t, DIL:, :]))
                if not gating:
                    mix = MIX[:, t, 0:HPD * HD].rearrange("p (h e) -> p h e", h=HPD)
                    do(v.tensor_tensor(mix, OALL[:, t, 0:HPD, :], OALL[:, t, HPD:2 * HPD, :], ALU.add))
                    do(v.tensor_tensor(mix, mix, OALL[:, t, 2 * HPD:3 * HPD, :], ALU.add))
            if gating:
                for g in range(N_SG):
                    if g % 4 == 0:
                        ve.wait_ge(s_gm, g // 4 + 1)
                    cols = slice(g * HD, (g + 1) * HD)
                    do(v.scalar_tensor_tensor(MIX[:, :, cols], bank[g // 4][:, g % 4 * P:(g % 4 + 1) * P].rearrange(
                        "p (a b) -> p a b", a=TT), SGB[:, g:g + 1], UG[:, :, cols], ALU.add, ALU.mult))
            v.memset(MEAN, 0.0).then_inc(s_mix, 1)
            for n in range(4):
                ve.wait_ge(s_om, n + 1)
                o = H[:, n // 2, n % 2 * 512:(n % 2 + 1) * 512]
                do(v.scalar_tensor_tensor(o, o, ALPHA, bank[4 + n][:, :], ALU.mult, ALU.add))
            ve.wait_ge(s_mix, 1)
            ve.wait_ge(s_wo, 48)
            layer_norm_scales(ve, do, v, H, CENT, SCR, MEAN, SS, D, s_var)
            layer_norm_apply(ve, do, v, H, CENT, RSTD, LG, LB, s_root, 2 if gating else 1)
            K.dve_n = ch.n


def attention_stage_0(K):
    attention_stage(K, 0)


def attention_stage_1(K):
    attention_stage(K, 1)


def moe_stage(K, layer):
    nc, cut, bank, d, ident, H = K.nc, K.cut, K.bank, K.dram, K.ident, K.h_res
    v, a, pe = nc.vector, nc.scalar, nc.tensor
    last_layer = layer == 1

    def sem(name):
        return K.sem(f"moe{layer}_{name}")

    C = P // 2
    PAIRS = NE // 2
    PASSES = T // C
    STEPS = (("w_gate", 0), ("w_gate", 1), ("w_up", 0), ("w_up", 1), ("w_down", 0), ("w_down", 1))
    NS = len(STEPS)
    AHEAD = NS // 2

    at = Room(K.cols)
    RING = [[cut(at.take(DC * 512), P, DC, 512) for _ in range(2)] for _ in range(AHEAD)]
    XE = cut(at.take(DC * P), P, DC, P)
    SG = cut(at.take(D), P, D)
    HS = cut(at.take(D), P, D)
    HT = cut(at.take(DC * P), P, DC, P)
    YE = cut(at.take(D), P, D)
    PK = cut(at.take(TT * P), P, TT, P)
    PG = cut(at.take(TT * P), P, TT, P)
    PGT = cut(at.take(T), P, T)
    Y = cut(at.take(TT * D), P, TT, D)
    XT = cut(at.take(DC * T), P, DC, T)
    WR = cut(at.take(DC * NE), P, DC, NE)
    IOTA = cut(at.take(P), P, P)
    TRI = cut(at.take(P), P, P)
    ONES = cut(at.take(P), P, P)
    LG = cut(at.take(D), P, D)
    LB = cut(at.take(D), P, D)
    CENT = cut(at.take(TT * D), P, TT, D)
    BR = cut(at.take(NE), P, NE)
    GRP = cut(at.take(NE), P, NE)
    RK = cut(at.take(TT * PASSES * NE), P, TT, PASSES * NE)
    GT = cut(at.take(TT * PASSES * NE), P, TT, PASSES * NE)
    PRB = cut(at.take(TT * NE), P, TT, NE)
    MSK = cut(at.take(TT * NE), P, TT, NE)
    sm = cut(at.take(300), P, 300)
    SEL, OH, TMPA, TMPB = (sm[:, 16 * n:16 * n + 16] for n in range(4))
    PAIR = sm[:, 64:88].rearrange("p (g k) -> p g k", g=NGRP)
    GS8, M8, E8F, G8 = sm[:, 88:96], sm[:, 96:104], sm[:, 104:112], sm[:, 112:120]
    E8, GI8 = sm[:, 120:128].bitcast(U32), sm[:, 128:136].bitcast(U32)
    NM_, SUMS, RS, CNT, NPF = sm[:, 136:138], sm[:, 138:140], sm[:, 140:142], sm[:, 142:143], sm[:, 143:144]
    MEAN, SS, RSTD = sm[:, 144:146], sm[:, 146:148], sm[:, 148:150]
    NPASS = sm[:, 150:151].bitcast(U32)

    s_w = [[sem(f"w{k}{j}_in") for j in range(2)] for k in range(AHEAD)]
    s_par, s_cst, s_x, s_xt, s_lm, s_lg, s_ex = (sem(n) for n in (
        "params_in", "constants", "x_turned", "xT", "logits_mm", "logit_max", "exp"))
    s_m, s_rk, s_np = sem("routed"), sem("rank_mm"), sem("passes")
    s_pk, s_pg, s_xm, s_xe, s_step, s_sg, s_h = (sem(n) for n in (
        "pack", "pack_gated", "xe_mm", "xe", "step_mm", "silu", "hidden"))
    s_htm, s_ht, s_pgm, s_pgt, s_ye, s_sc, s_acc = (sem(n) for n in (
        "hidden_turned", "hiddenT", "pack_turned", "packT", "ye", "add_back_mm", "added"))
    s_var, s_root, s_fin, s_out = sem("variance"), sem("root"), sem("result"), sem("out")

    def since(eng, s, count):
        if not (isinstance(count, int) and count <= 0):
            eng.wait_ge(s, count)

    def visits(eng, body, prologue=None, epilogue=None):
        def one_pass(q):
            if prologue:
                prologue(q * PAIRS)
            body(q * PAIRS, 0, True, False)
            with eng.Fori(1, PAIRS - 1) as e:
                body(q * PAIRS + e, e, False, False)
            body(q * PAIRS + (PAIRS - 1), PAIRS - 1, False, True)
            if epilogue:
                epilogue(q * PAIRS + (PAIRS - 1))

        one_pass(0)
        eng.wait_ge(s_np, 1)
        passes = eng.value_load(NPASS[0:1, 0:1], min_val=1, max_val=PASSES)
        with eng.If_ne(eng.lower_val(passes - 1), 0):
            with eng.Fori(1, passes) as q:
                one_pass(q)

    with nc.Block() as block:
        @block.sync
        def _(sp):
            sp.dma_start(WR, d["w_router"].rearrange("(c p) n -> p c n", p=P)).then_inc(s_par, 16)
            sp.dma_start(BR, d["b_router"].partition_broadcast(P)).then_inc(s_par, 16)
            sp.dma_start(LG, d["ln2_g"][layer].partition_broadcast(P)).then_inc(s_par, 16)
            sp.dma_start(LB, d["ln2_b"][layer].partition_broadcast(P)).then_inc(s_par, 16)

            def load(n, e, first, last):
                for i, (name, h) in enumerate(STEPS):
                    since(sp, s_step, n * NS + (i - AHEAD + 1))
                    for j in range(2):
                        src = d[name][bass.ds(e * 2 + (layer * NE + j), 1), :, h * 512:(h + 1) * 512]
                        sp.dma_start(RING[i % AHEAD][j], src.rearrange("o (c p) n -> p (o c) n", p=P)).then_inc(
                            s_w[i % AHEAD][j], 16)

            visits(sp, load)
            if last_layer:
                sp.wait_ge(s_fin, TT)
                sp.dma_start(K.out.rearrange("(m p) n -> p m n", p=P), H[:, :, :]).then_inc(s_out, 16)
                sp.wait_ge(s_out, 16)

        @block.gpsimd
        def _(pool):
            K.clear_stale(pool)
            nc.gpsimd.iota(IOTA, pattern=[[1, P]], base=0, channel_multiplier=0,
                           allow_small_or_imprecise_dtypes=True).then_inc(s_cst, 1)
            nc.gpsimd.iota(GRP, pattern=[[1, NGRP], [0, EPG]], base=0, channel_multiplier=0,
                           allow_small_or_imprecise_dtypes=True).then_inc(s_cst, 1)
            nc.gpsimd.memset(ONES, 1.0).then_inc(s_cst, 1)
            pool.wait_ge(s_cst, 3)
            nc.gpsimd.affine_select(out=TRI, in_=ONES, compare_op=ALU.is_gt, fill=0.0, base=0,
                                    pattern=[[1, P]], channel_multiplier=-1).then_inc(s_cst, 1)

        @block.scalar
        def _(act):
            for c in range(DC):
                act.wait_ge(s_x, c + 1)
                a.activation(XT[:, c, :], bank[c % 2][:, 0:T], ACT.Copy).then_inc(s_xt, 1)
            act.wait_ge(s_lg, TT)
            for t in range(TT):
                a.activation(PRB[:, t, :], bank[2][:, t * NE:(t + 1) * NE], ACT.Exp, bias=NM_[:, t:t + 1],
                             accum_out=SUMS[:, t:t + 1]).then_inc(s_ex, 1)

            def packed(m):
                for b in range(2):
                    act.wait_ge(s_xm, m * 2 + (b + 1))
                    a.activation(XE[:, 4 * b:4 * b + 4, :], bank[4 + b][:, :].rearrange("p (a b) -> p a b", a=4),
                                 ACT.Copy).then_inc(s_xe, 1)

            def visit(n, e, first, last):
                since(act, s_h, n * 2)
                for b in range(2):
                    act.wait_ge(s_step, n * NS + (b + 1))
                    a.activation(SG[:, b * 512:(b + 1) * 512], bank[b][:, :], ACT.Silu).then_inc(s_sg, 1)
                if not last:
                    packed(n + 1)
                for b in range(2):
                    act.wait_ge(s_htm, n * 2 + (b + 1))
                    a.activation(HT[:, 4 * b:4 * b + 4, :], bank[6 + b][:, :].rearrange("p (a b) -> p a b", a=4),
                                 ACT.Copy).then_inc(s_ht, 1)
                act.wait_ge(s_pgm, n + 1)
                a.activation(PGT, bank[6][:, 0:T], ACT.Copy).then_inc(s_pgt, 1)
                for b in range(2):
                    act.wait_ge(s_step, n * NS + (b + 5))
                    a.activation(YE[:, b * 512:(b + 1) * 512], bank[4 + b][:, :], ACT.Copy).then_inc(s_ye, 1)

            visits(act, visit, packed)
            act.wait_ge(s_var, 1)
            a.activation(RSTD, SS, ACT.Sqrt).then_inc(s_root, 1)

        @block.tensor
        def _(te):
            for c in range(DC):
                if c >= 2:
                    te.wait_ge(s_xt, c - 1)
                for t in range(TT):
                    m = pe.transpose(bank[c % 2][:, t * P:(t + 1) * P], H[:, t, c * P:(c + 1) * P], ident)
                m.then_inc(s_x, 1)
            te.wait_ge(s_xt, DC)
            te.wait_ge(s_par, 64)
            for t in range(TT):
                for c in range(DC):
                    m = pe.matmul(bank[2][:, t * NE:(t + 1) * NE], XT[:, c, t * P:(t + 1) * P], WR[:, c, :],
                                  start=(c == 0), stop=(c == DC - 1))
            m.then_inc(s_lm, 1)
            te.wait_ge(s_m, TT)
            te.wait_ge(s_cst, 4)
            pe.matmul(bank[3][:, 0:NE], TRI, MSK[:, 0, :], start=True, stop=True)
            pe.matmul(bank[3][:, NE:2 * NE], TRI, MSK[:, 1, :], start=True, stop=False)
            pe.matmul(bank[3][:, NE:2 * NE], ONES, MSK[:, 0, :], start=False, stop=True)
            pe.matmul(bank[3][:, 2 * NE:3 * NE], ONES, MSK[:, 0, :], start=True, stop=False)
            pe.matmul(bank[3][:, 2 * NE:3 * NE], ONES, MSK[:, 1, :], start=False, stop=True).then_inc(s_rk, 1)

            def pack(m, ye_used):
                te.wait_ge(s_pk, m * 4 + 4)
                since(te, s_ye, ye_used)
                for c in range(DC):
                    for t in range(TT):
                        x = pe.matmul(bank[4 + c // 4][:, c % 4 * P:(c % 4 + 1) * P], H[:, t, c * P:(c + 1) * P],
                                      PK[:, t, :], start=(t == 0), stop=(t == TT - 1))
                    if c % 4 == 3:
                        x.then_inc(s_xm, 1)

            def add_back(n):
                for k in range(4):
                    pe.matmul(bank[k][:, :], PGT[:, k // 2 * P:(k // 2 + 1) * P], YE[:, k % 2 * 512:(k % 2 + 1) * 512],
                              start=True, stop=True).then_inc(s_sc, 1)

            def step(n, i, operand, b):
                for j in range(2):
                    te.wait_ge(s_w[i % AHEAD][j], n * 32 + (i // AHEAD * 16 + 16))
                for c in range(DC):
                    for j in range(2):
                        x = pe.matmul(bank[b][j * C:(j + 1) * C, :], operand[:, c, j * C:(j + 1) * C],
                                      RING[i % AHEAD][j][:, c, :], start=(c == 0), stop=(c == DC - 1))
                x.then_inc(s_step, 1)

            def visit(n, e, first, last):
                te.wait_ge(s_xe, n * 2 + 2)
                te.wait_ge(s_acc, n * 4 + (TT if first else TT - 4))
                for i in range(4):
                    step(n, i, XE, i)
                if not last:
                    pack(n + 1, n * 2)
                since(te, s_pgt, n)
                since(te, s_ht, n * 2)
                for b in range(2):
                    te.wait_ge(s_h, n * 2 + (b + 1))
                    for c in range(4):
                        x = pe.transpose(bank[6 + b][:, c * P:(c + 1) * P], HS[:, (4 * b + c) * P:(4 * b + c + 1) * P], ident)
                    x.then_inc(s_htm, 1)
                if not first:
                    te.wait_ge(s_ye, n * 2)
                    add_back(n - 1)
                te.wait_ge(s_pg, n * 4 + 4)
                te.wait_ge(s_ht, n * 2 + 2)
                pe.transpose(bank[6][:, 0:P], PG[:, 0, :], ident)
                pe.transpose(bank[6][:, P:T], PG[:, 1, :], ident).then_inc(s_pgm, 1)
                te.wait_ge(s_xe, n * 2 + (2 if last else 4))
                for h in range(2):
                    step(n, 4 + h, HT, 4 + h)

            def finish(n):
                te.wait_ge(s_ye, n * 2 + 2)
                te.wait_ge(s_pgt, n + 1)
                te.wait_ge(s_acc, n * 4 + TT)
                add_back(n)

            visits(te, visit, lambda m: pack(m, m * 2), finish)

        @block.vector
        def _(ve):
            ch = Count(K.s_dve)
            ch.n = K.dve_n

            def do(ins):
                ch.by(ins, ve)

            ve.wait_ge(s_par, 64)
            ve.wait_ge(s_cst, 4)
            do(v.memset(GS8, -BIG))
            ve.wait_ge(s_lm, 1)
            for t in range(TT):
                v.tensor_reduce(NM_[:, t:t + 1], bank[2][:, t * NE:(t + 1) * NE], X_AXIS, ALU.max, negate=True).then_inc(s_lg, 1)
            for t in range(TT):
                v.tensor_scalar(Y[:, t, :], H[:, t, :], ALPHA, None, ALU.mult).then_inc(s_acc, 1)
            for t in range(TT):
                ve.wait_ge(s_ex, t + 1)
                prob = PRB[:, t, :]
                do(v.reciprocal(RS[:, t:t + 1], SUMS[:, t:t + 1]))
                do(v.tensor_scalar(prob, prob, RS[:, t:t + 1], None, ALU.mult))
                do(v.tensor_tensor(SEL, prob, BR, ALU.add))
                sel = SEL.rearrange("p (g k) -> p g k", g=NGRP)
                do(v.tensor_tensor(PAIR[:, :, 0:3], sel[:, :, 0:3], sel[:, :, 1:4], ALU.add))
                do(v.tensor_tensor(PAIR[:, :, 3:5], sel[:, :, 0:2], sel[:, :, 2:4], ALU.add))
                do(v.tensor_tensor(PAIR[:, :, 5:6], sel[:, :, 0:1], sel[:, :, 3:4], ALU.add))
                do(v.tensor_reduce(GS8[:, 0:NGRP], PAIR, X_AXIS, ALU.max))
                do(v.max(G8, GS8))
                do(v.max_index(GI8, G8, GS8))
                do(v.tensor_copy(TMPA[:, 0:1], GI8[:, 0:1]))
                do(v.tensor_scalar(OH, GRP, TMPA[:, 0:1], None, ALU.is_equal))
                do(v.tensor_tensor(SEL, SEL, OH, ALU.mult))
                do(v.tensor_scalar(OH, OH, 1.0, BIG, ALU.subtract, ALU.mult))
                do(v.tensor_tensor(SEL, SEL, OH, ALU.add))
                do(v.max(M8, SEL))
                do(v.max_index(E8, M8, SEL))
                do(v.tensor_copy(E8F, E8))
                do(v.tensor_scalar(TMPA, IOTA[:, 0:NE], E8F[:, 0:1], None, ALU.is_equal))
                do(v.tensor_scalar(TMPB, IOTA[:, 0:NE], E8F[:, 1:2], None, ALU.is_equal))
                v.tensor_tensor(MSK[:, t, :], TMPA, TMPB, ALU.add).then_inc(s_m, 1)
                ve.wait_ge(s_m, t + 1)
                do(v.tensor_tensor(TMPA, prob, MSK[:, t, :], ALU.mult))
                do(v.tensor_reduce(RS[:, t:t + 1], TMPA, X_AXIS, ALU.add))
                do(v.reciprocal(RS[:, t:t + 1], RS[:, t:t + 1]))
                for q in range(PASSES):
                    do(v.tensor_scalar(GT[:, t, q * NE:(q + 1) * NE], TMPA, RS[:, t:t + 1], None, ALU.mult))
            ve.wait_ge(s_rk, 1)
            for t in range(TT):
                do(v.scalar_tensor_tensor(TMPA, bank[3][:, t * NE:(t + 1) * NE], 1.0, MSK[:, t, :], ALU.add, ALU.mult))
                for q in range(PASSES):
                    do(v.tensor_scalar(RK[:, t, q * NE:(q + 1) * NE], TMPA, 1.0 + q * C, None, ALU.subtract))
            do(v.tensor_reduce(CNT, bank[3][:, 2 * NE:3 * NE], X_AXIS, ALU.max))
            do(v.tensor_scalar(NPF, CNT, C + 0.5, 1.0, ALU.is_gt, ALU.add))
            for q in range(2, PASSES):
                do(v.scalar_tensor_tensor(NPF, CNT, q * C + 0.5, NPF, ALU.is_gt, ALU.add))
            v.tensor_copy(NPASS, NPF).then_inc(s_np, 1)

            def build(m):
                for t in range(TT):
                    for j in range(2):
                        v.tensor_scalar(PK[:, t, j * C:(j + 1) * C], IOTA[:, 0:C], RK[:, t, bass.ds(m * 2 + j, 1)],
                                        None, ALU.is_equal).then_inc(s_pk, 1)

            def prologue(m):
                since(ve, s_xm, m * 2)
                build(m)

            def add(m):
                ve.wait_ge(s_acc, m * 4 + TT)
                for k in range(4):
                    ve.wait_ge(s_sc, m * 4 + (k + 1))
                    o = Y[:, k // 2, k % 2 * 512:(k % 2 + 1) * 512]
                    v.tensor_tensor(o, o, bank[k][:, :], ALU.add).then_inc(s_acc, 1)

            def visit(n, e, first, last):
                since(ve, s_pgm, n)
                for t in range(TT):
                    for j in range(2):
                        v.tensor_scalar(PG[:, t, j * C:(j + 1) * C], IOTA[:, 0:C], RK[:, t, bass.ds(n * 2 + j, 1)],
                                        GT[:, t, bass.ds(n * 2 + j, 1)], ALU.is_equal, ALU.mult).then_inc(s_pg, 1)
                if not last:
                    ve.wait_ge(s_xm, n * 2 + 2)
                    build(n + 1)
                since(ve, s_htm, n * 2)
                for b in range(2):
                    ve.wait_ge(s_step, n * NS + (b + 3))
                    ve.wait_ge(s_sg, n * 2 + (b + 1))
                    cs = slice(b * 512, (b + 1) * 512)
                    v.tensor_tensor(HS[:, cs], SG[:, cs], bank[2 + b][:, :], ALU.mult).then_inc(s_h, 1)
                if not first:
                    add(n - 1)

            visits(ve, visit, prologue, add)
            do(v.memset(MEAN, 0.0))
            layer_norm_scales(ve, do, v, Y, CENT, SG, MEAN, SS, D, s_var)
            layer_norm_apply(ve, do, v, H, CENT, RSTD, LG, LB, s_root, 1)
            if last_layer:
                for t in range(TT):
                    v.tensor_copy(Y[:, t, 0:1], H[:, t, 0:1]).then_inc(s_fin, 1)
            K.dve_n = ch.n


def moe_stage_0(K):
    moe_stage(K, 0)


def moe_stage_1(K):
    moe_stage(K, 1)


STAGES = (mixing_stage, peer_stage, attention_stage_0, moe_stage_0, attention_stage_1, moe_stage_1)


def build(nc, dram, out):
    with ExitStack() as ctx:
        K = Kit()
        K.nc, K.dram, K.out = nc, dram, out
        K.lasting_sem = lambda name: ctx.enter_context(nc.semaphore(name))
        K.bank = [ctx.enter_context(nc.psum_tensor(f"bank{i}", [P, 512], F32)) for i in range(8)]
        K.h_res = ctx.enter_context(nc.sbuf_tensor("h_res", [P, TT, D], F32))
        K.ident = ctx.enter_context(nc.sbuf_tensor("ident", [P, P], F32))[:, :]
        K.cols = 50900
        arena = ctx.enter_context(nc.sbuf_tensor("arena", [P, K.cols], F32))

        def cut(at, p, *shape):
            n = math.prod(shape)
            ap = arena[0:p, at:at + n]
            names = "abcd"[:len(shape)]
            if len(shape) == 1:
                return ap
            return ap.rearrange(f"p ({' '.join(names)}) -> p {' '.join(names)}", **dict(zip(names, shape)))

        def clear_stale(pool):
            for s in K.stale:
                pool.sem_clear(s)

        K.cut, K.clear_stale = cut, clear_stale
        K.s_ident = K.lasting_sem("identity")
        K.s_dve = K.lasting_sem("dve_chain")
        K.dve_n = 0
        K.stale = []
        for stage in STAGES:
            with ExitStack() as of_stage:
                own = []

                def sem(name):
                    own.append(of_stage.enter_context(nc.semaphore(name)))
                    return own[-1]

                K.sem = sem
                stage(K)
                assert not {s.num for s in own} & {s.num for s in K.stale}
            K.stale = own


def dft_constants():
    f32 = np.float32
    t = np.arange(L)[:, None].astype(np.float64)
    f = np.arange(NF)[None, :].astype(np.float64)
    ang = 2 * np.pi / NFFT * ((t * f) % NFFT)
    w = np.where((f == 0) | (f == NF - 1), 1.0, 2.0) / NFFT
    dft = np.stack([np.cos(ang), np.sin(ang)]).astype(f32)
    idft = np.stack([(np.cos(ang) * w).T[:, NM:], (np.sin(ang) * w).T[:, NM:]]).astype(f32)
    ts = np.linspace(0.0, 1.0, L, dtype=f32)[:, None]
    wv = (f32(2.0 * math.pi / L) * np.arange(L, dtype=f32))[:, None]
    n = (HY_EMB - 1) // 2
    bands = np.linspace(1e-4, n - 1, n, dtype=f32)[None, :]
    zT = np.concatenate([ts, np.cos(bands * wv), -np.sin(bands * wv)], axis=-1).T.astype(f32)
    deltas = np.abs(np.linspace(math.log(1e-2) / 0.3, math.log(1e-2) / 1.5, D_HY, dtype=f32))
    decay = np.exp(-ts * deltas).astype(f32)
    back = decay.copy()
    back[0] = 0
    return {"dft": dft, "idft": idft, "zT": np.ascontiguousarray(zT), "decay": np.stack([decay, back])}


def dilation_bias():
    slopes = (2.0 ** (-8.0 * np.arange(1, N_DH + 1, dtype=np.float32) / N_DH)).astype(np.float32)
    rel = np.arange(T)[:, None] - np.arange(T)[None, :]
    full = np.stack([np.where((rel >= 0) & (rel <= w) & (rel % r == 0), -slopes[g * HPD + j] * rel.astype(np.float32), -BIG)
                     for g, (w, r) in enumerate(DILS) for j in range(HPD)]).astype(np.float32)
    return np.concatenate([full[:, 0:P, 0:P], full[:, P:T, :]], 2).transpose(1, 0, 2)


def kernel(**inputs):
    import numpy as _np
    import concourse.bacc as _bacc
    from concourse import mybir as _mybir
    from concourse.bass_utils import run_bass_kernel_spmd as _run

    g = {k: _np.asarray(x) for k, x in inputs.items()}

    def tiles(a, n=P):
        return a.reshape(-1, n).T

    s_hy = 3 * D_HY
    w_in = g["w_in"][0]
    x0, x1, vv = (w_in[:, k * D_HY:(k + 1) * D_HY] for k in range(3))
    rx, rg, mg = w_in[:, s_hy:s_hy + D_RG], w_in[:, s_hy + D_RG:s_hy + 2 * D_RG], w_in[:, s_hy + 2 * D_RG:]

    def hy(a):
        return _np.concatenate([a[..., 2 * D_HY:], a[..., D_HY:2 * D_HY], a[..., :D_HY]], -1)

    cols = _np.concatenate([
        tiles(g["g_mix"]), _np.zeros((P, T_G1), _np.float32), tiles(g["b_gate"]), tiles(hy(g["hy_conv_w"][0])),
        tiles(hy(g["hy_conv_b"])), tiles(g["rg_conv_w"][0]), tiles(g["rg_conv_b"]), tiles(g["rg_gate_b"]),
        tiles(g["rg_lambda"]), tiles(g["hy_skip"])], 1)
    fr = g["hy_freq"][0]
    arrays = {
        "x": g["x"][0], "meta": g["meta"], "cols": cols,
        "w_in": _np.concatenate([rx, vv, x1, x0, rg, mg], 1),
        "hy_w1": g["hy_w1"][0], "hy_w2": g["hy_w2"][0],
        "hy_bf": _np.stack([g["hy_b1"][0], fr[0], g["hy_b2"][0], fr[1]], 1),
        "hy_w3b": _np.concatenate([g["hy_w3"][0], g["hy_b3"]], 0),
        "gate_w": g["rg_gate_w"][0], "rg_out": g["rg_out"][0], "hy_out": g["hy_out"][0], "w_out": g["w_out"][0],
    }
    arrays.update(dft_constants())
    arrays.update({
        "g_ffn": g["g_ffn"][0], "g_final": g["g_final"], "wq": g["peer_wq"][0],
        "keysT": g["peer_keys"][0].transpose(3, 0, 1, 2).reshape(P, 2 * PH, NKEYS),
        "peer_u": g["peer_u"][0], "peer_v": g["peer_v"][0],
    })
    arrays.update({
        "memT": g["mem_2"][0].T, "w_in0": g["w_in_a_2"][0], "w_in1": g["w_in_b_2"][0], "w_out0": g["w_out_a_2"][0],
        "w_out1": g["w_out_b_2"][0], "w_k": g["w_k_shared_2"], "w_v": g["w_v_shared_2"],
        "sg_wT": g["sg_w_2"][0].transpose(2, 0, 1), "sg_bT": g["sg_b_2"][0].T, "sg_ln_g": g["sg_ln_g_2"][0],
        "sg_ln_b": g["sg_ln_b_2"][0], "ln1_g": g["ln1_g_2"], "ln1_b": g["ln1_b_2"], "dil_bias": dilation_bias(),
    })
    for n in range(2):
        arrays[f"w_mem_k{n}"], arrays[f"w_mem_v{n}"] = g["w_mem_k_2"][n], g["w_mem_v_2"][n]
    arrays.update({
        "w_router": g["w_router_2"], "b_router": g["b_router_2"], "ln2_g": g["ln2_g_2"], "ln2_b": g["ln2_b_2"],
        "w_gate": g["w_gate_2"].reshape(2 * NE, D, D), "w_up": g["w_up_2"].reshape(2 * NE, D, D),
        "w_down": g["w_down_2"].reshape(2 * NE, D, D),
    })
    arrays = {"in_" + k: _np.ascontiguousarray(x) for k, x in arrays.items()}
    nc = _bacc.Bacc("TRN2", target_bir_lowering=False, num_devices=1)
    dram = {k[3:]: nc.dram_tensor(k, x.shape, _mybir.dt.from_np(x.dtype), kind="ExternalInput").ap() for k, x in arrays.items()}
    out = nc.dram_tensor("out", (T, D), F32, kind="ExternalOutput").ap()
    build(nc, dram, out)
    r = _run(nc, [arrays], core_ids=[0])
    return r.results[0]["out"].reshape(1, T, D)
```

```python
import math
from contextlib import ExitStack

import numpy as np

import concourse.bass as bass
from concourse import mybir

F32 = mybir.dt.float32
U32 = mybir.dt.uint32
ALU = mybir.AluOpType
ACT = mybir.ActivationFunctionType
X_AXIS = mybir.AxisListType.X

P = 128
D = 1024
DC = D // P
T = 256
TT = T // P
NM = 16
L = T + NM
EPS = 1e-6

D_HY = 512
HT = D_HY // P
HY_EMB = 33
HY_FFN = 64
D_RG = 1024
RH = D_RG // P
RG_CONV = 4
RG_C = 8.0
D_IN = 3 * D_HY + 2 * D_RG + 2 * D
PROJ_TILES = D_IN // P
BLOCKS = PROJ_TILES // 4
T_RX, T_HY, T_RG, T_G1, T_G2 = 0, RH, RH + 3 * HT, 2 * RH + 3 * HT, 3 * RH + 3 * HT

NFFT = 2 * L
NF = NFFT // 2 + 1
FP = NF // 3
TC = ((0, P), (P, P), (2 * P, L - 2 * P))

PH = 8
NKEYS = 128
TOPK = 16
SLOTS = PH * TOPK

SG_W = 768
N_SG = 12
HD = 64
MEM_H = 4
MEM_W = MEM_H * HD
DILS = ((128, 1), (512, 4), (2048, 16))
HPD = 4
N_DH = HPD * len(DILS)
NE = 16
NGRP = 4
EPG = NE // NGRP
ALPHA = 4 ** 0.25
LN_EPS = 1e-5
ATT_SCALE = 1.0 / math.sqrt(HD)
BIG = 1e30

TWO_PI_HI = 6.28125
TWO_PI_LO = 2 * math.pi - TWO_PI_HI
ROUND = 1.5 * 2.0 ** 23
PI_IN = 3.1415925

_widths = (("gmix", DC), ("pbias", PROJ_TILES), ("hyw", 3 * 3 * HT), ("hyb", 3 * HT), ("rgw", 2 * RG_CONV * RH),
           ("rgb", 2 * RH), ("gbias", 4 * RH), ("lam", 2 * RH), ("skip", HT))
COL = {}
NCOLS = 0
for _name, _w in _widths:
    COL[_name] = NCOLS
    NCOLS += _w


class Room:

    def __init__(self, total, at=0):
        self.total, self.at = total, at

    def take(self, n):
        o = self.at
        self.at += n
        assert self.at <= self.total, (self.at, self.total)
        return o


class Count:

    def __init__(self, sem):
        self.sem, self.n = sem, 0

    def by(self, ins, eng=None):
        ins.then_inc(self.sem, 1)
        self.n += 1
        if eng is not None:
            eng.wait_ge(self.sem, self.n)

    def here(self, eng):
        eng.wait_ge(self.sem, self.n)


class Kit:
    pass


def mixing_stage(K):
    nc, cut, bank, sem, d, ident, H = K.nc, K.cut, K.bank, K.sem, K.dram, K.ident, K.h_res
    v, a, pe = nc.vector, nc.scalar, nc.tensor

    at = Room(K.cols)
    nT = at.take(DC * L)
    proj = at.take(PROJ_TILES * L)
    ring = at.take(2 * DC * 512)
    gatew = at.take(4 * RH * P)
    xc = at.take(2 * RH * L)
    rr = at.take(2 * RH * L)
    ii = at.take(RH * L)
    th = at.take(RH * L)
    hc = at.take(3 * HT * L)
    dft = at.take(2 * 3 * NF)
    kspec = at.take(2 * 3 * D_HY)
    tmps = at.take(2 * D_HY)
    colss = at.take(NCOLS)
    small = at.take(290)
    hids = at.take(L)

    NT = cut(nT, P, DC, L)
    PROJ = cut(proj, P, PROJ_TILES, L)
    RING = [cut(ring + k * DC * 512, P, DC, 512) for k in range(2)]
    RGOUT = cut(ring, P, DC, D)
    GATEW = cut(gatew, P, 4 * RH, P)
    HYOUT = cut(gatew, P, HT, D)
    XN = cut(xc, P, 3, D)
    KFB = cut(xc + 3 * D, P, 2, D_HY)
    XC = cut(xc, P, 2 * RH, L)
    WOUT = cut(xc, P, DC, D)
    RR = cut(rr, P, 2 * RH, L)
    KPM = cut(rr, P, 2, 3, D_HY)
    II = cut(ii, P, RH, L)
    YRG = cut(ii, P, DC, T)
    TH = cut(th, P, RH, L)
    MERGED = cut(th, P, DC, T)
    DECAY = cut(ii, P, 2, 3, D_HY)
    HCV = cut(hc, P, 3 * HT, L)
    YHY = cut(hc + HT * L, P, HT, T)
    DFT = cut(dft, P, 2, 3, NF)
    IDFT = cut(nT, P, 2, 3, T)
    KSP = cut(kspec, P, 2, 3, D_HY)
    W3 = cut(tmps, P, 2 * D_HY)
    TMP = cut(tmps, P, 2, D_HY)
    UTOK = cut(proj, P, 3, D_HY)
    YSP = cut(proj + T_HY * L, P, 2, 3, D_HY)
    COLS = cut(colss, P, NCOLS)
    SM = cut(small, P, 290)
    ZT = cut(hids, HY_EMB, L)
    ARG = cut(kspec, HY_FFN, L)
    TURNS = cut(kspec + L, HY_FFN, L)
    HID = cut(hids, P, L)
    W1, W2, HB = SM[0:HY_EMB, 0:64], SM[0:HY_FFN, 64:128], SM[0:HY_FFN, 128:132]
    LT = [SM[:, 140 + 16 * n:156 + 16 * n] for n in range(8)]
    LAMC, NLAMC = LT[6], LT[7]
    SS, RSTD = SM[:, 280:283], SM[:, 284:287]
    ONE = SM[:, 288:289]
    SQ = cut(rr, P, D)

    def col(name, n=0):
        return COLS[:, COL[name] + n:COL[name] + n + 1]

    s_hy = sem("mix_filter_net_in")
    s_inv, s_one = sem("mix_inverse"), sem("mix_one")
    s_dft = K.lasting_sem("mix_dft_in")
    s_x, s_cols, s_idft, s_gw, s_rgo, s_hyo, s_wo = (sem("mix_" + n) for n in (
        "x_in", "cols_in", "idft_in", "gatew_in", "rgout_in", "hyout_in", "wout_in"))
    s_ring = [sem(f"mix_ring{k}_in") for k in range(2)]
    s_sq, s_root, s_nT, s_turn = sem("mix_squares"), sem("mix_root"), sem("mix_nT"), sem("mix_turned")
    s_ms, s_xn = sem("mix_meansq"), sem("mix_xn")
    s_mm, s_ev = sem("mix_proj_mm"), sem("mix_proj")
    s_fmm, s_arg, s_sin, s_kmm, s_kpm = (sem("mix_filter_" + n) for n in ("mm", "arg", "sin", "kmm", "k"))
    s_kfm, s_ksp = sem("mix_kspec_mm"), sem("mix_kspec")
    s_absl, s_el, s_lamc = sem("mix_abs_lambda"), sem("mix_exp_lambda"), sem("mix_decay_rate")
    s_rgc, s_hyc = sem("mix_rg_conv"), sem("mix_hy_conv")
    s_gm, s_ga, s_at, s_m2, s_mu, s_scan = (sem("mix_rg_" + n) for n in (
        "gate_mm", "gates", "a_tanh", "mult_sq", "mult", "scan"))
    s_sg, s_u, s_utm, s_ut = sem("mix_sigmoids"), sem("mix_u"), sem("mix_u_turned"), sem("mix_u_tok")
    s_usm, s_ysp, s_ymm, s_yhy, s_yrg = (sem("mix_" + n) for n in ("uspec_mm", "yspec", "y_mm", "yhy", "yrg"))
    s_hom, s_rom, s_mg, s_wm = sem("mix_hyout_mm"), sem("mix_rgout_mm"), sem("mix_merged"), sem("mix_wout_mm")
    N_DFT = 2 * 4
    N_GATES = 4 * RH

    with nc.Block() as block:
        @block.sync
        def _(sp):
            sp.dma_start(H[:, :, :], d["x"].rearrange("(m p) n -> p m n", p=P)).then_inc(s_x, 16)
            sp.dma_start(XN[0:NM, 2, :], d["meta"]).then_inc(s_x, 16)
            sp.dma_start(COLS, d["cols"]).then_inc(s_cols, 16)
            sp.dma_start(ZT, d["zT"]).then_inc(s_hy, 16)
            sp.dma_start(W1, d["hy_w1"]).then_inc(s_hy, 16)
            sp.dma_start(W2, d["hy_w2"]).then_inc(s_hy, 16)
            sp.dma_start(HB, d["hy_bf"]).then_inc(s_hy, 16)
            sp.dma_start(W3[0:HY_FFN + 1, :], d["hy_w3b"]).then_inc(s_hy, 16)
            w_in = d["w_in"].rearrange("(c p) n -> p c n", p=P)
            for k in range(2):
                sp.dma_start(RING[k], w_in[:, :, k * 512:(k + 1) * 512]).then_inc(s_ring[k], 16)

            def refill(b, k):
                sp.wait_ge(s_mm, b * 4 - 4)
                sp.dma_start(RING[k], w_in[:, :, bass.ds(b * 512, 512)]).then_inc(s_ring[k], 16)

            with sp.Fori(1, BLOCKS // 2) as i:
                for k in range(2):
                    refill(i * 2 + k, k)
            refill(BLOCKS - 1, 0)
            sp.dma_start(GATEW, d["gate_w"].rearrange("a g h i j -> i (a g h) j")).then_inc(s_gw, 16)
            sp.wait_ge(s_mm, PROJ_TILES)
            for k in range(2):
                sp.dma_start(IDFT[0:FP, k, :, :], d["idft"][k].rearrange("(c p) n -> p c n", p=FP)).then_inc(s_idft, 16)
            sp.dma_start(RGOUT, d["rg_out"].rearrange("(c p) n -> p c n", p=P)).then_inc(s_rgo, 16)
            sp.wait_ge(s_gm, N_GATES)
            sp.dma_start(HYOUT, d["hy_out"].rearrange("(c p) n -> p c n", p=P)).then_inc(s_hyo, 16)
            sp.wait_ge(s_yrg, 2)
            sp.dma_start(WOUT, d["w_out"].rearrange("(c p) n -> p c n", p=P)).then_inc(s_wo, 16)

        @block.gpsimd
        def _(pool):
            nc.gpsimd.memset(ident, 0.0).then_inc(K.s_ident, 1)
            pool.wait_ge(K.s_ident, 1)
            nc.gpsimd.affine_select(out=ident, in_=ident, compare_op=ALU.not_equal, fill=1.0, base=0,
                                    pattern=[[-1, P]], channel_multiplier=1).then_inc(K.s_ident, 1)
            for k in range(2):
                for c, (t0, n) in ((0, TC[0]), (2, TC[2])):
                    for dst, src in ((DECAY, "decay"), (DFT, "dft")):
                        if c == 0:
                            pool.dma_start(dst[:, k, 0:2, :], d[src][k, 0:2 * P, :].rearrange(
                                "(c p) n -> p c n", p=P)).then_inc(s_dft, 16)
                        else:
                            pool.dma_start(dst[0:n, k, 2, :], d[src][k, t0:L, :]).then_inc(s_dft, 16)

        @block.scalar
        def _(act):
            act.wait_ge(s_x, 32)
            act.wait_ge(s_ms, 1)
            for m in range(3):
                p = NM if m == 2 else P
                src = XN[0:NM, 2, :] if m == 2 else H[:, m, :]
                a.activation(SQ[0:p, :], src, ACT.Square, accum_out=SS[0:p, m:m + 1]).then_inc(s_sq, 1)
                act.wait_ge(s_sq, m + 1)
            act.wait_ge(s_ms, 2)
            a.activation(RSTD, SS, ACT.Sqrt).then_inc(s_root, 1)
            act.wait_ge(s_absl, 1)
            a.activation(LT[1], LT[0], ACT.Exp).then_inc(s_el, 1)
            act.wait_ge(s_arg, 1)
            a.activation(ARG, ARG, ACT.Sin).then_inc(s_sin, 1)

            def tile_out(i, k):
                act.wait_ge(s_mm, i * 2 + k + 1)
                a.activation(PROJ[:, bass.ds(i * 2 + k, 1), :], bank[k][:, 0:L], ACT.Identity,
                             bias=COLS[:, bass.ds(i * 2 + k + COL["pbias"], 1)]).then_inc(s_ev, 1)

            act.wait_ge(s_cols, 16)
            for n in range(4):
                tile_out(n // 2, n % 2)
            act.wait_ge(s_arg, 2)
            act.wait_ge(s_fmm, 1)
            a.activation(HID[0:HY_FFN, :], ARG, ACT.Sin).then_inc(s_sin, 1)
            for n in range(4, 8):
                tile_out(n // 2, n % 2)
            for n in range(6):
                act.wait_ge(s_kfm, n + 1)
                a.activation(KSP[0:FP, n // 3, n % 3, :], bank[4 + n % 4][0:FP, :], ACT.Copy).then_inc(s_ksp, 1)
            with act.Fori(4, PROJ_TILES // 2) as i:
                for k in range(2):
                    tile_out(i, k)
            act.wait_ge(s_ev, PROJ_TILES)
            act.wait_ge(s_lamc, 1)
            n = 0
            for dr in range(2):
                if dr:
                    act.wait_ge(s_scan, RH)
                for h in range(2 * RH):
                    act.wait_ge(s_gm, n + 1)
                    out = RR[:, dr * RH + h, :] if h < RH else II[:, h - RH, :]
                    a.activation(out, bank[2 + n % 2][:, 0:L], ACT.Sigmoid, bias=col("gbias", n)).then_inc(s_ga, 1)
                    n += 1
                act.wait_ge(s_ga, n)
                for h in range(RH):
                    c = dr * RH + h
                    a.activation(TH[:, h, :], RR[:, c, :], ACT.Tanh, scale=LAMC[:, c:c + 1]).then_inc(s_at, 1)
                act.wait_ge(s_at, dr * 2 * RH + RH)
                act.wait_ge(s_kfm, 6)
                act.wait_ge(s_one, 1)
                other = RR[:, (1 - dr) * RH:(2 - dr) * RH, :]
                a.activation(other, TH, ACT.Ln, bias=ONE).then_inc(s_inv, 1)
                act.wait_ge(s_inv, 2 * dr + 1)
                a.activation(other, other, ACT.Exp, scale=-1.0).then_inc(s_inv, 1)
                for h in range(RH):
                    c = dr * RH + h
                    a.activation(RR[:, c, :], RR[:, c, :], ACT.Exp, scale=NLAMC[:, c:c + 1]).then_inc(s_at, 1)
                act.wait_ge(s_m2, dr + 1)
                a.activation(TH, TH, ACT.Sqrt).then_inc(s_mu, 1)
                if dr == 0:
                    g = PROJ[:, T_G1:T_G1 + 2 * DC, NM:]
                    a.activation(g, g, ACT.Sigmoid).then_inc(s_sg, 1)
                    g = PROJ[:, T_RG:T_RG + RH, NM:]
                    a.activation(g, g, ACT.Gelu_apprx_tanh).then_inc(s_sg, 1)

        @block.tensor
        def _(te):
            def project(i, k, first=False):
                te.wait_ge(s_ring[k], i * 16 + 16)
                for q in range(4):
                    if not (first and q < 2):
                        te.wait_ge(s_ev, i * 8 + k * 4 + q - 1)
                    for c in range(DC):
                        m = pe.matmul(bank[q % 2][:, 0:L], RING[k][:, c, q * P:(q + 1) * P], NT[:, c, :],
                                      start=(c == 0), stop=(c == DC - 1))
                    m.then_inc(s_mm, 1)

            te.wait_ge(s_hy, 16 * 5)
            pe.matmul(bank[6][0:HY_FFN, 0:L], W1, ZT, start=True, stop=True).then_inc(s_fmm, 1)
            te.wait_ge(K.s_ident, 2)
            te.wait_ge(s_xn, 3)
            for c in range(DC):
                if c >= 2:
                    te.wait_ge(s_nT, c - 1)
                cs = slice(c * P, (c + 1) * P)
                pe.transpose(bank[4 + c % 2][:, 0:NM], XN[0:NM, 2, cs], ident[0:NM, 0:NM])
                pe.transpose(bank[4 + c % 2][:, NM:NM + P], XN[:, 0, cs], ident)
                pe.transpose(bank[4 + c % 2][:, NM + P:L], XN[:, 1, cs], ident).then_inc(s_turn, 1)
            te.wait_ge(s_nT, DC)
            project(0, 0, True)
            te.wait_ge(s_sin, 1)
            pe.matmul(bank[7][0:HY_FFN, 0:L], W2, ARG, start=True, stop=True).then_inc(s_fmm, 1)
            te.wait_ge(s_sin, 2)
            te.wait_ge(s_kpm, 1)
            for c, (t0, n) in enumerate(TC):
                if c == 2:
                    project(0, 1)
                    te.wait_ge(s_kpm, 2)
                for k in range(2):
                    pe.matmul(bank[4 + (2 * c + k + 2) % 4][0:n, :], HID[0:HY_FFN + 1, t0:t0 + n],
                              W3[0:HY_FFN + 1, k * D_HY:(k + 1) * D_HY], start=True, stop=True).then_inc(s_kmm, 1)
            te.wait_ge(s_kpm, 4)
            te.wait_ge(s_dft, 16 * N_DFT)
            for n in range(6):
                if n >= 4:
                    te.wait_ge(s_ksp, n - 3)
                k, f = n // 3, n % 3
                for c, (t0, p) in enumerate(TC):
                    m = pe.matmul(bank[4 + n % 4][0:FP, :], DFT[0:p, k, c, f * FP:(f + 1) * FP], KPM[0:p, k, c, :],
                                  start=(c == 0), stop=(c == 2))
                m.then_inc(s_kfm, 1)

            with te.Fori(1, BLOCKS // 2) as i:
                for k in range(2):
                    project(i, k)
            project(BLOCKS // 2, 0)

            def gates(dr):
                for h in range(2 * RH):
                    n = dr * 2 * RH + h
                    if n >= 2:
                        te.wait_ge(s_ga, n - 1)
                    pe.matmul(bank[2 + n % 2][:, 0:L], GATEW[:, n, :], XC[:, dr * RH + h % RH, :],
                              start=True, stop=True).then_inc(s_gm, 1)

            te.wait_ge(s_gw, 16)
            te.wait_ge(s_rgc, 8 * RH)
            gates(0)
            te.wait_ge(s_u, HT)
            te.wait_ge(s_ksp, 6)
            for c, (t0, n) in enumerate(TC):
                for t in range(HT):
                    m = pe.transpose(bank[4 + c][0:n, t * P:(t + 1) * P], HCV[:, t, t0:t0 + n], ident)
                m.then_inc(s_utm, 1)
            te.wait_ge(s_ut, 3)
            for f in range(3):
                if f == 2:
                    te.wait_ge(s_ev, PROJ_TILES)
                for k in range(2):
                    for c, (t0, p) in enumerate(TC):
                        m = pe.matmul(bank[(4 + 2 * f + k) % 8][0:FP, :], DFT[0:p, k, c, f * FP:(f + 1) * FP],
                                      UTOK[0:p, c, :], start=(c == 0), stop=(c == 2))
                m.then_inc(s_usm, 1)
            gates(1)
            te.wait_ge(s_ysp, 3)
            te.wait_ge(s_idft, 32)
            for t in range(HT):
                for n in range(6):
                    m = pe.matmul(bank[4 + t // 2][:, (t % 2) * T:(t % 2 + 1) * T],
                                  YSP[0:FP, n // 3, n % 3, t * P:(t + 1) * P], IDFT[0:FP, n // 3, n % 3, :],
                                  start=(n == 0), stop=(n == 5))
                m.then_inc(s_ymm, 1)
            te.wait_ge(s_yhy, HT)
            te.wait_ge(s_hyo, 16)
            for o in range(DC):
                for c in range(HT):
                    m = pe.matmul(bank[(6 + o // 2) % 8][:, (o % 2) * T:(o % 2 + 1) * T],
                                  HYOUT[:, c, o * P:(o + 1) * P], YHY[:, c, :], start=(c == 0), stop=(c == HT - 1))
            m.then_inc(s_hom, 1)
            te.wait_ge(s_yrg, 2)
            te.wait_ge(s_rgo, 16)
            for o in range(DC):
                for c in range(DC):
                    m = pe.matmul(bank[2 + o // 2][:, (o % 2) * T:(o % 2 + 1) * T],
                                  RGOUT[:, c, o * P:(o + 1) * P], YRG[:, c, :], start=(c == 0), stop=(c == DC - 1))
                if o % 2:
                    m.then_inc(s_rom, 1)
            te.wait_ge(s_mg, 4)
            te.wait_ge(s_wo, 16)
            for n in range(4):
                for c in range(DC):
                    m = pe.matmul(bank[n][:, :], MERGED[:, c, (n // 2) * P:(n // 2 + 1) * P],
                                  WOUT[:, c, (n % 2) * 512:(n % 2 + 1) * 512], start=(c == 0), stop=(c == DC - 1))
                m.then_inc(s_wm, 1)

        @block.vector
        def _(ve):
            ch = Count(K.s_dve)
            ch.n = K.dve_n

            def do(ins):
                ch.by(ins, ve)

            v.memset(SS, 0.0).then_inc(s_ms, 1)
            v.memset(ONE, 1.0).then_inc(s_one, 1)
            ve.wait_ge(s_sq, 3)
            ve.wait_ge(s_ms, 1)
            v.tensor_scalar(SS, SS, 1.0 / D, EPS, ALU.mult, ALU.add).then_inc(s_ms, 1)
            ve.wait_ge(s_root, 1)
            do(v.reciprocal(RSTD, RSTD))
            for m in range(3):
                p = NM if m == 2 else P
                src = XN[0:NM, 2, :] if m == 2 else H[:, m, :]
                v.tensor_scalar(XN[0:p, m, :], src, RSTD[0:p, m:m + 1], None, ALU.mult).then_inc(s_xn, 1)
            ve.wait_ge(s_cols, 16)
            lam = COLS[:, COL["lam"]:COL["lam"] + 2 * RH]
            v.scalar_tensor_tensor(LT[0], lam, -1.0, lam, ALU.mult, ALU.min).then_inc(s_absl, 1)

            def angle(src, b):
                do(v.tensor_scalar(ARG, src, HB[:, b:b + 1], HB[:, b + 1:b + 2], ALU.add, ALU.mult))
                do(v.tensor_scalar(TURNS, ARG, 1.0 / (2 * math.pi), ROUND, ALU.mult, ALU.add))
                do(v.tensor_scalar(TURNS, TURNS, ROUND, None, ALU.subtract))
                do(v.scalar_tensor_tensor(ARG, TURNS, -TWO_PI_HI, ARG, ALU.mult, ALU.add))
                do(v.scalar_tensor_tensor(ARG, TURNS, -TWO_PI_LO, ARG, ALU.mult, ALU.add))
                v.tensor_scalar(ARG, ARG, PI_IN, -PI_IN, ALU.min, ALU.max).then_inc(s_arg, 1)

            ve.wait_ge(s_fmm, 1)
            angle(bank[6][0:HY_FFN, 0:L], 0)
            for c in range(DC):
                ve.wait_ge(s_turn, c + 1)
                v.tensor_scalar(NT[:, c, :], bank[4 + c % 2][:, 0:L], col("gmix", c), None, ALU.mult).then_inc(s_nT, 1)
            ve.wait_ge(s_fmm, 2)
            angle(bank[7][0:HY_FFN, 0:L], 2)
            v.memset(HID[HY_FFN:HY_FFN + 1, :], 1.0).then_inc(s_kpm, 1)
            ve.wait_ge(s_el, 1)
            do(v.tensor_scalar(LT[2], LT[1], 2.0, None, ALU.add))
            do(v.reciprocal(LT[2], LT[2]))
            do(v.tensor_tensor(LT[2], LT[1], LT[2], ALU.mult))
            do(v.tensor_tensor(LT[3], LT[2], LT[2], ALU.mult))
            do(v.tensor_scalar(LT[4], LT[3], 1.0 / 17, None, ALU.mult))
            for n in range(15, 1, -2):
                do(v.scalar_tensor_tensor(LT[4], LT[4], 1.0 / n, LT[3], ALU.add, ALU.mult))
            do(v.scalar_tensor_tensor(LT[4], LT[4], 1.0, LT[2], ALU.add, ALU.mult))
            do(v.tensor_scalar(LT[5], lam, -1.0, 0.0, ALU.mult, ALU.max))
            do(v.scalar_tensor_tensor(LT[5], LT[4], 2.0, LT[5], ALU.mult, ALU.add))
            do(v.tensor_scalar(LAMC, LT[5], RG_C, None, ALU.mult))
            v.tensor_scalar(NLAMC, LT[5], -RG_C, None, ALU.mult).then_inc(s_lamc, 1)
            ve.wait_ge(s_xn, 3)
            ve.wait_ge(s_dft, 16 * N_DFT)
            for c, (t0, n) in enumerate(TC):
                ve.wait_ge(s_kmm, 2 * c + 2)
                for k in range(2):
                    do(v.tensor_tensor(KFB[0:n, k, :], bank[4 + (2 * c + k + 2) % 4][0:n, :], DECAY[0:n, k, c, :], ALU.mult))
                do(v.tensor_tensor(KPM[0:n, 0, c, :], KFB[0:n, 0, :], KFB[0:n, 1, :], ALU.add))
                v.tensor_tensor(KPM[0:n, 1, c, :], KFB[0:n, 0, :], KFB[0:n, 1, :], ALU.subtract).then_inc(s_kpm, 1)
                ve.wait_ge(s_kpm, c + 2)
            ve.wait_ge(s_nT, DC)
            with ve.Fori(0, RH) as h:
                ve.wait_ge(s_ev, h + 1)
                src = PROJ[:, bass.ds(h + T_RX, 1), :]

                def out(dr, lo, hi):
                    return XC[:, bass.ds(h + dr * RH, 1), lo:hi]

                def weight(dr, j):
                    return COLS[:, bass.ds(h + COL["rgw"] + (dr * RG_CONV + j) * RH, 1)]

                for j in range(RG_CONV):
                    if j:
                        ve.wait_ge(s_rgc, h * 8 + 2 * j)
                    if j == 0:
                        for dr in range(2):
                            v.tensor_scalar(out(dr, 0, L), src, weight(dr, 0),
                                            COLS[:, bass.ds(h + COL["rgb"] + dr * RH, 1)], ALU.mult, ALU.add).then_inc(s_rgc, 1)
                    else:
                        v.scalar_tensor_tensor(out(0, j, L), PROJ[:, bass.ds(h + T_RX, 1), 0:L - j], weight(0, j),
                                               out(0, j, L), ALU.mult, ALU.add).then_inc(s_rgc, 1)
                        v.scalar_tensor_tensor(out(1, 0, L - j), PROJ[:, bass.ds(h + T_RX, 1), j:L], weight(1, j),
                                               out(1, 0, L - j), ALU.mult, ALU.add).then_inc(s_rgc, 1)
            with ve.Fori(0, 3 * HT) as t:
                ve.wait_ge(s_ev, t + T_HY + 1)

                def tile(lo, hi):
                    return PROJ[:, bass.ds(t + T_HY, 1), lo:hi]

                def conv(lo, hi):
                    return HCV[:, bass.ds(t, 1), lo:hi]

                def tap(j):
                    return COLS[:, bass.ds(t + COL["hyw"] + j * 3 * HT, 1)]

                v.tensor_scalar(conv(0, L), tile(0, L), tap(1), COLS[:, bass.ds(t + COL["hyb"], 1)],
                                ALU.mult, ALU.add).then_inc(s_hyc, 1)
                ve.wait_ge(s_hyc, t * 3 + 1)
                v.scalar_tensor_tensor(conv(1, L), tile(0, L - 1), tap(0), conv(1, L), ALU.mult, ALU.add).then_inc(s_hyc, 1)
                ve.wait_ge(s_hyc, t * 3 + 2)
                v.scalar_tensor_tensor(conv(0, L - 1), tile(1, L), tap(2), conv(0, L - 1), ALU.mult, ALU.add).then_inc(s_hyc, 1)
            ve.wait_ge(s_hyc, 9 * HT)
            for t in range(HT):
                v.tensor_tensor(HCV[:, t, :], HCV[:, t, :], HCV[:, HT + t, :], ALU.mult).then_inc(s_u, 1)
            for c, (t0, n) in enumerate(TC):
                ve.wait_ge(s_utm, c + 1)
                ve.wait_ge(s_rgc, 8 * RH)
                v.tensor_copy(UTOK[0:n, c, :], bank[4 + c][0:n, :]).then_inc(s_ut, 1)

            def rg_input(dr):
                ve.wait_ge(s_inv, 2 * dr + 2)
                inverse = RR[:, (1 - dr) * RH:(2 - dr) * RH, :]
                v.scalar_tensor_tensor(TH, TH, 2.0, inverse, ALU.mult, ALU.mult).then_inc(s_m2, 1)

            def rg_scan(dr):
                ve.wait_ge(s_mu, dr + 1)
                first = 0 if dr == 0 else L - 1
                do(v.memset(TH[:, :, first:first + 1], 1.0))
                do(v.tensor_tensor(II, II, TH, ALU.mult))
                XD = XC[:, dr * RH:(dr + 1) * RH, :]
                do(v.tensor_tensor(II, II, XD, ALU.mult))
                ve.wait_ge(s_at, 2 * RH * (dr + 1))
                ve.wait_ge(s_gm, 2 * RH * (dr + 1))
                for h in range(RH):
                    o, x, y = XC[:, dr * RH + h, :], RR[:, dr * RH + h, :], II[:, h, :]
                    if dr:
                        o, x, y = o[:, ::-1], x[:, ::-1], y[:, ::-1]
                    v.tensor_tensor_scan(o, x, y, 0.0, ALU.mult, ALU.add).then_inc(s_scan, 1)

            rg_input(0)
            rg_scan(0)
            for f in range(3):
                ve.wait_ge(s_usm, f + 1)
                ve.wait_ge(s_hyc, 9 * HT)
                ve.wait_ge(s_ksp, 6)
                uc, us = (bank[(4 + 2 * f + k) % 8][0:FP, :] for k in range(2))
                t0, t1 = TMP[0:FP, 0, :], TMP[0:FP, 1, :]
                kc, ks = KSP[0:FP, 0, f, :], KSP[0:FP, 1, f, :]
                do(v.tensor_tensor(t0, uc, kc, ALU.mult))
                do(v.tensor_tensor(t1, us, ks, ALU.mult))
                do(v.tensor_tensor(YSP[0:FP, 0, f, :], t0, t1, ALU.subtract))
                do(v.tensor_tensor(t0, uc, ks, ALU.mult))
                do(v.tensor_tensor(t1, us, kc, ALU.mult))
                v.tensor_tensor(YSP[0:FP, 1, f, :], t0, t1, ALU.add).then_inc(s_ysp, 1)
                ve.wait_ge(s_ysp, f + 1)
            for t in range(HT):
                ve.wait_ge(s_ymm, t // 2 * 2 + 2)
                if t == 0:
                    ve.wait_ge(s_u, HT)
                do(v.scalar_tensor_tensor(YHY[:, t, :], HCV[:, t, NM:], col("skip", t),
                                          bank[4 + t // 2][:, (t % 2) * T:(t % 2 + 1) * T], ALU.mult, ALU.add))
                v.tensor_tensor(YHY[:, t, :], YHY[:, t, :], HCV[:, 2 * HT + t, NM:], ALU.mult).then_inc(s_yhy, 1)
            rg_input(1)
            rg_scan(1)
            ve.wait_ge(s_scan, 2 * RH)
            v.tensor_tensor(YRG, XC[:, 0:RH, NM:], XC[:, RH:, NM:], ALU.add).then_inc(s_yrg, 1)
            ve.wait_ge(s_yrg, 1)
            ve.wait_ge(s_sg, 2)
            v.tensor_tensor(YRG, YRG, PROJ[:, T_RG:T_RG + RH, NM:], ALU.mult).then_inc(s_yrg, 1)
            ve.wait_ge(s_hom, 1)
            for n in range(4):
                ve.wait_ge(s_rom, n + 1)
                g1 = PROJ[:, T_G1 + 2 * n:T_G1 + 2 * n + 2, NM:]
                g2 = PROJ[:, T_G2 + 2 * n:T_G2 + 2 * n + 2, NM:]
                hy = bank[(6 + n) % 8][:, :].rearrange("p (a b) -> p a b", a=2)
                rg = bank[2 + n][:, :].rearrange("p (a b) -> p a b", a=2)
                t0 = TMP[:, 0, :].rearrange("p (a b) -> p a b", a=2)
                t1 = TMP[:, 1, :].rearrange("p (a b) -> p a b", a=2)
                do(v.tensor_tensor(t0, hy, g1, ALU.mult))
                do(v.tensor_tensor(t1, rg, g2, ALU.mult))
                v.tensor_tensor(MERGED[:, 2 * n:2 * n + 2, :], t0, t1, ALU.add).then_inc(s_mg, 1)
                ve.wait_ge(s_mg, n + 1)
            for n in range(4):
                ve.wait_ge(s_wm, n + 1)
                o = H[:, n // 2, (n % 2) * 512:(n % 2 + 1) * 512]
                do(v.tensor_tensor(o, o, bank[n][:, :], ALU.add))
            K.dve_n = ch.n


def peer_stage(K):
    nc, cut, bank, sem, d, ident, H = K.nc, K.cut, K.bank, K.sem, K.dram, K.ident, K.h_res
    v, a, pe = nc.vector, nc.scalar, nc.tensor
    R = TOPK
    UNITS = TT * PH
    HP = 2 * PH
    GROUPS = TT * HP // 4

    at = Room(K.cols)
    ROWU = cut(at.take(R * D), P, R, D)
    wqo = at.take(DC * HP * P)
    WQ = cut(wqo, P, 4, DC, 4 * P)
    ROWV = cut(wqo, P, R, D)
    qto = at.take(HP * T)
    QT = cut(qto, P, TT, HP, P)
    DIAG = cut(qto, P, R, P)
    KEYS = cut(at.take(HP * NKEYS), P, HP, NKEYS)
    xto = at.take(DC * T)
    XT = cut(xto, P, DC, T)
    GL = cut(xto, P, D)
    XF = cut(at.take(TT * D), P, TT, D)
    so = at.take(UNITS * 2 * NKEYS)
    S = cut(so, P, UNITS * 2 * NKEYS)
    GF, PROD = cut(so, P, D), cut(so + D, P, D)
    SCR = cut(at.take(D), P, D)
    CAND = cut(at.take(TOPK * TOPK), P, TOPK * TOPK)
    EQ = cut(at.take(TOPK * TOPK), P, TOPK, TOPK)
    SU = cut(at.take(2 * NKEYS), P, 2, NKEYS)
    TS = cut(at.take(2 * TOPK), P, 2, TOPK)
    TI = cut(at.take(2 * TOPK), P, 2, TOPK).bitcast(U32)
    TIF = cut(at.take(2 * TOPK), P, 2, TOPK)
    CS = cut(at.take(TOPK), P, TOPK)
    CI = cut(at.take(TOPK), P, TOPK).bitcast(U32)
    CJ = cut(at.take(TOPK), P, TOPK).bitcast(U32)
    CF = cut(at.take(TOPK), P, TOPK)
    E12 = cut(at.take(2 * TOPK), P, 2, TOPK)
    CHOSEN = cut(at.take(TOPK), P, TOPK).bitcast(U32)
    EXPS = cut(at.take(TOPK), P, TOPK)
    DOTS = cut(at.take(TOPK), P, TOPK)
    GELU = cut(at.take(TOPK), P, TOPK)
    IDX = cut(at.take(UNITS * TOPK), P, UNITS * TOPK).bitcast(U32)
    GATE = cut(at.take(UNITS * TOPK), P, UNITS * TOPK)
    WGT = cut(at.take(UNITS * TOPK), P, UNITS * TOPK)
    ICOL = {n: cut(at.take(TOPK), P, TOPK).bitcast(U32) for n in "uv"}
    IOTA = cut(at.take(TOPK), P, TOPK)
    SM = cut(at.take(8), P, 8)
    SS, RSTD, SUM, RSUM, HELD = SM[:, 0:2], SM[:, 2:4], SM[:, 4:5], SM[:, 5:6], SM[:, 6:7]
    ROWS = {"u": ROWU, "v": ROWV}

    s_gf, s_gl, s_keys = sem("peer_gain_in"), sem("peer_final_gain_in"), sem("peer_keys_in")
    s_wq = [sem(f"peer_wq{k}_in") for k in range(4)]
    s_iota = sem("peer_iota")
    s_sq, s_ms, s_root, s_xf, s_tr, s_xt = (sem("peer_" + n) for n in ("squares", "meansq", "root", "xn", "turned", "xT"))
    s_qm, s_q, s_sm, s_s = sem("peer_q_mm"), sem("peer_qT"), sem("peer_score_mm"), sem("peer_scores")
    s_cs, s_ex, s_idx, s_icol = sem("peer_chosen"), sem("peer_exp"), sem("peer_indices"), sem("peer_index_cols")
    s_row = {n: [K.lasting_sem(f"peer_{n}{k}_in") for k in range(R)] for n in "uv"}
    s_dot, s_gel, s_wgt, s_diag, s_pv = (sem("peer_" + n) for n in ("dots", "gelu", "weights", "diag", "rows_summed"))
    s_h, s_route = sem("peer_h"), sem("peer_route_step")

    with nc.Block() as block:
        @block.sync
        def _(sp):
            wq = d["wq"].rearrange("(c p) n -> p c n", p=P)
            sp.dma_start(GF, d["g_ffn"].partition_broadcast(P)).then_inc(s_gf, 16)
            for k in range(4):
                sp.dma_start(WQ[:, k, :, :], wq[:, :, k * 4 * P:(k + 1) * 4 * P]).then_inc(s_wq[k], 16)
                if k == 0:
                    sp.dma_start(KEYS, d["keysT"]).then_inc(s_keys, 16)
            sp.wait_ge(s_qm, GROUPS)
            sp.dma_start(GL, d["g_final"].partition_broadcast(P)).then_inc(s_gl, 16)

        @block.gpsimd
        def _(pool):
            K.clear_stale(pool)
            nc.gpsimd.iota(IOTA, pattern=[[1, TOPK]], base=0, channel_multiplier=0,
                           allow_small_or_imprecise_dtypes=True).then_inc(s_iota, 1)
            pool.wait_ge(s_iota, 1)

            def gather(n, table, unit, free=lambda k: None, column=None):
                cols = ICOL[column or table]
                nc.gpsimd.tensor_copy(cols, IDX[:, bass.ds(unit * R, R)]).then_inc(s_icol, 1)
                pool.wait_ge(s_icol, n * 2 + 1)
                nc.gpsimd.tensor_tensor(HELD, IOTA[:, 0:1], IOTA[:, 0:1], ALU.add).then_inc(s_icol, 1)
                for k in range(R):
                    free(k)
                    nc.gpsimd.indirect_dma_start(ROWS[table][:, k, :], None, d["peer_" + table],
                                                 bass.IndirectOffsetOnAxis(cols[:, k:k + 1], 0)).then_inc(s_row[table][k], 16)

            pool.wait_ge(s_idx, 1)
            gather(0, "u", 0)
            pool.wait_ge(s_idx, 2)
            pool.wait_ge(s_dot, R)
            gather(1, "u", 1)
            gather(2, "v", 0, lambda k: pool.wait_ge(s_qm, GROUPS - 3 + k // 4))
            pool.wait_ge(s_idx, 3)
            pool.wait_ge(s_dot, 2 * R)
            gather(3, "u", 2)
            with pool.Fori(1, UNITS - 2) as i:
                pool.wait_ge(s_pv, i * R)
                gather(i * 2 + 2, "v", i)
                pool.wait_ge(s_idx, i + 3)
                pool.wait_ge(s_dot, i * R + 2 * R)
                gather(i * 2 + 3, "u", i + 2)
            pool.wait_ge(s_pv, (UNITS - 2) * R)
            gather(UNITS * 2 - 2, "v", UNITS - 2)
            pool.wait_ge(s_dot, UNITS * R)
            gather(UNITS * 2 - 1, "v", UNITS - 1, lambda k: pool.wait_ge(s_pv, (UNITS - 2) * R + (k + 1)), "u")

        @block.scalar
        def _(act):
            act.wait_ge(s_ms, 1)
            for t in range(TT):
                a.activation(PROD, H[:, t, :], ACT.Square, accum_out=SS[:, t:t + 1]).then_inc(s_sq, 1)
                act.wait_ge(s_sq, t + 1)
            act.wait_ge(s_ms, 2)
            a.activation(RSTD, SS, ACT.Sqrt).then_inc(s_root, 1)
            for c in range(DC):
                act.wait_ge(s_tr, c + 1)
                a.activation(XT[:, c, :], bank[c % 2][:, 0:T], ACT.Copy).then_inc(s_xt, 1)

            def leave_banks(g):
                t, k = g // 4, g % 4
                act.wait_ge(s_qm, g + 1)
                a.activation(QT[:, t, 4 * k:4 * k + 4, :], bank[2 + g % 2][:, :].rearrange("p (a b) -> p a b", a=4),
                             ACT.Copy).then_inc(s_q, 1)
                act.wait_ge(s_sm, g + 1)
                a.activation(S[:, g * 512:(g + 1) * 512], bank[4 + g % 2][:, :], ACT.Copy).then_inc(s_s, 1)

            def exps(unit):
                act.wait_ge(s_cs, unit + 1)
                a.activation(EXPS, EXPS, ACT.Exp).then_inc(s_ex, 1)

            def gelu(unit):
                act.wait_ge(s_dot, unit * R + R)
                a.activation(GELU, DOTS, ACT.Gelu_apprx_tanh).then_inc(s_gel, 1)

            def diagonals(unit, first=False):
                act.wait_ge(s_wgt, unit + 1)
                for k in range(R):
                    if not first:
                        act.wait_ge(s_pv, unit * R + (k + 1 - R))
                    a.activation(DIAG[:, k, :], ident, ACT.Copy, scale=WGT[:, bass.ds(unit * R + k, 1)]).then_inc(s_diag, 1)

            leave_banks(0)
            leave_banks(1)
            exps(0)
            leave_banks(2)
            exps(1)
            for g in range(3, GROUPS):
                leave_banks(g)
            gelu(0)
            exps(2)
            diagonals(0, True)
            with act.Fori(1, UNITS - 2) as i:
                gelu(i)
                exps(i + 2)
                diagonals(i)
            for i in (UNITS - 2, UNITS - 1):
                gelu(i)
                diagonals(i)
            act.wait_ge(s_h, 1)
            for t in range(TT):
                a.activation(PROD, H[:, t, :], ACT.Square, accum_out=SS[:, t:t + 1]).then_inc(s_sq, 1)
                act.wait_ge(s_sq, TT + t + 1)
            act.wait_ge(s_ms, 3)
            a.activation(RSTD, SS, ACT.Sqrt).then_inc(s_root, 1)

        @block.tensor
        def _(te):
            te.wait_ge(s_xf, TT)
            for c in range(DC):
                if c >= 2:
                    te.wait_ge(s_xt, c - 1)
                for t in range(TT):
                    m = pe.transpose(bank[c % 2][:, t * P:(t + 1) * P], XF[:, t, c * P:(c + 1) * P], ident)
                m.then_inc(s_tr, 1)
            te.wait_ge(s_xt, DC)
            for g in range(GROUPS):
                t, k = g // 4, g % 4
                te.wait_ge(s_wq[k], 16)
                if g >= 2:
                    te.wait_ge(s_q, g - 1)
                for j in range(4):
                    for c in range(DC):
                        m = pe.matmul(bank[2 + g % 2][:, j * P:(j + 1) * P], WQ[:, k, c, j * P:(j + 1) * P],
                                      XT[:, c, t * P:(t + 1) * P], start=(c == 0), stop=(c == DC - 1))
                m.then_inc(s_qm, 1)
                te.wait_ge(s_keys, 16)
                te.wait_ge(s_q, g + 1)
                if g >= 2:
                    te.wait_ge(s_s, g - 1)
                for j in range(4):
                    m = pe.matmul(bank[4 + g % 2][:, j * P:(j + 1) * P], QT[:, t, 4 * k + j, :], KEYS[:, 4 * k + j, :],
                                  start=True, stop=True)
                m.then_inc(s_sm, 1)

            def add_rows(unit, t, first, last):
                for k in range(R):
                    te.wait_ge(s_row["v"][k], unit * 16 + 16)
                    te.wait_ge(s_diag, unit * R + (k + 1))
                    for n in range(2):
                        m = pe.matmul(bank[(6 if t else 0) + n][:, :], DIAG[:, k, :], ROWV[:, k, n * 512:(n + 1) * 512],
                                      start=(first and k == 0), stop=(last and k == R - 1))
                    m.then_inc(s_pv, 1)

            for t in range(TT):
                add_rows(t * PH, t, True, False)
                with te.Fori(t * PH + 1, (t + 1) * PH - 1) as i:
                    add_rows(i, t, False, False)
                add_rows((t + 1) * PH - 1, t, False, True)

        @block.vector
        def _(ve):
            ch = Count(K.s_dve)
            ch.n = K.dve_n
            v.memset(SS, 0.0).then_inc(s_ms, 1)
            ve.wait_ge(s_sq, TT)
            ve.wait_ge(s_ms, 1)
            v.tensor_scalar(SS, SS, 1.0 / D, EPS, ALU.mult, ALU.add).then_inc(s_ms, 1)
            ve.wait_ge(s_root, 1)
            ch.by(v.reciprocal(RSTD, RSTD), ve)
            ve.wait_ge(s_gf, 16)
            for t in range(TT):
                v.scalar_tensor_tensor(XF[:, t, :], H[:, t, :], RSTD[:, t:t + 1], GF, ALU.mult, ALU.mult).then_inc(s_xf, 1)
            ve.wait_ge(s_iota, 1)

            def route(unit):
                ve.sem_clear(s_route)
                steps = Count(s_route)

                def do(ins):
                    steps.by(ins, ve)

                def top16(val, idx, src, spare):
                    do(v.max(val[:, 0:8], src))
                    do(v.match_replace(spare, val[:, 0:8], src, -BIG))
                    do(v.max_index(idx[:, 0:8], val[:, 0:8], src))
                    do(v.max(val[:, 8:16], spare))
                    do(v.max_index(idx[:, 8:16], val[:, 8:16], spare))

                mine = bass.ds(unit * TOPK, TOPK)
                square = [P, TOPK, TOPK]
                do(v.tensor_copy(SU.rearrange("p a b -> p (a b)"), S[:, bass.ds(unit * (2 * NKEYS), 2 * NKEYS)]))
                for half in range(2):
                    top16(TS[:, half, :], TI[:, half, :], SU[:, half, :], SCR[:, 0:NKEYS])
                do(v.tensor_copy(TIF, TI))
                do(v.tensor_tensor(CAND.rearrange("p (i j) -> p i j", i=TOPK), TS[:, 0, :].unsqueeze(2).to_broadcast(square),
                                   TS[:, 1, :].unsqueeze(1).to_broadcast(square), ALU.add))
                top16(CS, CI, CAND, SCR[:, 0:TOPK * TOPK])
                v.tensor_scalar(EXPS, CS, CS[:, 0:1], None, ALU.subtract).then_inc(s_cs, 1)
                for half in range(2):
                    op = (ALU.logical_shift_right, 4) if half == 0 else (ALU.bitwise_and, 15)
                    do(v.tensor_scalar(CJ, CI, op[1], None, op[0]))
                    do(v.tensor_copy(CF, CJ))
                    do(v.tensor_tensor(EQ, CF.unsqueeze(2).to_broadcast(square), IOTA.unsqueeze(1).to_broadcast(square), ALU.is_equal))
                    do(v.tensor_tensor(EQ, EQ, TIF[:, half, :].unsqueeze(1).to_broadcast(square), ALU.mult))
                    do(v.tensor_reduce(E12[:, half, :], EQ, X_AXIS, ALU.add))
                do(v.scalar_tensor_tensor(CHOSEN, E12[:, 0, :], float(NKEYS), E12[:, 1, :], ALU.mult, ALU.add))
                v.tensor_copy(IDX[:, mine], CHOSEN).then_inc(s_idx, 1)
                ve.wait_ge(s_ex, unit + 1)
                do(v.tensor_reduce(SUM, EXPS, X_AXIS, ALU.add))
                do(v.reciprocal(RSUM, SUM))
                do(v.tensor_scalar(GATE[:, mine], EXPS, RSUM, None, ALU.mult))
                ve.wait_ge(s_idx, unit + 1)

            def dots(unit, t):
                for k in range(R):
                    ve.wait_ge(s_row["u"][k], unit * 16 + 16)
                    v.tensor_tensor_reduce(SCR, ROWU[:, k, :], XF[:, t, :], 1.0, 0.0, ALU.mult, ALU.add,
                                           DOTS[:, k:k + 1]).then_inc(s_dot, 1)
                    ve.wait_ge(s_dot, unit * R + (k + 1))

            def weigh(unit):
                mine = bass.ds(unit * TOPK, TOPK)
                ve.wait_ge(s_gel, unit + 1)
                v.tensor_tensor(WGT[:, mine], GELU, GATE[:, mine], ALU.mult).then_inc(s_wgt, 1)

            ve.wait_ge(s_s, 1)
            route(0)
            route(1)
            for t in range(TT):
                with ve.Fori(t * PH, (t + 1) * PH if t < TT - 1 else UNITS - 2) as i:
                    dots(i, t)
                    weigh(i)
                    ve.wait_ge(s_s, GROUPS)
                    route(i + 2)
            for i in (UNITS - 2, UNITS - 1):
                dots(i, TT - 1)
                weigh(i)
            for t in range(TT):
                ve.wait_ge(s_pv, (t + 1) * SLOTS)
                for n in range(2):
                    o = H[:, t, n * 512:(n + 1) * 512]
                    ch.by(v.tensor_tensor(o, o, bank[(6 if t else 0) + n][:, :], ALU.add), ve)
            v.memset(SS, 0.0).then_inc(s_h, 1)
            ve.wait_ge(s_sq, 2 * TT)
            v.tensor_scalar(SS, SS, 1.0 / D, EPS, ALU.mult, ALU.add).then_inc(s_ms, 1)
            ve.wait_ge(s_root, 2)
            ch.by(v.reciprocal(RSTD, RSTD), ve)
            ve.wait_ge(s_gl, 16)
            for t in range(TT):
                ch.by(v.scalar_tensor_tensor(H[:, t, :], H[:, t, :], RSTD[:, t:t + 1], GL, ALU.mult, ALU.mult), ve)
            K.dve_n = ch.n


class LayerNorm:

    def __init__(self, sem, mean, ss, rstd, scratch):
        self.mean, self.ss, self.rstd, self.scratch = mean, ss, rstd, scratch
        self.s_mean, self.s_sq, self.s_var, self.s_root = (sem(n) for n in ("mean", "squares", "variance", "root"))

    def vector(self, ve, do, v, dst, src, cent, width, g, b, n=1):
        do(v.memset(self.ss, 0.0))
        for t in range(TT):
            do(v.tensor_reduce(self.mean[:, t:t + 1], src[:, t, :], X_AXIS, ALU.add))
        v.tensor_scalar(self.mean, self.mean, -1.0 / width, None, ALU.mult).then_inc(self.s_mean, 1)
        ve.wait_ge(self.s_mean, n)
        for t in range(TT):
            do(v.scalar_tensor_tensor(cent[:, t, :], src[:, t, :], self.mean[:, t:t + 1], g, ALU.add, ALU.mult))
        ve.wait_ge(self.s_sq, n * TT)
        v.tensor_scalar(self.ss, self.ss, 1.0 / width, LN_EPS, ALU.mult, ALU.add).then_inc(self.s_var, 1)
        ve.wait_ge(self.s_root, n)
        do(v.reciprocal(self.rstd, self.rstd))
        for t in range(TT):
            do(v.scalar_tensor_tensor(dst[:, t, :], cent[:, t, :], self.rstd[:, t:t + 1], b, ALU.mult, ALU.add))

    def scalar(self, act, a, src, width, n=1):
        act.wait_ge(self.s_mean, n)
        for t in range(TT):
            a.activation(self.scratch[:, 0:width], src[:, t, :], ACT.Square, bias=self.mean[:, t:t + 1],
                         accum_out=self.ss[:, t:t + 1]).then_inc(self.s_sq, 1)
            act.wait_ge(self.s_sq, (n - 1) * TT + t + 1)
        act.wait_ge(self.s_var, n)
        a.activation(self.rstd, self.ss, ACT.Sqrt).then_inc(self.s_root, 1)


def attention_stage(K, layer):
    nc, cut, bank, d, ident, H = K.nc, K.cut, K.bank, K.dram, K.ident, K.h_res
    v, a, pe = nc.vector, nc.scalar, nc.tensor
    gating = layer == 0

    def sem(name):
        return K.sem(f"att{layer}_{name}")

    HEADS = MEM_H if gating else N_DH + MEM_H
    DIL = HEADS - MEM_H
    UNITS = [(h, t) for t in range(TT) for h in range(HEADS)]
    CW = SG_W + MEM_W if gating else HPD * HD + MEM_W
    CC = CW // P
    QTILES = 2 if gating else (DIL + MEM_H) * HD // P

    at = Room(K.cols)
    XT = cut(at.take(DC * T), P, DC, T)
    MEMT = cut(at.take(DC * T), P, DC, T)
    wmk = at.take(DC * MEM_W)
    WMK = cut(wmk, P, DC, MEM_W)
    WMV = cut(at.take(DC * MEM_W), P, DC, MEM_W)
    MKT = cut(at.take(2 * T), P, 2, T)
    MV = cut(at.take(2 * MEM_W), P, 2, MEM_W)
    QT = cut(at.take(QTILES * T), P, QTILES, T)
    SB = cut(at.take(2 * T), P, 2, T)
    PB = cut(at.take(2 * T), P, 2, T)
    PT = cut(at.take(2 * T), P, 2, 2, P)
    OALL = cut(at.take(TT * HEADS * HD), P, TT, HEADS, HD)
    MIX = cut(at.take(TT * CW), P, TT, CW)
    MIXT = cut(at.take(CC * T), P, CC, T)
    WO = cut(at.take(CC * D) if gating else wmk, P, CC, D)
    LG = cut(at.take(D), P, D)
    LB = cut(at.take(D), P, D)
    SCR = cut(at.take(D), P, D)
    stats = cut(at.take(400), P, 400)
    NEGM, LSUM, RL = (stats[:, 64 * n:64 * n + TT * HEADS].rearrange("p (t h) -> p t h", t=TT) for n in range(3))
    MEAN, SS, RSTD = stats[:, 200:202], stats[:, 202:204], stats[:, 204:206]
    SGB = stats[:, 210:210 + N_SG]
    lse, lmx, lex, lsm = (stats[:, 224 + 24 * n:248 + 24 * n] for n in range(4))
    if gating:
        CENTG = MIX.rearrange("p t c -> p (t c)")[:, 0:TT * SG_W].rearrange("p (t c) -> p t c", t=TT)
        UG = cut(at.take(TT * 2 * SG_W), P, TT, 2 * SG_W)
        SGW = cut(at.take(N_SG * P), P, N_SG, P)
        SGG = cut(at.take(SG_W), P, SG_W)
        SGO = cut(at.take(SG_W), P, SG_W)
        q_at = 2 * SG_W
        assert at.at <= K.cols - MOE_EARLY * 2 * DC * 512
        WIN = cut(at.take(DC * (2 * SG_W + MEM_W)), P, DC, 2 * SG_W + MEM_W)
    else:
        KT = cut(at.take(DIL * HD // P * T), P, DIL * HD // P, T)
        VV = cut(at.take(TT * DIL * HD), P, TT, DIL * HD)
        BIAS = cut(at.take(DIL * (P + T)), P, DIL, P + T)
        q_at = 0
        assert at.at <= K.cols - MOE_EARLY * 2 * DC * 512
        WIN = cut(at.take(DC * (DIL * HD + MEM_W)), P, DC, DIL * HD + MEM_W)
        WK = cut(at.take(DC * DIL * HD), P, DC, DIL * HD)
        WV = cut(at.take(DC * DIL * HD), P, DC, DIL * HD)
    CENT = cut(0, P, TT, D)
    norm = LayerNorm(sem, MEAN, SS, RSTD, SCR)
    K.s_moe_w = [[K.lasting_sem(f"moe{layer}_w{i}{j}_in") for j in range(2)] for i in range(MOE_EARLY)]

    s_mem, s_kv, s_wo, s_par = (sem(n) for n in ("mem_in", "kv_in", "wout_in", "params_in"))
    WIN_PARTS = (0, 512, 1024, 1536, 2 * SG_W + MEM_W) if gating else (0, 512, 1024)
    s_win = [sem(f"win{n}_in") for n in range(len(WIN_PARTS) - 1)]
    s_xt, s_x, s_mk, s_mko = sem("x_turned"), sem("xT"), sem("mem_kv_mm"), sem("mem_kv")
    s_pm, s_pj = sem("proj_mm"), sem("proj")
    s_sm, s_sb, s_ex, s_tm, s_pt, s_vm, s_o = (sem(n) for n in (
        "score_mm", "score_max", "exp", "p_turned", "pT", "pv_mm", "heads"))
    s_msk, s_gv, s_gm, s_mix = sem("masked"), sem("gv"), sem("gate_mm"), sem("mix")
    s_lse, s_ln, s_le = sem("sums"), sem("log_sum"), sem("lse_exp")
    s_mt, s_mixt, s_om = sem("mix_turned"), sem("mixT"), sem("out_mm")
    JOBS = [("q", n) for n in range(QTILES)]
    if gating:
        JOBS += [("ug", n) for n in range(3 * TT)]
    else:
        JOBS += [("k", n) for n in range(DIL * HD // P)] + [("v", n) for n in range(2 * TT)]
    if gating:
        JOBS = [("ug", t * 3 + n) for n in range(3) for t in range(TT)] + JOBS[:QTILES]
    BEFORE_MEM = 3 * TT if gating else len(JOBS)

    def keys_of(u):
        h, t = UNITS[u]
        return P * (t + 1) if h < DIL else T

    with nc.Block() as block:
        @block.sync
        def _(sp):
            def rows(name):
                return d[name].rearrange("(c p) n -> p c n", p=P)

            for n, (lo, hi) in enumerate(zip(WIN_PARTS, WIN_PARTS[1:])):
                sp.dma_start(WIN[:, :, lo:hi], rows(f"w_in{layer}")[:, :, lo:hi]).then_inc(s_win[n], 16)
            if not gating:
                sp.dma_start(WK, rows("w_k")).then_inc(s_kv, 16)
                sp.dma_start(WV, rows("w_v")).then_inc(s_kv, 16)
            sp.dma_start(MEMT, rows("memT")).then_inc(s_mem, 16)
            sp.dma_start(WMK, rows(f"w_mem_k{layer}")).then_inc(s_mem, 16)
            sp.dma_start(WMV, rows(f"w_mem_v{layer}")).then_inc(s_mem, 16)
            if not gating:
                sp.dma_start(BIAS, d["dil_bias"]).then_inc(s_par, 16)
            else:
                sp.dma_start(SGW, d["sg_wT"]).then_inc(s_par, 16)
                sp.dma_start(SGB, d["sg_bT"]).then_inc(s_par, 16)
                sp.dma_start(SGG, d["sg_ln_g"].partition_broadcast(P)).then_inc(s_par, 16)
                sp.dma_start(SGO, d["sg_ln_b"].partition_broadcast(P)).then_inc(s_par, 16)
            sp.dma_start(LG, d["ln1_g"][layer].partition_broadcast(P)).then_inc(s_wo, 16)
            sp.dma_start(LB, d["ln1_b"][layer].partition_broadcast(P)).then_inc(s_wo, 16)
            if not gating:
                sp.wait_ge(s_mk, 4)
            sp.dma_start(WO, rows(f"w_out{layer}")).then_inc(s_wo, 16)
            sp.wait_ge(s_pm, len(JOBS))
            for i in range(MOE_EARLY):
                for j in range(2):
                    moe_load(K, sp, layer, i, j, 0).then_inc(K.s_moe_w[i][j], 16)

        @block.gpsimd
        def _(pool):
            K.clear_stale(pool)
            if gating:
                pool.wait_ge(s_par, 64)
                nc.gpsimd.affine_select(out=SGW, in_=SGW, compare_op=ALU.is_ge, fill=0.0, base=0,
                                        pattern=[[0, N_SG], [1, P]], channel_multiplier=-1).then_inc(s_msk, 1)

        @block.scalar
        def _(act):
            for c in range(DC):
                act.wait_ge(s_xt, c + 1)
                a.activation(XT[:, c, :], bank[c % 2][:, 0:T], ACT.Copy).then_inc(s_x, 1)

            def leave_banks(n):
                kind, i = JOBS[n]
                act.wait_ge(s_pm, n + 1)
                b = bank[2 + n % 2]
                if kind == "q":
                    m = a.activation(QT[:, i, :], b[:, 0:T], ACT.Copy)
                elif kind == "k":
                    m = a.activation(KT[:, i, :], b[:, 0:T], ACT.Copy)
                elif kind == "v":
                    w = DIL * HD // 2
                    m = a.activation(VV[:, i // 2, i % 2 * w:(i % 2 + 1) * w], b[:, 0:w], ACT.Copy)
                else:
                    m = a.activation(UG[:, i // 3, i % 3 * 512:(i % 3 + 1) * 512], b[:, :], ACT.Gelu)
                m.then_inc(s_pj, 1)

            for n in range(BEFORE_MEM):
                leave_banks(n)
            for n in range(4):
                act.wait_ge(s_mk, n + 1)
                dst = MKT[:, n, :] if n < 2 else MV[:, n - 2, :]
                a.activation(dst, bank[4 + n][:, 0:T], ACT.Copy).then_inc(s_mko, 1)
            if gating:
                norm.scalar(act, a, UG[:, :, SG_W:], SG_W)
            for n in range(BEFORE_MEM, len(JOBS)):
                leave_banks(n)

            def turned(u):
                act.wait_ge(s_tm, u + 1)
                if u >= 2:
                    act.wait_ge(s_vm, u - 1)
                n = keys_of(u) // P
                a.activation(PT[:, u % 2, 0:n, :], bank[2 + u % 2][:, 0:n * P].rearrange(
                    "p (a b) -> p a b", a=n), ACT.Copy).then_inc(s_pt, 1)

            for u, (h, t) in enumerate(UNITS):
                n = keys_of(u)
                act.wait_ge(s_sb, u + 1)
                if u >= 2:
                    act.wait_ge(s_tm, u - 1)
                a.activation(PB[:, u % 2, 0:n], SB[:, u % 2, 0:n], ACT.Exp, bias=NEGM[:, t, h:h + 1],
                             accum_out=LSUM[:, t, h:h + 1]).then_inc(s_ex, 1)
                if u:
                    turned(u - 1)
            turned(len(UNITS) - 1)
            if not gating:
                act.wait_ge(s_ex, len(UNITS))
                a.activation(lse.rearrange("p (t h) -> p t h", t=TT), LSUM[:, :, 0:DIL], ACT.Ln).then_inc(s_ln, 1)
                act.wait_ge(s_lse, 1)
                a.activation(lex, lex, ACT.Exp).then_inc(s_le, 1)
            act.wait_ge(s_mt, 1)
            for c in range(CC):
                act.wait_ge(s_mt, c + 1)
                a.activation(MIXT[:, c, :], bank[c % 2][:, 0:T], ACT.Copy).then_inc(s_mixt, 1)
            norm.scalar(act, a, H, D, 2 if gating else 1)

        @block.tensor
        def _(te):
            for c in range(DC):
                if c >= 2:
                    te.wait_ge(s_x, c - 1)
                for t in range(TT):
                    m = pe.transpose(bank[c % 2][:, t * P:(t + 1) * P], H[:, t, c * P:(c + 1) * P], ident)
                m.then_inc(s_xt, 1)
            te.wait_ge(s_x, DC)

            def memory():
                te.wait_ge(s_mem, 48)
                for n in range(4):
                    for c in range(DC):
                        if n < 2:
                            m = pe.matmul(bank[4 + n][:, 0:T], WMK[:, c, n * P:(n + 1) * P], MEMT[:, c, :],
                                          start=(c == 0), stop=(c == DC - 1))
                        else:
                            m = pe.matmul(bank[4 + n][:, 0:MEM_W], MEMT[:, c, (n - 2) * P:(n - 1) * P], WMV[:, c, :],
                                          start=(c == 0), stop=(c == DC - 1))
                    m.then_inc(s_mk, 1)

            for n, (kind, i) in enumerate(JOBS):
                if n == BEFORE_MEM:
                    memory()
                if kind in ("ug", "q"):
                    te.wait_ge(s_win[i % 3 if kind == "ug" else (q_at + i * P) // 512], 16)
                if n >= 2:
                    te.wait_ge(s_pj, n - 1)
                if kind in "kv":
                    te.wait_ge(s_kv, 32)
                b = bank[2 + n % 2]
                for c in range(DC):
                    if kind in "qk":
                        w = WIN[:, c, q_at + i * P:q_at + (i + 1) * P] if kind == "q" else WK[:, c, i * P:(i + 1) * P]
                        m = pe.matmul(b[:, 0:T], w, XT[:, c, :], start=(c == 0), stop=(c == DC - 1))
                    elif kind == "v":
                        w = DIL * HD // 2
                        m = pe.matmul(b[:, 0:w], XT[:, c, i // 2 * P:(i // 2 + 1) * P], WV[:, c, i % 2 * w:(i % 2 + 1) * w],
                                      start=(c == 0), stop=(c == DC - 1))
                    else:
                        m = pe.matmul(b[:, :], XT[:, c, i // 3 * P:(i // 3 + 1) * P], WIN[:, c, i % 3 * 512:(i % 3 + 1) * 512],
                                      start=(c == 0), stop=(c == DC - 1))
                m.then_inc(s_pm, 1)
            if BEFORE_MEM == len(JOBS):
                memory()
            te.wait_ge(s_pj, len(JOBS))
            te.wait_ge(s_mko, 4)

            def scores(u):
                h, t = UNITS[u]
                r = slice(h % 2 * HD, (h % 2 + 1) * HD)
                if u >= 2:
                    te.wait_ge(s_sb, u - 1)
                keys = MKT[r, (h - DIL) // 2, :] if h >= DIL else KT[r, h // 2, 0:keys_of(u)]
                pe.matmul(bank[u % 2][:, 0:keys_of(u)], QT[r, h // 2, t * P:(t + 1) * P], keys,
                          start=True, stop=True).then_inc(s_sm, 1)

            def turn(u):
                te.wait_ge(s_ex, u + 1)
                if u >= 2:
                    te.wait_ge(s_pt, u - 1)
                for n in range(keys_of(u) // P):
                    m = pe.transpose(bank[2 + u % 2][:, n * P:(n + 1) * P], PB[:, u % 2, n * P:(n + 1) * P], ident)
                m.then_inc(s_tm, 1)

            def values(u):
                h, t = UNITS[u]
                te.wait_ge(s_pt, u + 1)
                n = keys_of(u) // P
                b = bank[4 + 2 * t + h // 8]
                for k in range(n):
                    vals = MV[:, k, (h - DIL) * HD:(h - DIL + 1) * HD] if h >= DIL else VV[:, k, h * HD:(h + 1) * HD]
                    m = pe.matmul(b[:, h % 8 * HD:(h % 8 + 1) * HD], PT[:, u % 2, k, :], vals,
                                  start=(k == 0), stop=(k == n - 1))
                m.then_inc(s_vm, 1)

            for u in range(len(UNITS) + 2):
                if u < len(UNITS):
                    scores(u)
                if 0 < u <= len(UNITS):
                    turn(u - 1)
                if u >= 2:
                    values(u - 2)
            if gating:
                te.wait_ge(s_gv, 1)
                te.wait_ge(s_msk, 1)
                te.wait_ge(s_sb, len(UNITS))
                te.wait_ge(s_pt, len(UNITS))
                for g in range(N_SG):
                    m = pe.matmul(bank[g // 4][:, g % 4 * P:(g % 4 + 1) * P].rearrange("p (a b) -> p a b", a=TT), SGW[:, g, :],
                                  UG[:, :, SG_W + g * HD:SG_W + (g + 1) * HD], start=True, stop=True)
                    if g % 4 == 3:
                        m.then_inc(s_gm, 1)
            te.wait_ge(s_mix, 1)
            for c in range(CC):
                if c >= 2:
                    te.wait_ge(s_mixt, c - 1)
                for t in range(TT):
                    m = pe.transpose(bank[c % 2][:, t * P:(t + 1) * P], MIX[:, t, c * P:(c + 1) * P], ident)
                m.then_inc(s_mt, 1)
            te.wait_ge(s_mixt, CC)
            te.wait_ge(s_wo, 48)
            for n in range(4):
                for c in range(CC):
                    m = pe.matmul(bank[4 + n][:, :], MIXT[:, c, n // 2 * P:(n // 2 + 1) * P],
                                  WO[:, c, n % 2 * 512:(n % 2 + 1) * 512], start=(c == 0), stop=(c == CC - 1))
                m.then_inc(s_om, 1)

        @block.vector
        def _(ve):
            ch = Count(K.s_dve)
            ch.n = K.dve_n

            def do(ins):
                ch.by(ins, ve)

            if gating:
                GV = UG[:, :, SG_W:]
                ve.wait_ge(s_pj, BEFORE_MEM)
                ve.wait_ge(s_par, 64)
                norm.vector(ve, do, v, GV, GV, CENTG, SG_W, SGG, SGO)
                v.memset(MEAN, 0.0).then_inc(s_gv, 1)
                ve.wait_ge(s_gv, 1)
            else:
                ve.wait_ge(s_par, 16)
            for u, (h, t) in enumerate(UNITS):
                n = keys_of(u)
                ve.wait_ge(s_sm, u + 1)
                if u >= 2:
                    ve.wait_ge(s_ex, u - 1)
                if h >= DIL:
                    do(v.tensor_scalar(SB[:, u % 2, 0:n], bank[u % 2][:, 0:n], ATT_SCALE, None, ALU.mult))
                else:
                    do(v.scalar_tensor_tensor(SB[:, u % 2, 0:n], bank[u % 2][:, 0:n], ATT_SCALE,
                                              BIAS[:, h, t * P:t * P + n], ALU.mult, ALU.add))
                v.tensor_reduce(NEGM[:, t, h:h + 1], SB[:, u % 2, 0:n], X_AXIS, ALU.max, negate=True).then_inc(s_sb, 1)
            ve.wait_ge(s_vm, len(UNITS))
            ve.wait_ge(s_ex, len(UNITS))
            for t in range(TT):
                for b in range((HEADS + 7) // 8):
                    hs = slice(b * 8, min(b * 8 + 8, HEADS))
                    do(v.tensor_copy(OALL[:, t, hs, :], bank[4 + 2 * t + b][:, 0:(hs.stop - hs.start) * HD].rearrange(
                        "p (a b) -> p a b", b=HD)))
            do(v.reciprocal(RL, LSUM))
            if not gating:
                def tgj(x):
                    return x.rearrange("p (t g j) -> p t g j", t=TT, g=len(DILS))

                do(v.tensor_copy(lex.rearrange("p (t h) -> p t h", t=TT), NEGM[:, :, 0:DIL]))
                ve.wait_ge(s_ln, 1)
                do(v.tensor_tensor(lse, lse, lex, ALU.subtract))
                top = lmx[:, 0:TT * HPD].rearrange("p (t j) -> p t j", t=TT)
                do(v.tensor_tensor(top, tgj(lse)[:, :, 0, :], tgj(lse)[:, :, 1, :], ALU.max))
                do(v.tensor_tensor(top, top, tgj(lse)[:, :, 2, :], ALU.max))
                full = [P, TT, len(DILS), HPD]
                v.tensor_tensor(tgj(lex), tgj(lse), top.unsqueeze(2).to_broadcast(full), ALU.subtract).then_inc(s_lse, 1)
                ve.wait_ge(s_le, 1)
                tot = lsm[:, 0:TT * HPD].rearrange("p (t j) -> p t j", t=TT)
                do(v.tensor_tensor(tot, tgj(lex)[:, :, 0, :], tgj(lex)[:, :, 1, :], ALU.add))
                do(v.tensor_tensor(tot, tot, tgj(lex)[:, :, 2, :], ALU.add))
                do(v.reciprocal(tot, tot))
                do(v.tensor_tensor(tgj(lex), tgj(lex), tot.unsqueeze(2).to_broadcast(full), ALU.mult))
                do(v.tensor_tensor(RL[:, :, 0:DIL], RL[:, :, 0:DIL], lex.rearrange("p (t h) -> p t h", t=TT), ALU.mult))
            for t in range(TT):
                do(v.tensor_tensor(OALL[:, t, :, :], OALL[:, t, :, :], RL[:, t, :].unsqueeze(2).to_broadcast([P, HEADS, HD]), ALU.mult))
                mem = MIX[:, t, CW - MEM_W:].rearrange("p (h e) -> p h e", h=MEM_H)
                do(v.tensor_copy(mem, OALL[:, t, DIL:, :]))
                if not gating:
                    mix = MIX[:, t, 0:HPD * HD].rearrange("p (h e) -> p h e", h=HPD)
                    do(v.tensor_tensor(mix, OALL[:, t, 0:HPD, :], OALL[:, t, HPD:2 * HPD, :], ALU.add))
                    do(v.tensor_tensor(mix, mix, OALL[:, t, 2 * HPD:3 * HPD, :], ALU.add))
            if gating:
                for g in range(N_SG):
                    if g % 4 == 0:
                        ve.wait_ge(s_gm, g // 4 + 1)
                    cols = slice(g * HD, (g + 1) * HD)
                    do(v.scalar_tensor_tensor(MIX[:, :, cols], bank[g // 4][:, g % 4 * P:(g % 4 + 1) * P].rearrange(
                        "p (a b) -> p a b", a=TT), SGB[:, g:g + 1], UG[:, :, cols], ALU.add, ALU.mult))
            v.memset(MEAN, 0.0).then_inc(s_mix, 1)
            for n in range(4):
                ve.wait_ge(s_om, n + 1)
                o = H[:, n // 2, n % 2 * 512:(n % 2 + 1) * 512]
                do(v.scalar_tensor_tensor(o, o, ALPHA, bank[4 + n][:, :], ALU.mult, ALU.add))
            ve.wait_ge(s_mix, 1)
            ve.wait_ge(s_wo, 48)
            norm.vector(ve, do, v, H, H, CENT, D, LG, LB, 2 if gating else 1)
            K.dve_n = ch.n


def attention_stage_0(K):
    attention_stage(K, 0)


def attention_stage_1(K):
    attention_stage(K, 1)


MOE_STEPS = (("w_gate", 0), ("w_gate", 1), ("w_up", 0), ("w_up", 1), ("w_down", 0), ("w_down", 1))
MOE_EARLY = 2


def moe_slot(K, i, j):
    return K.cut(K.cols - (2 * i + j + 1) * DC * 512, P, DC, 512)


def moe_load(K, sp, layer, i, j, pair):
    name, h = MOE_STEPS[i]
    src = K.dram[name][bass.ds(pair * 2 + (layer * NE + j), 1), :, h * 512:(h + 1) * 512]
    return sp.dma_start(moe_slot(K, i % (len(MOE_STEPS) // 2), j), src.rearrange("o (c p) n -> p (o c) n", p=P))


def moe_stage(K, layer):
    nc, cut, bank, d, ident, H = K.nc, K.cut, K.bank, K.dram, K.ident, K.h_res
    v, a, pe = nc.vector, nc.scalar, nc.tensor
    last_layer = layer == 1

    def sem(name):
        return K.sem(f"moe{layer}_{name}")

    C = P // 2
    PAIRS = NE // 2
    PASSES = T // C
    STEPS = MOE_STEPS
    NS = len(STEPS)
    AHEAD = NS // 2

    at = Room(K.cols - 2 * AHEAD * DC * 512)
    RING = [[moe_slot(K, i, j) for j in range(2)] for i in range(AHEAD)]
    XE = cut(at.take(DC * P), P, DC, P)
    SG = cut(at.take(D), P, D)
    HS = cut(at.take(D), P, D)
    HT = cut(at.take(DC * P), P, DC, P)
    YE = cut(at.take(D), P, D)
    PK = cut(at.take(TT * P), P, TT, P)
    PG = cut(at.take(TT * P), P, TT, P)
    PGT = cut(at.take(T), P, T)
    Y = cut(at.take(TT * D), P, TT, D)
    XT = cut(at.take(DC * T), P, DC, T)
    WR = cut(at.take(DC * NE), P, DC, NE)
    IOTA = cut(at.take(P), P, P)
    TRI = cut(at.take(P), P, P)
    ONES = cut(at.take(P), P, P)
    LG = cut(at.take(D), P, D)
    LB = cut(at.take(D), P, D)
    CENT = cut(at.take(TT * D), P, TT, D)
    BR = cut(at.take(NE), P, NE)
    GRP = cut(at.take(NE), P, NE)
    RK = cut(at.take(TT * PASSES * NE), P, TT, PASSES * NE)
    GT = cut(at.take(TT * PASSES * NE), P, TT, PASSES * NE)
    PRB = cut(at.take(TT * NE), P, TT, NE)
    MSK = cut(at.take(TT * NE), P, TT, NE)
    sm = cut(at.take(320), P, 320)
    SEL, OH, TMPA, TMPB = (sm[:, 32 * n:32 * n + 32].rearrange("p (t e) -> p t e", t=TT) for n in range(4))
    PAIR = sm[:, 128:176].rearrange("p (g k) -> p g k", k=6)
    GS8, M8, E8F, G8, E8, GI8 = (sm[:, 176 + 16 * n:192 + 16 * n].rearrange("p (t k) -> p t k", t=TT) for n in range(6))
    E8, GI8 = E8.bitcast(U32), GI8.bitcast(U32)
    NM_, SUMS, RS, GRPF, MEAN, SS, RSTD = (sm[:, 272 + 2 * n:274 + 2 * n] for n in range(7))
    CNT, NPF, NPASS = sm[:, 286:287], sm[:, 287:288], sm[:, 288:289].bitcast(U32)

    s_w = K.s_moe_w + [[sem(f"w{k}{j}_in") for j in range(2)] for k in range(MOE_EARLY, AHEAD)]
    s_par, s_cst, s_x, s_xt, s_lm, s_lg, s_ex = (sem(n) for n in (
        "params_in", "constants", "x_turned", "xT", "logits_mm", "logit_max", "exp"))
    s_m, s_rk, s_np = sem("routed"), sem("rank_mm"), sem("passes")
    s_pk, s_pg, s_xm, s_xe, s_step, s_sg, s_h = (sem(n) for n in (
        "pack", "pack_gated", "xe_mm", "xe", "step_mm", "silu", "hidden"))
    s_htm, s_ht, s_pgm, s_pgt, s_ye, s_sc, s_acc = (sem(n) for n in (
        "hidden_turned", "hiddenT", "pack_turned", "packT", "ye", "add_back_mm", "added"))
    s_fin, s_out = sem("result"), sem("out")
    norm = LayerNorm(sem, MEAN, SS, RSTD, SG)

    def since(eng, s, count):
        if not (isinstance(count, int) and count <= 0):
            eng.wait_ge(s, count)

    def visits(eng, body, prologue=None, epilogue=None):
        def one_pass(q):
            if prologue:
                prologue(q * PAIRS)
            body(q * PAIRS, 0, True, False)
            with eng.Fori(1, PAIRS - 1) as e:
                body(q * PAIRS + e, e, False, False)
            body(q * PAIRS + (PAIRS - 1), PAIRS - 1, False, True)
            if epilogue:
                epilogue(q * PAIRS + (PAIRS - 1))

        one_pass(0)
        eng.wait_ge(s_np, 1)
        passes = eng.value_load(NPASS[0:1, 0:1], min_val=1, max_val=PASSES)
        with eng.If_ne(eng.lower_val(passes - 1), 0):
            with eng.Fori(1, passes) as q:
                one_pass(q)

    with nc.Block() as block:
        @block.sync
        def _(sp):
            sp.dma_start(WR, d["w_router"].rearrange("(c p) n -> p c n", p=P)).then_inc(s_par, 16)
            sp.dma_start(BR, d["b_router"].partition_broadcast(P)).then_inc(s_par, 16)
            sp.dma_start(LG, d["ln2_g"][layer].partition_broadcast(P)).then_inc(s_par, 16)
            sp.dma_start(LB, d["ln2_b"][layer].partition_broadcast(P)).then_inc(s_par, 16)

            def load(n, e, first, last):
                for i in range(MOE_EARLY if isinstance(n, int) and n == 0 else 0, NS):
                    since(sp, s_step, n * NS + (i - AHEAD + 1))
                    for j in range(2):
                        moe_load(K, sp, layer, i, j, e).then_inc(s_w[i % AHEAD][j], 16)

            visits(sp, load)
            if last_layer:
                sp.wait_ge(s_fin, TT)
                sp.dma_start(K.out.rearrange("(m p) n -> p m n", p=P), H[:, :, :]).then_inc(s_out, 16)
                sp.wait_ge(s_out, 16)

        @block.gpsimd
        def _(pool):
            K.clear_stale(pool)
            nc.gpsimd.iota(IOTA, pattern=[[1, P]], base=0, channel_multiplier=0,
                           allow_small_or_imprecise_dtypes=True).then_inc(s_cst, 1)
            nc.gpsimd.iota(GRP, pattern=[[1, NGRP], [0, EPG]], base=0, channel_multiplier=0,
                           allow_small_or_imprecise_dtypes=True).then_inc(s_cst, 1)
            nc.gpsimd.memset(ONES, 1.0).then_inc(s_cst, 1)
            pool.wait_ge(s_cst, 3)
            nc.gpsimd.affine_select(out=TRI, in_=ONES, compare_op=ALU.is_gt, fill=0.0, base=0,
                                    pattern=[[1, P]], channel_multiplier=-1).then_inc(s_cst, 1)

        @block.scalar
        def _(act):
            for c in range(DC):
                act.wait_ge(s_x, c + 1)
                a.activation(XT[:, c, :], bank[c % 2][:, 0:T], ACT.Copy).then_inc(s_xt, 1)
            act.wait_ge(s_lg, TT)
            for t in range(TT):
                a.activation(PRB[:, t, :], bank[2][:, t * NE:(t + 1) * NE], ACT.Exp, bias=NM_[:, t:t + 1],
                             accum_out=SUMS[:, t:t + 1]).then_inc(s_ex, 1)

            def packed(m):
                for b in range(2):
                    act.wait_ge(s_xm, m * 2 + (b + 1))
                    a.activation(XE[:, 4 * b:4 * b + 4, :], bank[4 + b][:, :].rearrange("p (a b) -> p a b", a=4),
                                 ACT.Copy).then_inc(s_xe, 1)

            def visit(n, e, first, last):
                since(act, s_h, n * 2)
                for b in range(2):
                    act.wait_ge(s_step, n * NS + (b + 1))
                    a.activation(SG[:, b * 512:(b + 1) * 512], bank[b][:, :], ACT.Silu).then_inc(s_sg, 1)
                if not last:
                    packed(n + 1)
                for b in range(2):
                    act.wait_ge(s_htm, n * 2 + (b + 1))
                    a.activation(HT[:, 4 * b:4 * b + 4, :], bank[6 + b][:, :].rearrange("p (a b) -> p a b", a=4),
                                 ACT.Copy).then_inc(s_ht, 1)
                act.wait_ge(s_pgm, n + 1)
                a.activation(PGT, bank[6][:, 0:T], ACT.Copy).then_inc(s_pgt, 1)
                for b in range(2):
                    act.wait_ge(s_step, n * NS + (b + 5))
                    a.activation(YE[:, b * 512:(b + 1) * 512], bank[4 + b][:, :], ACT.Copy).then_inc(s_ye, 1)

            visits(act, visit, packed)
            norm.scalar(act, a, Y, D)

        @block.tensor
        def _(te):
            for c in range(DC):
                if c >= 2:
                    te.wait_ge(s_xt, c - 1)
                for t in range(TT):
                    m = pe.transpose(bank[c % 2][:, t * P:(t + 1) * P], H[:, t, c * P:(c + 1) * P], ident)
                m.then_inc(s_x, 1)
            te.wait_ge(s_xt, DC)
            te.wait_ge(s_par, 64)
            for t in range(TT):
                for c in range(DC):
                    m = pe.matmul(bank[2][:, t * NE:(t + 1) * NE], XT[:, c, t * P:(t + 1) * P], WR[:, c, :],
                                  start=(c == 0), stop=(c == DC - 1))
            m.then_inc(s_lm, 1)
            te.wait_ge(s_m, 1)
            te.wait_ge(s_cst, 4)
            pe.matmul(bank[3][:, 0:NE], TRI, MSK[:, 0, :], start=True, stop=True)
            pe.matmul(bank[3][:, NE:2 * NE], TRI, MSK[:, 1, :], start=True, stop=False)
            pe.matmul(bank[3][:, NE:2 * NE], ONES, MSK[:, 0, :], start=False, stop=True)
            pe.matmul(bank[3][:, 2 * NE:3 * NE], ONES, MSK[:, 0, :], start=True, stop=False)
            pe.matmul(bank[3][:, 2 * NE:3 * NE], ONES, MSK[:, 1, :], start=False, stop=True).then_inc(s_rk, 1)

            def pack(m, ye_used):
                te.wait_ge(s_pk, m * 4 + 4)
                since(te, s_ye, ye_used)
                for c in range(DC):
                    for t in range(TT):
                        x = pe.matmul(bank[4 + c // 4][:, c % 4 * P:(c % 4 + 1) * P], H[:, t, c * P:(c + 1) * P],
                                      PK[:, t, :], start=(t == 0), stop=(t == TT - 1))
                    if c % 4 == 3:
                        x.then_inc(s_xm, 1)

            def add_back(n):
                for k in range(4):
                    pe.matmul(bank[k][:, :], PGT[:, k // 2 * P:(k // 2 + 1) * P], YE[:, k % 2 * 512:(k % 2 + 1) * 512],
                              start=True, stop=True).then_inc(s_sc, 1)

            def step(n, i, operand, b):
                for j in range(2):
                    te.wait_ge(s_w[i % AHEAD][j], n * 32 + (i // AHEAD * 16 + 16))
                for c in range(DC):
                    for j in range(2):
                        x = pe.matmul(bank[b][j * C:(j + 1) * C, :], operand[:, c, j * C:(j + 1) * C],
                                      RING[i % AHEAD][j][:, c, :], start=(c == 0), stop=(c == DC - 1))
                x.then_inc(s_step, 1)

            def visit(n, e, first, last):
                te.wait_ge(s_xe, n * 2 + 2)
                te.wait_ge(s_acc, n * 4 + (TT if first else TT - 4))
                for i in range(4):
                    step(n, i, XE, i)
                if not last:
                    pack(n + 1, n * 2)
                since(te, s_pgt, n)
                since(te, s_ht, n * 2)
                for b in range(2):
                    te.wait_ge(s_h, n * 2 + (b + 1))
                    for c in range(4):
                        x = pe.transpose(bank[6 + b][:, c * P:(c + 1) * P], HS[:, (4 * b + c) * P:(4 * b + c + 1) * P], ident)
                    x.then_inc(s_htm, 1)
                if not first:
                    te.wait_ge(s_ye, n * 2)
                    add_back(n - 1)
                te.wait_ge(s_pg, n * 4 + 4)
                te.wait_ge(s_ht, n * 2 + 2)
                pe.transpose(bank[6][:, 0:P], PG[:, 0, :], ident)
                pe.transpose(bank[6][:, P:T], PG[:, 1, :], ident).then_inc(s_pgm, 1)
                te.wait_ge(s_xe, n * 2 + (2 if last else 4))
                for h in range(2):
                    step(n, 4 + h, HT, 4 + h)

            def finish(n):
                te.wait_ge(s_ye, n * 2 + 2)
                te.wait_ge(s_pgt, n + 1)
                te.wait_ge(s_acc, n * 4 + TT)
                add_back(n)

            visits(te, visit, lambda m: pack(m, m * 2), finish)

        @block.vector
        def _(ve):
            ch = Count(K.s_dve)
            ch.n = K.dve_n

            def do(ins):
                ch.by(ins, ve)

            ve.wait_ge(s_par, 64)
            ve.wait_ge(s_cst, 4)
            do(v.memset(GS8, -BIG))
            ve.wait_ge(s_lm, 1)
            for t in range(TT):
                v.tensor_reduce(NM_[:, t:t + 1], bank[2][:, t * NE:(t + 1) * NE], X_AXIS, ALU.max, negate=True).then_inc(s_lg, 1)
            for t in range(TT):
                v.tensor_scalar(Y[:, t, :], H[:, t, :], ALPHA, None, ALU.mult).then_inc(s_acc, 1)
            full = [P, TT, NE]

            def wide(x):
                return x.unsqueeze(2).to_broadcast(full)

            def both(x):
                return x.unsqueeze(1).to_broadcast(full)

            ve.wait_ge(s_ex, TT)
            do(v.reciprocal(RS, SUMS))
            do(v.tensor_tensor(PRB, PRB, wide(RS), ALU.mult))
            do(v.tensor_tensor(SEL, PRB, both(BR), ALU.add))
            sel = SEL.rearrange("p t (g k) -> p (t g) k", g=NGRP)
            do(v.tensor_tensor(PAIR[:, :, 0:3], sel[:, :, 0:3], sel[:, :, 1:4], ALU.add))
            do(v.tensor_tensor(PAIR[:, :, 3:5], sel[:, :, 0:2], sel[:, :, 2:4], ALU.add))
            do(v.tensor_tensor(PAIR[:, :, 5:6], sel[:, :, 0:1], sel[:, :, 3:4], ALU.add))
            do(v.tensor_reduce(GS8[:, :, 0:NGRP], PAIR.rearrange("p (t g) k -> p t g k", t=TT), X_AXIS, ALU.max))
            for t in range(TT):
                do(v.max(G8[:, t, :], GS8[:, t, :]))
                do(v.max_index(GI8[:, t, :], G8[:, t, :], GS8[:, t, :]))
            do(v.tensor_copy(GRPF, GI8[:, :, 0]))
            do(v.tensor_tensor(OH, both(GRP), wide(GRPF), ALU.is_equal))
            do(v.tensor_tensor(SEL, SEL, OH, ALU.mult))
            do(v.tensor_scalar(OH, OH, 1.0, BIG, ALU.subtract, ALU.mult))
            do(v.tensor_tensor(SEL, SEL, OH, ALU.add))
            for t in range(TT):
                do(v.max(M8[:, t, :], SEL[:, t, :]))
                do(v.max_index(E8[:, t, :], M8[:, t, :], SEL[:, t, :]))
            do(v.tensor_copy(E8F, E8))
            do(v.tensor_tensor(TMPA, both(IOTA[:, 0:NE]), wide(E8F[:, :, 0]), ALU.is_equal))
            do(v.tensor_tensor(TMPB, both(IOTA[:, 0:NE]), wide(E8F[:, :, 1]), ALU.is_equal))
            v.tensor_tensor(MSK, TMPA, TMPB, ALU.add).then_inc(s_m, 1)
            ve.wait_ge(s_m, 1)
            do(v.tensor_tensor(TMPB, PRB, MSK, ALU.mult))
            do(v.tensor_reduce(RS, TMPB, X_AXIS, ALU.add))
            do(v.reciprocal(RS, RS))
            for q in range(PASSES):
                do(v.tensor_tensor(GT[:, :, q * NE:(q + 1) * NE], TMPB, wide(RS), ALU.mult))
            ve.wait_ge(s_rk, 1)
            do(v.scalar_tensor_tensor(TMPA, bank[3][:, 0:TT * NE].rearrange("p (t e) -> p t e", t=TT), 1.0, MSK, ALU.add, ALU.mult))
            for q in range(PASSES):
                do(v.tensor_scalar(RK[:, :, q * NE:(q + 1) * NE], TMPA, 1.0 + q * C, None, ALU.subtract))
            do(v.tensor_reduce(CNT, bank[3][:, 2 * NE:3 * NE], X_AXIS, ALU.max))
            do(v.tensor_scalar(NPF, CNT, C + 0.5, 1.0, ALU.is_gt, ALU.add))
            for q in range(2, PASSES):
                do(v.scalar_tensor_tensor(NPF, CNT, q * C + 0.5, NPF, ALU.is_gt, ALU.add))
            v.tensor_copy(NPASS, NPF).then_inc(s_np, 1)

            def build(m):
                for t in range(TT):
                    for j in range(2):
                        v.tensor_scalar(PK[:, t, j * C:(j + 1) * C], IOTA[:, 0:C], RK[:, t, bass.ds(m * 2 + j, 1)],
                                        None, ALU.is_equal).then_inc(s_pk, 1)

            def prologue(m):
                since(ve, s_xm, m * 2)
                build(m)

            def add(m):
                ve.wait_ge(s_acc, m * 4 + TT)
                for k in range(4):
                    ve.wait_ge(s_sc, m * 4 + (k + 1))
                    o = Y[:, k // 2, k % 2 * 512:(k % 2 + 1) * 512]
                    v.tensor_tensor(o, o, bank[k][:, :], ALU.add).then_inc(s_acc, 1)

            def visit(n, e, first, last):
                since(ve, s_pgm, n)
                for t in range(TT):
                    for j in range(2):
                        v.tensor_scalar(PG[:, t, j * C:(j + 1) * C], IOTA[:, 0:C], RK[:, t, bass.ds(n * 2 + j, 1)],
                                        GT[:, t, bass.ds(n * 2 + j, 1)], ALU.is_equal, ALU.mult).then_inc(s_pg, 1)
                if not last:
                    ve.wait_ge(s_xm, n * 2 + 2)
                    build(n + 1)
                since(ve, s_htm, n * 2)
                for b in range(2):
                    ve.wait_ge(s_step, n * NS + (b + 3))
                    ve.wait_ge(s_sg, n * 2 + (b + 1))
                    cs = slice(b * 512, (b + 1) * 512)
                    v.tensor_tensor(HS[:, cs], SG[:, cs], bank[2 + b][:, :], ALU.mult).then_inc(s_h, 1)
                if not first:
                    add(n - 1)

            visits(ve, visit, prologue, add)
            norm.vector(ve, do, v, H, Y, CENT, D, LG, LB)
            if last_layer:
                for t in range(TT):
                    v.tensor_copy(Y[:, t, 0:1], H[:, t, 0:1]).then_inc(s_fin, 1)
            K.dve_n = ch.n


def moe_stage_0(K):
    moe_stage(K, 0)


def moe_stage_1(K):
    moe_stage(K, 1)


STAGES = (mixing_stage, peer_stage, attention_stage_0, moe_stage_0, attention_stage_1, moe_stage_1)


def build(nc, dram, out):
    with ExitStack() as ctx:
        K = Kit()
        K.nc, K.dram, K.out = nc, dram, out
        K.lasting_sem = lambda name: ctx.enter_context(nc.semaphore(name))
        K.bank = [ctx.enter_context(nc.psum_tensor(f"bank{i}", [P, 512], F32)) for i in range(8)]
        K.h_res = ctx.enter_context(nc.sbuf_tensor("h_res", [P, TT, D], F32))
        K.ident = ctx.enter_context(nc.sbuf_tensor("ident", [P, P], F32))[:, :]
        K.cols = 50900
        arena = ctx.enter_context(nc.sbuf_tensor("arena", [P, K.cols], F32))

        def cut(at, p, *shape):
            n = math.prod(shape)
            ap = arena[0:p, at:at + n]
            names = "abcd"[:len(shape)]
            if len(shape) == 1:
                return ap
            return ap.rearrange(f"p ({' '.join(names)}) -> p {' '.join(names)}", **dict(zip(names, shape)))

        def clear_stale(pool):
            for s in K.stale:
                pool.sem_clear(s)

        K.cut, K.clear_stale = cut, clear_stale
        K.s_ident = K.lasting_sem("identity")
        K.s_dve = K.lasting_sem("dve_chain")
        K.dve_n = 0
        K.stale = []
        for stage in STAGES:
            with ExitStack() as of_stage:
                own = []

                def sem(name):
                    own.append(of_stage.enter_context(nc.semaphore(name)))
                    return own[-1]

                K.sem = sem
                stage(K)
                assert not {s.num for s in own} & {s.num for s in K.stale}
            K.stale = own


def dft_constants():
    f32 = np.float32
    t = np.arange(L)[:, None].astype(np.float64)
    f = np.arange(NF)[None, :].astype(np.float64)
    ang = 2 * np.pi / NFFT * ((t * f) % NFFT)
    w = np.where((f == 0) | (f == NF - 1), 1.0, 2.0) / NFFT
    dft = np.stack([np.cos(ang), np.sin(ang)]).astype(f32)
    idft = np.stack([(np.cos(ang) * w).T[:, NM:], (np.sin(ang) * w).T[:, NM:]]).astype(f32)
    ts = np.linspace(0.0, 1.0, L, dtype=f32)[:, None]
    wv = (f32(2.0 * math.pi / L) * np.arange(L, dtype=f32))[:, None]
    n = (HY_EMB - 1) // 2
    bands = np.linspace(1e-4, n - 1, n, dtype=f32)[None, :]
    zT = np.concatenate([ts, np.cos(bands * wv), -np.sin(bands * wv)], axis=-1).T.astype(f32)
    deltas = np.abs(np.linspace(math.log(1e-2) / 0.3, math.log(1e-2) / 1.5, D_HY, dtype=f32))
    decay = np.exp(-ts * deltas).astype(f32)
    back = decay.copy()
    back[0] = 0
    return {"dft": dft, "idft": idft, "zT": np.ascontiguousarray(zT), "decay": np.stack([decay, back])}


def dilation_bias():
    slopes = (2.0 ** (-8.0 * np.arange(1, N_DH + 1, dtype=np.float32) / N_DH)).astype(np.float32)
    rel = np.arange(T)[:, None] - np.arange(T)[None, :]
    full = np.stack([np.where((rel >= 0) & (rel <= w) & (rel % r == 0), -slopes[g * HPD + j] * rel.astype(np.float32), -BIG)
                     for g, (w, r) in enumerate(DILS) for j in range(HPD)]).astype(np.float32)
    return np.concatenate([full[:, 0:P, 0:P], full[:, P:T, :]], 2).transpose(1, 0, 2)


def kernel(**inputs):
    import numpy as _np
    import concourse.bacc as _bacc
    from concourse import mybir as _mybir
    from concourse.bass_utils import run_bass_kernel_spmd as _run

    g = {k: _np.asarray(x) for k, x in inputs.items()}

    def tiles(a, n=P):
        return a.reshape(-1, n).T

    s_hy = 3 * D_HY
    w_in = g["w_in"][0]
    x0, x1, vv = (w_in[:, k * D_HY:(k + 1) * D_HY] for k in range(3))
    rx, rg, mg = w_in[:, s_hy:s_hy + D_RG], w_in[:, s_hy + D_RG:s_hy + 2 * D_RG], w_in[:, s_hy + 2 * D_RG:]

    def hy(a):
        return _np.concatenate([a[..., 2 * D_HY:], a[..., D_HY:2 * D_HY], a[..., :D_HY]], -1)

    cols = _np.concatenate([
        tiles(g["g_mix"]), _np.zeros((P, T_G1), _np.float32), tiles(g["b_gate"]), tiles(hy(g["hy_conv_w"][0])),
        tiles(hy(g["hy_conv_b"])), tiles(g["rg_conv_w"][0]), tiles(g["rg_conv_b"]), tiles(g["rg_gate_b"]),
        tiles(g["rg_lambda"]), tiles(g["hy_skip"])], 1)
    fr = g["hy_freq"][0]
    arrays = {
        "x": g["x"][0], "meta": g["meta"], "cols": cols,
        "w_in": _np.concatenate([rx, vv, x1, x0, rg, mg], 1),
        "hy_w1": g["hy_w1"][0], "hy_w2": g["hy_w2"][0],
        "hy_bf": _np.stack([g["hy_b1"][0], fr[0], g["hy_b2"][0], fr[1]], 1),
        "hy_w3b": _np.concatenate([g["hy_w3"][0], g["hy_b3"]], 0),
        "gate_w": g["rg_gate_w"][0], "rg_out": g["rg_out"][0], "hy_out": g["hy_out"][0], "w_out": g["w_out"][0],
    }
    arrays.update(dft_constants())
    arrays.update({
        "g_ffn": g["g_ffn"][0], "g_final": g["g_final"], "wq": g["peer_wq"][0],
        "keysT": g["peer_keys"][0].transpose(3, 0, 1, 2).reshape(P, 2 * PH, NKEYS),
        "peer_u": g["peer_u"][0], "peer_v": g["peer_v"][0],
    })
    arrays.update({
        "memT": g["mem_2"][0].T, "w_in0": g["w_in_a_2"][0], "w_in1": g["w_in_b_2"][0], "w_out0": g["w_out_a_2"][0],
        "w_out1": g["w_out_b_2"][0], "w_k": g["w_k_shared_2"], "w_v": g["w_v_shared_2"],
        "sg_wT": g["sg_w_2"][0].transpose(2, 0, 1), "sg_bT": g["sg_b_2"][0].T, "sg_ln_g": g["sg_ln_g_2"][0],
        "sg_ln_b": g["sg_ln_b_2"][0], "ln1_g": g["ln1_g_2"], "ln1_b": g["ln1_b_2"], "dil_bias": dilation_bias(),
    })
    for n in range(2):
        arrays[f"w_mem_k{n}"], arrays[f"w_mem_v{n}"] = g["w_mem_k_2"][n], g["w_mem_v_2"][n]
    arrays.update({
        "w_router": g["w_router_2"], "b_router": g["b_router_2"], "ln2_g": g["ln2_g_2"], "ln2_b": g["ln2_b_2"],
        "w_gate": g["w_gate_2"].reshape(2 * NE, D, D), "w_up": g["w_up_2"].reshape(2 * NE, D, D),
        "w_down": g["w_down_2"].reshape(2 * NE, D, D),
    })
    arrays = {"in_" + k: _np.ascontiguousarray(x) for k, x in arrays.items()}
    nc = _bacc.Bacc("TRN2", target_bir_lowering=False, num_devices=1)
    dram = {k[3:]: nc.dram_tensor(k, x.shape, _mybir.dt.from_np(x.dtype), kind="ExternalInput").ap() for k, x in arrays.items()}
    out = nc.dram_tensor("out", (T, D), F32, kind="ExternalOutput").ap()
    build(nc, dram, out)
    r = _run(nc, [arrays], core_ids=[0])
    return r.results[0]["out"].reshape(1, T, D)
```
